# Optimizing a Trainium2 kernel written in Bass

```python
import jax, jax.numpy as jnp
from jax import lax
import numpy as np

D_MODEL = 1024
BATCH = 1
SEQ = 512
DEPTH = 2
DEC_BATCH = 8
DEC_SEQ = 4
PAST_LEN = 512
PAGE_SIZE = 128

N_MIXERS = 2
N_ATTN_LAYERS = (DEPTH + 1) // 2
N_REC_LAYERS = DEPTH // 2
N_HEADS = 16
HEAD_DIM = D_MODEL // N_HEADS
KV_GROUPS = 2
HEADS_PER_GROUP = N_HEADS // KV_GROUPS
CMP_BLOCK = 32
CMP_STRIDE = 16
CMP_HIDDEN = 256
SEL_BLOCK = 64
SEL_TOPK = 16
WINDOW = 512
Q_BLOCK = 64
NSA_Q_COLS = N_HEADS * HEAD_DIM
NSA_KV_COLS = 6 * KV_GROUPS * HEAD_DIM
NSA_IN_COLS = NSA_Q_COLS + NSA_KV_COLS + 3 * N_HEADS
ATTN_SCALE = HEAD_DIM ** -0.5
FORCE_SCORE = 1e6
NEG_INF = -1e30
D_RNN = D_MODEL
RG_BLOCKS = 4
RG_BLOCK_DIM = D_RNN // RG_BLOCKS
RG_CONV = 4
RG_C = 8.0
D_FF = 3 * D_MODEL
FFN_CONV = 3
D_PLE = 256
ALPHA = (2 * DEPTH) ** 0.25
BETA = (8 * DEPTH) ** -0.25
LN_EPS = 1e-5

kernel_name = 'nsa_rglru_convffn_hybrid_step'

def layer_norm(x, g, b):
    xf = x.astype(jnp.float32)
    mu = jnp.mean(xf, axis=-1, keepdims=True)
    var = jnp.mean(jnp.square(xf - mu), axis=-1, keepdims=True)
    y = (xf - mu) * lax.rsqrt(var + LN_EPS) * g.astype(jnp.float32) + b.astype(jnp.float32)
    return y.astype(x.dtype)

def masked_softmax(s, mask):
    s = jnp.where(mask, s, NEG_INF)
    m = jnp.max(s, axis=-1, keepdims=True)
    e = jnp.where(mask, jnp.exp(s - m), 0.0)
    return e / jnp.maximum(jnp.sum(e, axis=-1, keepdims=True), 1e-30)

def causal_dwconv(u, w, b, prev):
    K = w.shape[0]
    T = u.shape[1]
    ext = jnp.concatenate([prev.astype(u.dtype), u], axis=1)
    out = b + ext[:, 0:T] * w[0]
    for k in range(1, K):
        out = out + ext[:, k:k + T] * w[k]
    return out, ext[:, T:]

def nsa_project(x, w_in):
    B, T, _ = x.shape
    proj = x @ w_in
    q = proj[..., :NSA_Q_COLS].reshape(B, T, KV_GROUPS, HEADS_PER_GROUP, HEAD_DIM)
    kv = proj[..., NSA_Q_COLS:NSA_Q_COLS + NSA_KV_COLS].reshape(B, T, 6, KV_GROUPS, HEAD_DIM)
    gates = jax.nn.sigmoid(proj[..., NSA_Q_COLS + NSA_KV_COLS:]).reshape(B, T, KV_GROUPS, HEADS_PER_GROUP, 3)
    return q, kv, gates

def compress(rows, pe, w1, b1, w2):
    nc = (rows.shape[1] - CMP_BLOCK) // CMP_STRIDE + 1
    idx = jnp.arange(nc)[:, None] * CMP_STRIDE + jnp.arange(CMP_BLOCK)[None, :]
    blk = rows[:, idx] + pe[:, None, :]
    hid = jax.nn.gelu(jnp.einsum('bclgd,ldh->bcgh', blk, w1) + b1)
    return jnp.einsum('bcgh,hd->bcgd', hid, w2)

def nsa_keys(rows, cmp):
    pe, w1, b1, w2 = cmp
    B, Tk = rows.shape[:2]
    kc = compress(rows[:, :, 0], pe[0], w1[0], b1[0], w2[0])
    vc = compress(rows[:, :, 1], pe[1], w1[1], b1[1], w2[1])
    nc = kc.shape[1]
    c_start = jnp.arange(nc) * CMP_STRIDE
    c_end = c_start + (CMP_BLOCK - 1)
    ns = -(-Tk // SEL_BLOCK)
    b_start = jnp.arange(ns) * SEL_BLOCK
    overlap = ((c_start[:, None] < b_start[None, :] + SEL_BLOCK)
               & (c_end[:, None] >= b_start[None, :])).astype(jnp.float32)
    sel = jnp.pad(rows[:, :, 2:4], ((0, 0), (0, ns * SEL_BLOCK - Tk), (0, 0), (0, 0), (0, 0)))
    sel = sel.reshape(B, ns, SEL_BLOCK, 2, KV_GROUPS, HEAD_DIM).transpose(3, 0, 4, 1, 2, 5)
    return (kc, vc, c_end, sel[0], sel[1], overlap)

def nsa_attend(q, gates, q_pos, ctx, kw, vw, w_pos):
    kc, vc, c_end, ks, vs, overlap = ctx
    B, Q = q.shape[:2]
    ns = ks.shape[2]
    f32 = jnp.float32
    s_c = jnp.einsum('bqghd,bcgd->bghqc', q, kc).astype(f32) * ATTN_SCALE
    p_c = masked_softmax(s_c, c_end[None, :] <= q_pos[:, None])
    o_c = jnp.einsum('bghqc,bcgd->bqghd', p_c.astype(vc.dtype), vc)
    imp = jnp.einsum('bghqc,cn->bgqn', p_c, overlap)
    blk = jnp.arange(ns)[None, :]
    cur = (q_pos // SEL_BLOCK)[:, None]
    imp = jnp.where((blk == 0) | (blk == cur) | (blk == cur - 1), FORCE_SCORE, imp)
    imp = jnp.where(blk > cur, -1.0, imp)
    n_top = min(SEL_TOPK, ns)
    _, idx = lax.top_k(imp, n_top)
    bi = jnp.arange(B)[:, None, None, None]
    gi = jnp.arange(KV_GROUPS)[None, :, None, None]
    k_sel = ks[bi, gi, idx].reshape(B, KV_GROUPS, Q, n_top * SEL_BLOCK, HEAD_DIM)
    v_sel = vs[bi, gi, idx].reshape(B, KV_GROUPS, Q, n_top * SEL_BLOCK, HEAD_DIM)
    s_pos = (idx[..., None] * SEL_BLOCK + jnp.arange(SEL_BLOCK)).reshape(B, KV_GROUPS, Q, n_top * SEL_BLOCK)
    s_s = jnp.einsum('bqghd,bgqkd->bghqk', q, k_sel).astype(f32) * ATTN_SCALE
    p_s = masked_softmax(s_s, (s_pos <= q_pos[None, None, :, None])[:, :, None])
    o_s = jnp.einsum('bghqk,bgqkd->bqghd', p_s.astype(v_sel.dtype), v_sel)
    s_w = jnp.einsum('bqghd,bwgd->bghqw', q, kw).astype(f32) * ATTN_SCALE
    dist = q_pos[:, None] - w_pos[None, :]
    p_w = masked_softmax(s_w, (dist >= 0) & (dist <= WINDOW) & (w_pos[None, :] >= 0))
    o_w = jnp.einsum('bghqw,bwgd->bqghd', p_w.astype(vw.dtype), vw)
    g = gates.astype(o_c.dtype)
    return g[..., 0:1] * o_c + g[..., 1:2] * o_s + g[..., 2:3] * o_w

def nsa_prompt(x, w_in, w_out, cmp):
    B, T, _ = x.shape
    q, kv, gates = nsa_project(x, w_in)
    ctx = nsa_keys(kv[:, :, :4], cmp)
    kw_pad = jnp.pad(kv[:, :, 4:6], ((0, 0), (WINDOW, 0), (0, 0), (0, 0), (0, 0)))
    nb = T // Q_BLOCK
    qb = q.reshape(B, nb, Q_BLOCK, KV_GROUPS, HEADS_PER_GROUP, HEAD_DIM).swapaxes(0, 1)
    gb = gates.reshape(B, nb, Q_BLOCK, KV_GROUPS, HEADS_PER_GROUP, 3).swapaxes(0, 1)

    def block(args):
        qc, gc, c = args
        start = c * Q_BLOCK
        kwc = lax.dynamic_slice_in_dim(kw_pad, start, WINDOW + Q_BLOCK, axis=1)
        q_pos = start + jnp.arange(Q_BLOCK)
        w_pos = start - WINDOW + jnp.arange(WINDOW + Q_BLOCK)
        return nsa_attend(qc, gc, q_pos, ctx, kwc[:, :, 0], kwc[:, :, 1], w_pos)

    o = lax.map(block, (qb, gb, jnp.arange(nb)))
    o = o.swapaxes(0, 1).reshape(B, T, N_HEADS * HEAD_DIM)
    return o @ w_out, kv[:, :, :4], kv[:, T - min(WINDOW, T):, 4:6]

def nsa_sample(x, kv_pool, page_table, win_buf, w_in, w_out, cmp):
    B, S, _ = x.shape
    q, kv, gates = nsa_project(x, w_in)
    past = kv_pool[page_table]
    past = past.reshape(B, -1, 4, KV_GROUPS, HEAD_DIM)
    P = past.shape[1]
    rows = jnp.concatenate([past.astype(kv.dtype), kv[:, :, :4]], axis=1)
    ctx = nsa_keys(rows, cmp)
    Wb = win_buf.shape[1]
    kw = jnp.concatenate([win_buf.astype(kv.dtype), kv[:, :, 4:6]], axis=1)
    q_pos = P + jnp.arange(S)
    w_pos = P - Wb + jnp.arange(Wb + S)
    o = nsa_attend(q, gates, q_pos, ctx, kw[:, :, 0], kw[:, :, 1], w_pos)
    return o.reshape(B, S, N_HEADS * HEAD_DIM) @ w_out, kv[:, :, :4], kw[:, S:]

def rglru_scan(x, h0, ga_w, ga_b, gx_w, gx_b, lam):
    B, T, _ = x.shape
    f32 = jnp.float32
    xb = x.reshape(B, T, RG_BLOCKS, RG_BLOCK_DIM)
    r = jax.nn.sigmoid((jnp.einsum('btnc,ncd->btnd', xb, ga_w).reshape(B, T, D_RNN) + ga_b).astype(f32))
    i = jax.nn.sigmoid((jnp.einsum('btnc,ncd->btnd', xb, gx_w).reshape(B, T, D_RNN) + gx_b).astype(f32))
    log_a = -RG_C * r * jax.nn.softplus(-lam.astype(f32))
    a = jnp.exp(log_a)
    u = jnp.sqrt(-jnp.expm1(2.0 * log_a)) * i * x.astype(f32)

    def step(h, au):
        a_t, u_t = au
        h = a_t * h + u_t
        return h, h

    h_last, hs = lax.scan(step, h0.astype(f32), (a.swapaxes(0, 1), u.swapaxes(0, 1)))
    return hs.swapaxes(0, 1).astype(x.dtype), h_last.astype(h0.dtype)

def rglru_block(x, h0, conv_prev, w_in, conv_w, conv_b, ga_w, ga_b, gx_w, gx_b, lam, w_out):
    u = x @ w_in
    gate_br, rec_br = u[..., :D_RNN], u[..., D_RNN:]
    rec, conv_state = causal_dwconv(rec_br, conv_w, conv_b, conv_prev)
    h, h_last = rglru_scan(rec, h0, ga_w, ga_b, gx_w, gx_b, lam)
    return (h * jax.nn.gelu(gate_br)) @ w_out, h_last, conv_state

def conv_ffn(x, prev, w_up, conv_w, conv_b, w_down):
    u, state = causal_dwconv(x @ w_up, conv_w, conv_b, prev)
    return (jax.nn.gelu(u[..., :D_FF]) * u[..., D_FF:]) @ w_down, state

def layer_tail(x, mix, ffn_prev, p, ln_mg, ln_mb, ln_fg, ln_fb, w_up, conv_w, conv_b, w_down, w_proj, w_gate):
    h = layer_norm(ALPHA * x + mix, ln_mg, ln_mb)
    f, ffn_state = conv_ffn(h, ffn_prev, w_up, conv_w, conv_b, w_down)
    h = layer_norm(ALPHA * h + f, ln_fg, ln_fb)
    return h + jax.nn.sigmoid(h @ w_gate) * (p @ w_proj), ffn_state

def setup_inputs(seed: int = 0) -> dict:
    key = jax.random.key(seed)
    keys = iter(jax.random.split(key, 64))

    def nrm(shape, scale):
        return jax.random.normal(next(keys), shape, jnp.float32) * scale

    n_pages = PAST_LEN // PAGE_SIZE
    n_pool = (DEC_BATCH * n_pages * 5) // 4
    win_buf = min(WINDOW, PAST_LEN)
    A, R = N_ATTN_LAYERS, N_REC_LAYERS
    x_prompt = nrm((BATCH, SEQ, D_MODEL), 1.0)
    x_sample = nrm((DEC_BATCH, DEC_SEQ, D_MODEL), 1.0)
    cache_nsa_kv = nrm((A, n_pool, PAGE_SIZE, 4, KV_GROUPS, HEAD_DIM), 1.0)
    cache_nsa_win = nrm((A, DEC_BATCH, win_buf, 2, KV_GROUPS, HEAD_DIM), 1.0)
    state_rglru_h = nrm((R, DEC_BATCH, D_RNN), 0.5)
    state_rglru_conv = nrm((R, DEC_BATCH, RG_CONV - 1, D_RNN), 1.0)
    state_ffn_conv = nrm((DEPTH, DEC_BATCH, FFN_CONV - 1, 2 * D_FF), 1.0)
    page_table = jax.random.permutation(next(keys), n_pool)[:DEC_BATCH * n_pages]
    page_table = page_table.reshape(DEC_BATCH, n_pages).astype(jnp.int32)
    p_prompt = nrm((DEPTH, BATCH, SEQ, D_PLE), 1.0)
    p_sample = nrm((DEPTH, DEC_BATCH, DEC_SEQ, D_PLE), 1.0)
    u = jax.random.uniform(next(keys), (R, D_RNN), jnp.float32, 0.9, 0.999)
    s = u ** (1.0 / RG_C)
    rg_lambda = jnp.log(s) - jnp.log1p(-s)
    return {
        'x_prompt': x_prompt,
        'x_sample': x_sample,
        'cache_nsa_kv': cache_nsa_kv,
        'cache_nsa_win': cache_nsa_win,
        'state_rglru_h': state_rglru_h,
        'state_rglru_conv': state_rglru_conv,
        'state_ffn_conv': state_ffn_conv,
        'page_table': page_table,
        'p_prompt': p_prompt,
        'p_sample': p_sample,
        'nsa_w_in': nrm((A, D_MODEL, NSA_IN_COLS), D_MODEL ** -0.5),
        'nsa_w_out': nrm((A, N_HEADS * HEAD_DIM, D_MODEL), BETA * (N_HEADS * HEAD_DIM) ** -0.5),
        'nsa_cmp_pe': nrm((A, 2, CMP_BLOCK, HEAD_DIM), 0.1),
        'nsa_cmp_w1': nrm((A, 2, CMP_BLOCK, HEAD_DIM, CMP_HIDDEN), (CMP_BLOCK * HEAD_DIM) ** -0.5),
        'nsa_cmp_b1': nrm((A, 2, CMP_HIDDEN), 0.01),
        'nsa_cmp_w2': nrm((A, 2, CMP_HIDDEN, HEAD_DIM), CMP_HIDDEN ** -0.5),
        'rg_w_in': nrm((R, D_MODEL, 2 * D_RNN), D_MODEL ** -0.5),
        'rg_conv_w': nrm((R, RG_CONV, D_RNN), RG_CONV ** -0.5),
        'rg_conv_b': nrm((R, D_RNN), 0.01),
        'rg_gate_a_w': nrm((R, RG_BLOCKS, RG_BLOCK_DIM, RG_BLOCK_DIM), RG_BLOCK_DIM ** -0.5),
        'rg_gate_a_b': nrm((R, D_RNN), 0.01),
        'rg_gate_x_w': nrm((R, RG_BLOCKS, RG_BLOCK_DIM, RG_BLOCK_DIM), RG_BLOCK_DIM ** -0.5),
        'rg_gate_x_b': nrm((R, D_RNN), 0.01),
        'rg_lambda': rg_lambda,
        'rg_w_out': nrm((R, D_RNN, D_MODEL), BETA * D_RNN ** -0.5),
        'ffn_w_up': nrm((DEPTH, D_MODEL, 2 * D_FF), D_MODEL ** -0.5),
        'ffn_conv_w': nrm((DEPTH, FFN_CONV, 2 * D_FF), FFN_CONV ** -0.5),
        'ffn_conv_b': nrm((DEPTH, 2 * D_FF), 0.01),
        'ffn_w_down': nrm((DEPTH, D_FF, D_MODEL), BETA * D_FF ** -0.5),
        'ln_mix_g': 1.0 + nrm((DEPTH, D_MODEL), 0.05),
        'ln_mix_b': nrm((DEPTH, D_MODEL), 0.02),
        'ln_ffn_g': 1.0 + nrm((DEPTH, D_MODEL), 0.05),
        'ln_ffn_b': nrm((DEPTH, D_MODEL), 0.02),
        'ple_w_proj': nrm((DEPTH, D_PLE, D_MODEL), 0.5 * D_PLE ** -0.5),
        'ple_w_gate': nrm((DEPTH, D_MODEL, D_MODEL), D_MODEL ** -0.5),
    }

def reference(x_prompt, x_sample, cache_nsa_kv, cache_nsa_win, state_rglru_h, state_rglru_conv,
              state_ffn_conv, page_table, p_prompt, p_sample,
              nsa_w_in, nsa_w_out, nsa_cmp_pe, nsa_cmp_w1, nsa_cmp_b1, nsa_cmp_w2,
              rg_w_in, rg_conv_w, rg_conv_b, rg_gate_a_w, rg_gate_a_b, rg_gate_x_w, rg_gate_x_b,
              rg_lambda, rg_w_out,
              ffn_w_up, ffn_conv_w, ffn_conv_b, ffn_w_down,
              ln_mix_g, ln_mix_b, ln_ffn_g, ln_ffn_b, ple_w_proj, ple_w_gate):
    xp, xs = x_prompt, x_sample
    bp = xp.shape[0]
    kv_p, kv_s, win_p, win_s = [], [], [], []
    h_p, h_s, rc_p, rc_s = [], [], [], []
    fc_p, fc_s = [], []
    for i in range(DEPTH):
        j = i // N_MIXERS
        if i % N_MIXERS == 0:
            cmp = (nsa_cmp_pe[j], nsa_cmp_w1[j], nsa_cmp_b1[j], nsa_cmp_w2[j])
            mix_p, rows_p, wnd_p = nsa_prompt(xp, nsa_w_in[j], nsa_w_out[j], cmp)
            mix_s, rows_s, wnd_s = nsa_sample(xs, cache_nsa_kv[j], page_table, cache_nsa_win[j],
                                              nsa_w_in[j], nsa_w_out[j], cmp)
            kv_p.append(rows_p)
            kv_s.append(rows_s)
            win_p.append(wnd_p)
            win_s.append(wnd_s)
        else:
            rg = (rg_w_in[j], rg_conv_w[j], rg_conv_b[j], rg_gate_a_w[j], rg_gate_a_b[j],
                  rg_gate_x_w[j], rg_gate_x_b[j], rg_lambda[j], rg_w_out[j])
            h0 = jnp.zeros((bp, D_RNN), jnp.float32)
            c0 = jnp.zeros((bp, RG_CONV - 1, D_RNN), xp.dtype)
            mix_p, hl_p, cs_p = rglru_block(xp, h0, c0, *rg)
            mix_s, hl_s, cs_s = rglru_block(xs, state_rglru_h[j], state_rglru_conv[j], *rg)
            h_p.append(hl_p)
            h_s.append(hl_s)
            rc_p.append(cs_p)
            rc_s.append(cs_s)
        tail = (ln_mix_g[i], ln_mix_b[i], ln_ffn_g[i], ln_ffn_b[i], ffn_w_up[i], ffn_conv_w[i],
                ffn_conv_b[i], ffn_w_down[i], ple_w_proj[i], ple_w_gate[i])
        f0 = jnp.zeros((bp, FFN_CONV - 1, 2 * D_FF), xp.dtype)
        xp, fs_p = layer_tail(xp, mix_p, f0, p_prompt[i], *tail)
        xs, fs_s = layer_tail(xs, mix_s, state_ffn_conv[i], p_sample[i], *tail)
        fc_p.append(fs_p)
        fc_s.append(fs_s)
    return (xp, xs,
            jnp.stack(kv_p), jnp.stack(kv_s),
            jnp.stack(win_p), jnp.stack(win_s),
            jnp.stack(h_p), jnp.stack(h_s),
            jnp.stack(rc_p), jnp.stack(rc_s),
            jnp.stack(fc_p), jnp.stack(fc_s))


_drawn_inputs = setup_inputs


def setup_inputs(seed=0):
    import zlib

    import numpy as np

    out = dict(_drawn_inputs(seed))
    spreads = {}
    factors = {'nsa_cmp_b1': 8.0, 'rg_gate_a_b': 25.124, 'rg_gate_x_b': 8.0, 'ffn_conv_b': 6.806}
    for name, (base, spread) in spreads.items():
        noise = np.random.default_rng([zlib.crc32(name.encode()), seed]).standard_normal(out[name].shape)
        drawn = base * np.exp(spread * noise) if base else spread * noise
        out[name] = __import__('jax').numpy.asarray(drawn.astype(out[name].dtype))
    for name, factor in factors.items():
        out[name] = (out[name] * factor).astype(out[name].dtype)
    return out
```

```python
from contextlib import ExitStack

import numpy as np
import concourse.bass as bass
from concourse import mybir

F32 = mybir.dt.float32
F32R = mybir.dt.float32r
BF16 = mybir.dt.bfloat16
I32 = mybir.dt.int32
ALU = mybir.AluOpType
ACT = mybir.ActivationFunctionType
AX_X = mybir.AxisListType.X

P = 128
D = 1024
KT = D // P
SEQ = 512
NB, NS = 8, 4
HALF = 272
HP = 256
TOK = 2 * HALF
HD = 64
NJ = 8
PAGES = 4
NC = 31
SCALE = HD ** -0.5
NEG = -1e30
ALPHA = 4 ** 0.25
EPS = 1e-5
FT = 24
THIRD = 8
CH = KT * P
OPW = 4624

IN_TILES = ["kcmp", "vcmp", "ksel", "vsel", "kwin", "vwin", "gate"] + ["q"] * 8


def plan():
    first_chunk, first_tile = {}, {}
    taker, last_user, used_up = [], [], []

    def section(name, tiles, takers, chunks_of):
        first_chunk[name], first_tile[name] = len(last_user), len(taker)
        n_chunks = 1 + max(max(chunks_of(n)) for n in range(tiles))
        base_t, base_c = len(taker), len(last_user)
        last = [0] * n_chunks
        for n in range(tiles):
            taker.append(takers(n))
            for c in chunks_of(n):
                last[c] = base_t + n
        last_user.extend(last)
        for n in range(tiles):
            used_up.append(base_c + sum(1 for u in last if u <= base_t + n))

    one = lambda n: [n]
    section("w_in", 15, lambda n: "act", one)
    section("cmp", 8, lambda n: "dve" if n % 2 else "act", one)
    section("w_out", 8, lambda n: "dve", one)
    for layer in (0, 1):
        if layer == 1:
            section("rec", 8, lambda n: "act", one)
            section("rgate", 16, lambda n: "act", lambda n: [2 * (n // 8) + n % 2])
            section("gbr", 8, lambda n: "act", one)
            section("rg_out", 8, lambda n: "dve", one)
        section(f"ffn{layer}", 72, lambda n: "act" if n % 24 < 16 else "dve", one)
        section(f"proj{layer}", 8, lambda n: "act", lambda n: [n // 4])
        section(f"gate{layer}", 8, lambda n: "act", one)
    return first_chunk, first_tile, taker, last_user, used_up


C0, O0, TAKER, LAST_USER, USED_UP = plan()
N_CHUNKS = len(LAST_USER)
RAWS, SLOTS, AHEAD = 2, 4, 3


def taken(o):
    return TAKER[o], sum(1 for t in TAKER[:o + 1] if t == TAKER[o])


PCOL = {}
_n = 0
for _name, _w in ([(f"{k}{i}", w) for i in (0, 1) for k, w in
                   (("conv", 192), ("ln_mg", 8), ("ln_mb", 8), ("ln_fg", 8), ("ln_fb", 8))]
                  + [("rconv_w", 32), ("rconv_b", 8), ("ga_b", 8), ("gx_b", 8), ("lam", 8), ("cmp_b1", 4),
                     ("pe", 32), ("h0", 64), ("rstate", 192)]):
    PCOL[_name] = _n
    _n += _w
NPAR = _n

U = 2 + SEQ + NB * 6
UO = U - 2
UR = 3 + SEQ + NB * 7
URO = UR - 3


def build(nc, a, outs):
    ctx = ExitStack()
    with ctx:
        def sb(name, cols, dt=F32, parts=P):
            return ctx.enter_context(nc.sbuf_tensor(name, [parts, cols], dt))

        def sem(name):
            return ctx.enter_context(nc.semaphore(name))

        RAW = sb("RAW", RAWS * CH)
        HI, LO = sb("HI", SLOTS * CH, F32R), sb("LO", SLOTS * CH, F32R)
        XH, XL = sb("XH", OPW, F32R), sb("XL", OPW, F32R)
        GH, GL = sb("GH", OPW, F32R), sb("GL", OPW, F32R)
        X = sb("X", KT * TOK)
        PAR = sb("PAR", NPAR)
        IDENT, IDENTB, ONES = sb("IDENT", P), sb("IDENTB", P, BF16), sb("ONES", P)
        DMASK = sb("DMASK", P, BF16)
        CMASK = sb("CMASK", 4 * 32)
        SMASK = sb("SMASK", 8)
        SMALL = sb("SMALL", 512)
        CWS = sb("CWS", 16)
        PAGE = sb("PAGE", NB * PAGES, I32, parts=1)
        NA = (nc.sbuf_bytes_remaining if not callable(nc.sbuf_bytes_remaining) else nc.sbuf_bytes_remaining()) // 4 - 8
        ARENA = sb("ARENA", NA)
        PS = ctx.enter_context(nc.psum_tensor("PS", [P, 8, 512], F32))

        def carve(at, sizes):
            views = []
            for n in sizes:
                views.append(ARENA[:, at:at + n])
                at += n
            assert at <= NA, (at, NA)
            return views, at

        (CACHE, KT4, VP, VM, KS, QS, KC, KCP, GT, GS), at = carve(
            0, [8192, 2048, 1024, 1024, 192, 256, 256, 32, 192, 16])
        (AT, HS, HPR, KR, XPR, GTC), _ = carve(at, [578, 1024, 128, 1024, 1024, TOK])
        VCP = SMALL[:, 352:480]
        (PB, PT, SC, PCT, OS, OTMP), _ = carve(at, [2048, 1024, 512, 512, 512, 384])
        Q = X[:, 0:NJ * SEQ].rearrange("p (j t) -> p j t", j=NJ)
        (PP, SQ, RS, LT, PRAW), at_ln = carve(0, [KT * TOK, 2 * TOK, TOK, 2 * TOK, 2 * TOK])
        (EXT, CV, G1, PR, ST, CS), _ = carve(at_ln, [4 * U, 4 * U, U, TOK, 48 * 16, 48 * 18])
        (REC, RR, VV, REXT, RCV, RTM, LAST), _ = carve(0, [KT * TOK, KT * TOK, KT * TOK, 2 * UR, UR, 2 * TOK, 8 * 36])

        def t3(ap, n=KT):
            return ap.rearrange("p (k t) -> p k t", k=n)

        X3, PP3, REC3, RR3, VV3 = t3(X[:, :]), t3(PP), t3(REC), t3(RR), t3(VV)
        XH3, XL3 = t3(XH[:, 0:KT * TOK]), t3(XL[:, 0:KT * TOK])
        GH3, GL3 = t3(GH[:, 0:KT * TOK]), t3(GL[:, 0:KT * TOK])

        def par(name, k=0, n=1):
            return PAR[:, PCOL[name] + k:PCOL[name] + k + n]

        def half(ap, h):
            return ap[:, h * HALF:(h + 1) * HALF]

        def halves(ap):
            return ap.rearrange("p (h t) -> p h t", h=2)

        def banks(o):
            b = 2 * (o % 2)
            return PS[:, b:b + 2, 0:HALF]

        raw_landed = [sem(f"raw_landed{i}") for i in range(RAWS)]
        hi_ready, lo_ready = sem("hi_ready"), sem("lo_ready")
        tile_done = sem("tile_done")
        act_took, dve_took = sem("act_took"), sem("dve_took")
        act_chain, dve_chain, pool_chain = sem("act_chain"), sem("dve_chain"), sem("pool_chain")
        phase_end = sem("phase_end")
        x_back = sem("x_back")
        x_landed, par_landed, page_landed = sem("x_landed"), sem("par_landed"), sem("page_landed")
        cmp_landed, cache_landed = sem("cmp_landed"), [sem("cache_landed0"), sem("cache_landed1")]
        w2_landed, st_landed, p_landed = sem("w2_landed"), sem("st_landed"), sem("p_landed")
        consts_ready = sem("consts_ready")
        xh_ready, xl_ready = sem("xh_ready"), sem("xl_ready")
        gh_ready, gl_ready = sem("gh_ready"), sem("gl_ready")
        shift_landed = sem("shift_landed")
        cs_hi, cs_lo = sem("cs_hi"), sem("cs_lo")
        hid_sum, hid_ready, w2_done, w2_took = sem("hid_sum"), sem("hid_ready"), sem("w2_done"), sem("w2_took")
        tr_done, tr_took = sem("tr_done"), sem("tr_took")
        out_dma, gate_dma = sem("out_dma"), sem("gate_dma")
        sc_done, sc_masked, pc_ready, pct_done, pct_took = (sem("sc_done"), sem("sc_masked"), sem("pc_ready"),
                                                            sem("pct_done"), sem("pct_took"))
        s_done, negmax_ready, p_ready = sem("s_done"), sem("negmax_ready"), sem("p_ready")
        pt_done, pt_act, pt_dve, pv_done = sem("pt_done"), sem("pt_act"), sem("pt_dve"), sem("pv_done")
        o_ready, ot_done, ot_hi, ot_lo = sem("o_ready"), sem("ot_done"), sem("ot_hi"), sem("ot_lo")
        mean_done, d_ready, sq_ready, var_done = sem("mean_done"), sem("d_ready"), sem("sq_ready"), sem("var_done")
        r0_ready, n_ready, ln_out, res_ready = sem("r0_ready"), sem("n_ready"), sem("ln_out"), sem("res_ready")
        v_ready, rs_ready = sem("v_ready"), sem("rs_ready")
        ext_free, old_in, tap0_done, gelu_done = (sem("ext_free"), sem("old_in"),
                                                                      sem("tap0_done"), sem("gelu_done"))
        prod_done = sem("prod_done")
        ph_ready, pl_ready = sem("ph_ready"), sem("pl_ready")
        y_ready = sem("y_ready")
        rec_ready, m_ready, lam_ready, sp_ready = sem("rec_ready"), sem("m_ready"), sem("lam_ready"), sem("sp_ready")
        sig_ready, a_ready, sqrt_ready, h_ready, act_g = (sem("sig_ready"), sem("a_ready"), sem("sqrt_ready"),
                                                          sem("h_ready"), sem("act_g"))

        XL_COUNT = {name: 8 * n for n, name in enumerate(("x", "ln1_0", "x1", "ln1_1"))}
        GL_COUNT = {"ffn0": 1, "ln2_0": 25, "rec": 33, "gated": 41, "ffn1": 49, "ln2_1": 73}
        PROD0 = (2, 2 + 24 + 8 + 2)
        GATED0 = 26
        EXT0 = (4, 4 + 48 + 4)

        class Chain:

            def __init__(self, eng, s):
                self.eng, self.s, self.n = eng, s, 0

            def did(self, ins):
                self.n += 1
                ins.then_inc(self.s, 1)

            def sync(self):
                self.eng.wait_ge(self.s, self.n)

        def wait_taken(eng, o, t=None):
            who, n = taken(o)
            if t is None:
                eng.wait_ge(act_took if who == "act" else dve_took, n)
            elif who == "act":
                eng.wait_ge(act_took, 16 * t + n)
            else:
                eng.wait_ge(dve_took, 8 * t + n)

        def dyn(n, t, k):
            return n if t is None else k * t + n

        def at_phase(eng, n):
            eng.wait_ge(phase_end, 3 * n)
            if n == 1:
                eng.wait_ge(tr_done, 2)
            elif n == 2:
                eng.wait_ge(ot_done, 10)
            else:
                eng.wait_ge(tile_done, O0["rec"] if n == 3 else O0["ffn1"])

        def split_hi(act, c, t=None):
            s = c % SLOTS
            act.wait_ge(raw_landed[c % RAWS], dyn(16 * (c // RAWS + 1), t, 16 * 24 // RAWS))
            if c >= SLOTS:
                act.wait_ge(tile_done, dyn(LAST_USER[c - SLOTS] + 1, t, 24))
            nc.scalar.activation(HI[:, s * CH:(s + 1) * CH], RAW[:, (c % RAWS) * CH:(c % RAWS + 1) * CH],
                                 ACT.Copy).then_inc(hi_ready, 1)

        def split_lo(dve, c, t=None):
            s = c % SLOTS
            dve.wait_ge(hi_ready, dyn(c + 1, t, 24))
            nc.vector.tensor_tensor(LO[:, s * CH:(s + 1) * CH], RAW[:, (c % RAWS) * CH:(c % RAWS + 1) * CH],
                                    HI[:, s * CH:(s + 1) * CH].bitcast(F32), ALU.subtract).then_inc(lo_ready, 1)

        class Splits:

            def __init__(self, eng, fn):
                self.eng, self.fn, self.c = eng, fn, 0

            def after(self, o, t=None):
                upto = (USED_UP[o] if o >= 0 else 0) + AHEAD
                while self.c < upto:
                    if self.c < N_CHUNKS:
                        self.fn(self.eng, self.c, t)
                    self.c += 1

        block = ctx.enter_context(nc.Block())

        @block.sync
        def _(sp):
            W = a["w_stream"]

            def load(c, slot):
                sp.dma_start(RAW[:, slot * CH:(slot + 1) * CH], W[c * P:(c + 1) * P, :]).then_inc(raw_landed[slot], 16)

            sp.dma_start(X[:, :], a["x"]).then_inc(x_landed, 16)
            load(0, 0)
            load(1, 1)
            with sp.Fori(1, N_CHUNKS // RAWS) as r:
                for k in range(RAWS):
                    sp.wait_ge(lo_ready, RAWS * r + (k + 1 - RAWS))
                    sp.dma_start(RAW[:, k * CH:(k + 1) * CH],
                                 W[bass.ds((RAWS * r + k) * P, P), :]).then_inc(raw_landed[k], 16)
            for c in range(N_CHUNKS // RAWS * RAWS, N_CHUNKS):
                sp.wait_ge(lo_ready, c + 1 - RAWS)
                load(c, c % RAWS)

        @block.gpsimd
        def _(pool):
            g = nc.gpsimd
            chain = Chain(pool, pool_chain)
            pool.dma_start(PAGE[:, :], a["pages"]).then_inc(page_landed, 16)
            pool.dma_start(PAR[:, :], a["params"]).then_inc(par_landed, 16)
            pool.wait_ge(page_landed, 16)
            CR = CACHE.rearrange("p (n c) -> p n c", n=NB * PAGES)
            for n in range(NB * PAGES):
                pg = pool.value_load(PAGE[0:1, n:n + 1], min_val=0, max_val=a["cache_cmp"].shape[0] // P - 1)
                pool.dma_start(CR[:, n, :], a["cache_cmp"][bass.ds(pg * P, P), :]).then_inc(cmp_landed, 16)
            pool.dma_start(outs["win_old"], a["win_copy"]).then_inc(out_dma, 16)
            chain.did(g.memset(IDENT[:, :], 0.0))
            chain.did(g.memset(ONES[:, :], 1.0 / D))
            chain.did(g.memset(DMASK[:, :], 0.0))
            chain.did(g.memset(CMASK[:, :], 0.0))
            chain.did(g.memset(SMALL[:, 0:1], 1.0))
            chain.did(g.memset(SMALL[:, 1:512], 0.0))
            chain.sync()
            chain.did(g.affine_select(out=IDENT[:, :], in_=IDENT[:, :], compare_op=ALU.not_equal, fill=1.0, base=0,
                                      pattern=[[-1, P]], channel_multiplier=1))
            chain.did(g.affine_select(out=DMASK[:, :], in_=DMASK[:, :], compare_op=ALU.is_ge, fill=NEG, base=0,
                                      pattern=[[-1, P]], channel_multiplier=1))
            cm = CMASK[:, :].rearrange("p (i c) -> p i c", i=4)
            chain.did(g.affine_select(out=cm, in_=cm, compare_op=ALU.is_ge, fill=NEG, base=-31,
                                      pattern=[[P, 4], [-16, 32]], channel_multiplier=1))
            chain.did(g.affine_select(out=SMALL[:, 0:1], in_=SMALL[:, 0:1], compare_op=ALU.is_ge, fill=0.0, base=-31,
                                      pattern=[[0, 1]], channel_multiplier=1))
            chain.sync()
            chain.did(g.tensor_copy(IDENTB[:, :], IDENT[:, :]))
            chain.did(g.memset(cm[:, :, NC:NC + 1], NEG))
            chain.sync()
            pool.dma_start(SMASK[:, :], a["smask"]).then_inc(par_landed, 16)
            pool.dma_start(VP[:, 0:256], a["cmp_w2"]).then_inc(w2_landed, 16)
            g.memset(SMALL[:, 1:2], EPS).then_inc(consts_ready, 1)

            for kv in range(2):
                pool.wait_ge(act_took, kv + 1)
                for gg in range(2):
                    for pr in range(2):
                        src = KR[gg * 64:gg * 64 + 64, kv * 512 + pr * 256:kv * 512 + pr * 256 + 256]
                        dst = XPR[pr * 64:pr * 64 + 64, kv * 512 + gg * 256:kv * 512 + gg * 256 + 256]
                        pool.dma_start(dst, src).then_inc(shift_landed, 16)
            pool.wait_ge(act_took, 6)
            pool.dma_start(outs["kcmp"], KR).then_inc(out_dma, 16)
            pool.dma_start(outs["kt4"], KT4).then_inc(out_dma, 16)
            pool.dma_start(outs["ks"], KS).then_inc(out_dma, 16)
            pool.wait_ge(act_took, 7)
            gsc = a["gate_scratch"]
            with nc.allow_non_contiguous_dma(reason="48 gates per sampled token, 4 bytes each"):
                for h in range(2):
                    for bs in range(4 * NS):
                        rows = gsc[h].rearrange("(b j s) r -> b s j r", b=4, j=NJ)[bs // NS, bs % NS]
                        pool.dma_start(rows, GTC[0:48, h * HALF + HP + bs:h * HALF + HP + bs + 1]).then_inc(gate_dma, 16)
            pool.wait_ge(gate_dma, 16 * 32)
            for h in range(2):
                pool.dma_start(GS[:, h * 6:h * 6 + 6], gsc[h]).then_inc(gate_dma, 16)
            CA = CACHE.rearrange("p (k b n c) -> p k b n c", k=2, b=4, n=PAGES)

            def load_cache(hb):
                for bb in range(4):
                    b = 4 * hb + bb
                    for n in range(PAGES):
                        pg = pool.value_load(PAGE[0:1, b * PAGES + n:b * PAGES + n + 1], min_val=0,
                                             max_val=a["cache_sel"].shape[0] // P - 1)
                        pool.dma_start(CA[:, 0, bb, n, :], a["cache_sel"][bass.ds(pg * P, P), :])\
                            .then_inc(cache_landed[hb], 16)
                    pool.dma_start(CACHE[:, 4096 + bb * 1024:4096 + (bb + 1) * 1024], a["cache_win"][b])\
                        .then_inc(cache_landed[hb], 16)

            pool.wait_ge(cs_lo, 4)
            load_cache(0)
            pool.wait_ge(out_dma, 64)
            g.memset(SMALL[:, 501:502], 0.0).then_inc(phase_end, 1)
            pool.wait_ge(s_done, 64)
            pool.dma_start(X[:, :], a["x"]).then_inc(x_back, 16)
            pool.wait_ge(pv_done, 66)
            load_cache(1)
            g.memset(SMALL[:, 502:503], 0.0).then_inc(phase_end, 1)

            def tail(layer, ph):
                base_a = taken(O0[f"ffn{layer}"])[1] - 1
                at_phase(pool, ph)
                pool.dma_start(ST[:, :], a["ffn_state"][layer]).then_inc(st_landed, 16)
                pool.dma_start(PRAW[:, :], a["p"][layer]).then_inc(p_landed, 16)
                ln(2 * layer, "ln_mg", "ln_mb", layer)
                for k in range(KT):
                    pool.wait_ge(xl_ready, XL_COUNT[f"ln1_{layer}"] + k + 1)
                    g.tensor_scalar(X3[:, k, :], X3[:, k, :], ALPHA, None, ALU.mult).then_inc(res_ready, 1)
                pool.wait_ge(st_landed, 16 * (layer + 1))
                nb = 48 * layer
                with pool.Fori(0, 3) as t:
                    for n in range(16):
                        f = (n // 2) if n % 2 == 0 else 24 + n // 2
                        e = EXT[:, (n % 4) * U:(n % 4 + 1) * U]
                        es = e[:, 2 + SEQ:U].rearrange("p (b c) -> p b c", b=NB)
                        cv = CV[:, (n % 4) * U:(n % 4) * U + UO]
                        pool.wait_ge(ext_free, 16 * t + (nb + 4 * layer + n + 1))
                        g.tensor_copy(CWS[:, 4 * (n % 4):4 * (n % 4) + 4],
                                      PAR[:, bass.ds(32 * t + (PCOL[f"conv{layer}"] + 4 * f), 4)]).then_inc(pool_chain, 1)
                        g.tensor_copy(es[:, :, 0:2], ST[:, bass.ds(128 * t + 16 * f, 16)]
                                      .rearrange("p (b c) -> p b c", b=NB)).then_inc(old_in, 1)
                        pool.wait_ge(act_took, 16 * t + (base_a + n + 1))
                        pool.wait_ge(old_in, 16 * t + (nb + n + 1))
                        pool.wait_ge(prod_done, 8 * t + (PROD0[layer] + n // 2 - 1))
                        g.tensor_copy(CS[:, bass.ds(144 * t + 18 * f, 2)], e[:, SEQ:SEQ + 2]).then_inc(pool_chain, 1)
                        g.tensor_copy(CS[:, bass.ds(144 * t + (18 * f + 2), 16)].rearrange("p (b c) -> p b c", b=NB),
                                      es[:, :, 4:6]).then_inc(pool_chain, 1)
                        g.tensor_scalar(cv, e[:, 0:UO], CWS[:, 4 * (n % 4):4 * (n % 4) + 1],
                                        CWS[:, 4 * (n % 4) + 3:4 * (n % 4) + 4], ALU.mult, ALU.add)\
                            .then_inc(tap0_done, 1)
                chain.n += 3 * 48
                chain.sync()
                pool.dma_start(outs["ffn_conv"][layer], CS[:, :]).then_inc(out_dma, 16)
                ln(2 * layer + 1, "ln_fg", "ln_fb", layer)

            def ln(idx, gn, bn, layer):
                for k in range(KT):
                    pool.wait_ge(n_ready, 8 * idx + k + 1)
                    g.tensor_scalar(X3[:, k, :], X3[:, k, :], par(f"{gn}{layer}", k), par(f"{bn}{layer}", k),
                                    ALU.mult, ALU.add).then_inc(ln_out, 1)

            pool.wait_ge(par_landed, 32)
            tail(0, 2)
            pool.wait_ge(out_dma, 80)
            g.memset(SMALL[:, 503:504], 0.0).then_inc(phase_end, 1)
            at_phase(pool, 3)
            pool.wait_ge(h_ready, 9)
            pool.dma_start(outs["rg"], LAST[:, :]).then_inc(out_dma, 16)
            pool.wait_ge(out_dma, 96)
            g.memset(SMALL[:, 504:505], 0.0).then_inc(phase_end, 1)
            tail(1, 4)
            pool.wait_ge(y_ready, 16)
            pool.dma_start(outs["y"], X[:, :]).then_inc(out_dma, 16)
            pool.wait_ge(out_dma, 128)

        @block.scalar
        def _(act):
            s = nc.scalar
            chain = Chain(act, act_chain)
            splits = Splits(act, split_hi)
            act.wait_ge(x_landed, 16)
            for k in range(KT):
                s.activation(XH3[:, k, :], X3[:, k, :], ACT.Copy).then_inc(xh_ready, 1)
                if k in (0, 1, 2):
                    splits.c = k
                    split_hi(act, k)
            splits.c = 3
            CR = CACHE.rearrange("p (n v m c) -> p n v m c", n=NB * PAGES, v=2, m=16)

            def cmp_hi(kv, dst):
                out = dst[:, 0:4096].rearrange("p (m b n c) -> p b n m c", m=16, b=NB, n=PAGES)
                for b in range(NB):
                    ins = s.activation(out[:, b], CR[:, b * PAGES:(b + 1) * PAGES, kv], ACT.Copy)
                    if b < NB - 1:
                        chain.did(ins)
                ins.then_inc(cs_hi, 1)

            def cmp_hi_prompt(kv, dst):
                out = dst[:, 4096:OPW].rearrange("p (m c) -> p m c", m=8)
                for gg in range(2):
                    chain.did(s.activation(out[:, :, gg * 32:gg * 32 + 32],
                                           XPR[:, kv * 512 + gg * 256:kv * 512 + gg * 256 + 256]
                                           .rearrange("p (m c) -> p m c", m=8), ACT.Copy))
                s.activation(out[:, :, 64:66], par("pe", kv * 16, 16).rearrange("p (m c) -> p m c", m=8),
                             ACT.Copy).then_inc(cs_hi, 1)

            for n in range(15):
                act.wait_ge(tile_done, n + 1)
                o = banks(n)
                if n < 2:
                    for h in range(2):
                        dst = KR[:, n * 512:(n + 1) * 512].rearrange("p (r m h c) -> p h c m r", r=2, m=8, h=2)
                        chain.did(s.activation(dst[:, h], o[:, h, 0:HP].rearrange("p (c m r) -> p c m r", m=8, r=2),
                                               ACT.Copy))
                elif n < 6:
                    chain.did(s.activation(KT4[:, (n - 2) * SEQ:(n - 1) * SEQ].rearrange("p (h t) -> p h t", h=2),
                                           o[:, :, 0:HP], ACT.Copy))
                elif n == 6:
                    s.activation(halves(GTC[0:48, :]), o[0:48, :, :], ACT.Sigmoid).then_inc(act_took, 1)
                else:
                    j = n - 7
                    if j == 0:
                        act.wait_ge(xl_ready, 8)
                    chain.did(s.activation(Q[:, j, :].rearrange("p (h t) -> p h t", h=2), o[:, :, 0:HP], ACT.Copy))
                    qs = QS.rearrange("p (h b j s) -> p h b j s", h=2, b=4, j=NJ)
                    s.activation(qs[:, :, :, j, :], o[:, :, HP:HALF].rearrange("p h (b s) -> p h b s", b=4),
                                 ACT.Copy).then_inc(act_took, 1)
                if n < 6:
                    s.activation(KS[:, n * 32:(n + 1) * 32].rearrange("p (h t) -> p h t", h=2), o[:, :, HP:HALF],
                                 ACT.Copy).then_inc(act_took, 1)
                splits.after(n)
                if n == 3:
                    act.wait_ge(cmp_landed, 16 * NB * PAGES)
                    cmp_hi(0, GH)
            act.wait_ge(shift_landed, 128)
            act.wait_ge(par_landed, 32)
            cmp_hi_prompt(0, GH)
            cmp_hi(1, XH)
            cmp_hi_prompt(1, XH)
            for n in range(8):
                kv, hh = n // 4, (n // 2) % 2
                o = O0["cmp"] + n
                b = 2 * (o % 2)
                if n % 2 == 0:
                    act.wait_ge(tile_done, o + 1)
                    if n:
                        act.wait_ge(hid_sum, n // 2)
                    chain.did(s.activation(AT[:, 0:512], PS[:, b, :], ACT.Copy))
                    s.activation(AT[:, 512:578], PS[:, b + 1, 0:66], ACT.Copy).then_inc(act_took, 1)
                else:
                    act.wait_ge(hid_sum, n // 2 + 1)
                    bt = SMALL[:, 8 + n // 2:9 + n // 2]
                    hs = HS[:, hh * 512:(hh + 1) * 512].rearrange("p (r c) -> p r c", c=32)[:, :, 0:NC]
                    hp = HPR[:, hh * 64:(hh + 1) * 64].rearrange("p (r c) -> p r c", c=32)[:, :, 0:NC]
                    chain.did(s.activation(hs, hs, ACT.Gelu_apprx_tanh, bias=bt))
                    s.activation(hp, hp, ACT.Gelu_apprx_tanh, bias=bt).then_inc(hid_ready, 1)
                splits.after(o)
                if n == 3:
                    act.wait_ge(w2_done, 1)
                    chain.did(s.activation(KC, PS[:, 4, 0:256], ACT.Copy))
                    s.activation(KCP, PS[:, 5, 0:32], ACT.Copy).then_inc(w2_took, 1)
                if n == 7:
                    act.wait_ge(w2_done, 2)
                    vm = VM[0:32, :].rearrange("p (h c) -> p h c", h=2)
                    chain.did(s.activation(vm, PS[0:32, 6:8, :], ACT.Copy))
                    s.activation(VCP, PS[:, 5, 0:128], ACT.Copy).then_inc(w2_took, 1)
            act.wait_ge(tr_done, 1)
            chain.did(s.activation(VP.rearrange("p (h c) -> p h c", h=2), PS[:, 0:2, :], ACT.Copy))
            s.activation(GT, PS[:, 2, 0:192], ACT.Copy).then_inc(tr_took, 1)
            act.wait_ge(tr_done, 2)
            for r in (32, 64):
                ins = s.activation(VM[r:r + 4, :].rearrange("p (h c) -> p h c", h=2),
                                   PS[r:r + 4, (4 if r == 32 else 6):(6 if r == 32 else 8), :], ACT.Copy)
                if r == 32:
                    chain.did(ins)
            ins.then_inc(phase_end, 1)
            at_phase(act, 1)
            P4 = PB.rearrange("p (u r k) -> p u r k", u=2, r=2)
            PT3 = PT.rearrange("p (r k) -> p r k", r=2)
            SUMS = SMALL[:, 64:64 + 96].rearrange("p (u c) -> p u c", u=2)

            def exps(u, w):
                act.wait_ge(negmax_ready, u + 1)
                if u >= 2:
                    act.wait_ge(pt_done, u - 1)
                jj, gg = (u // 2) % NJ, u % 2
                for r in range(2):
                    c = (u // 16 % 2, jj * 6 + gg * 3 + 1 + r)
                    ins = s.activation(P4[:, u % 2, r, 0:w], PS[:, 2 * (u % 2) + r, 0:w], ACT.Exp, scale=SCALE,
                                       bias=SMALL[:, 16 + 2 * (u % 2) + r:17 + 2 * (u % 2) + r],
                                       accum_out=SUMS[:, c[0], c[1]:c[1] + 1])
                    if r == 0:
                        chain.did(ins)
                ins.then_inc(p_ready, 1)

            for i in range(4):
                w = P * (i + 1)
                act.wait_ge(sc_masked, i + 1)
                s.activation(SC, SC, ACT.Exp, scale=SCALE).then_inc(pc_ready, 1)
                act.wait_ge(pct_done, i + 1)
                s.activation(PCT, PS[:, 4, :], ACT.Copy).then_inc(pct_took, 1)
                exps(16 * i, w)
                for v in range(16):
                    u = 16 * i + v
                    if v < 15:
                        exps(u + 1, w)
                    act.wait_ge(pt_done, u + 1)
                    if u:
                        act.wait_ge(pv_done, u)
                    s.activation(PT3[:, 1, 0:w], PS[:, 5, 0:w], ACT.Copy).then_inc(pt_act, 1)
                    if v % 8 == 7:
                        n = u // 8
                        act.wait_ge(ot_done, n + 1)
                        jj = 4 * (n % 2)
                        c0 = (i // 2) * HALF + P * (i % 2)
                        s.activation(XH3[:, jj:jj + 4, c0:c0 + P], PS[:, 4, :].rearrange("p (j t) -> p j t", j=4),
                                     ACT.Copy).then_inc(ot_hi, 1)
            PMS = SC[:, 0:96]
            for v in range(4):
                u = 64 + v
                hb, gg = v // 2, v % 2
                act.wait_ge(negmax_ready, u + 1)
                act.wait_ge(pt_done, u - 1)
                nm = lambda r: SMALL[:, 24 + r:25 + r]
                sm = lambda r: SMALL[:, 32 + r:33 + r]
                for r in range(2):
                    chain.did(s.activation(P4[:, u % 2, r, :], PS[:, 2 * (u % 2) + r, :], ACT.Exp, scale=SCALE,
                                           bias=nm(1 + r), accum_out=sm(1 + r)))
                    reg = PMS[:, 32 * (r + 1):32 * (r + 1) + 4]
                    chain.did(s.activation(reg, reg, ACT.Exp, scale=SCALE, bias=nm(1 + r), accum_out=sm(3 + r)))
                s.activation(PMS[:, 0:32], PMS[:, 0:32], ACT.Exp, scale=SCALE, bias=nm(0), accum_out=sm(0))\
                    .then_inc(p_ready, 1)
                act.wait_ge(pt_done, u + 1)
                s.activation(PT3[:, 1, :], PS[:, 5, :], ACT.Copy).then_inc(pt_act, 1)
                if gg == 1:
                    act.wait_ge(ot_done, 8 + hb + 1)
                    xo = XH3[:, :, hb * HALF + HP:(hb + 1) * HALF].rearrange("p j (b s) -> p b j s", b=4)
                    s.activation(xo, PS[:, 4, 0:P].rearrange("p (b j s) -> p b j s", b=4, j=NJ), ACT.Copy)\
                        .then_inc(ot_hi, 1)
            act.wait_ge(ot_hi, 10)
            s.activation(SMALL[:, 509:510], SMALL[:, 1:2], ACT.Copy).then_inc(phase_end, 1)
            for k in range(8):
                act.wait_ge(tile_done, O0["w_out"] + k + 1)
                splits.after(O0["w_out"] + k)

            def ln(idx, outh, sem_h):
                for k in range(KT):
                    act.wait_ge(d_ready, 8 * idx + k + 1)
                    if k >= 2 or idx > 0:
                        act.wait_ge(var_done, 8 * idx + k - 1)
                    s.activation(SQ[:, (k % 2) * TOK:(k % 2 + 1) * TOK], X3[:, k, :], ACT.Square).then_inc(sq_ready, 1)
                act.wait_ge(v_ready, idx + 1)
                chain.did(s.activation(RS, LT[:, 0:TOK], ACT.Ln))
                chain.sync()
                s.activation(RS, RS, ACT.Exp, scale=-0.5).then_inc(r0_ready, 1)
                for k in range(KT):
                    act.wait_ge(ln_out, 8 * idx + k + 1)
                    s.activation(outh[:, k, :], X3[:, k, :], ACT.Copy).then_inc(sem_h, 1)

            def tail(layer):
                if layer == 0:
                    s.activation(SMALL[:, 508:509], SMALL[:, 1:2], ACT.Copy).then_inc(gh_ready, 1)
                ln(2 * layer, XH3, xh_ready)
                base = O0[f"ffn{layer}"]
                nb = 48 * layer
                at_a = taken(base)[1] - 1
                c_start = splits.c
                with act.Fori(0, 3) as t:
                    for n in range(16):
                        e = EXT[:, (n % 4) * U:(n % 4 + 1) * U]
                        es = e[:, 2 + SEQ:U].rearrange("p (h b c) -> p h b c", h=2, b=4)
                        act.wait_ge(tile_done, 24 * t + (base + n + 1))
                        act.wait_ge(ext_free, 16 * t + (nb + 4 * layer + n + 1))
                        o = banks(base + n)
                        s.activation(e[:, 2:2 + SEQ].rearrange("p (h t) -> p h t", h=2), o[:, :, 0:HP], ACT.Copy)\
                            .then_inc(act_chain, 1)
                        s.activation(es[:, :, :, 2:6], o[:, :, HP:HALF].rearrange("p h (b s) -> p h b s", b=4),
                                     ACT.Copy).then_inc(act_took, 1)
                        splits.after(base + n, t)
                        if n % 2 == 1:
                            p = n // 2
                            act.wait_ge(ext_free, 16 * t + (EXT0[layer] + n))
                            s.activation(G1[:, 0:UO], CV[:, ((n - 1) % 4) * U:((n - 1) % 4) * U + UO], ACT.Gelu_apprx_tanh)\
                                .then_inc(gelu_done, 1)
                            act.wait_ge(prod_done, 8 * t + (PROD0[layer] + p + 1))
                            s.activation(GH3[:, p, :], PR, ACT.Copy).then_inc(gh_ready, 1)
                    for n in range(8):
                        act.wait_ge(tile_done, 24 * t + (base + 16 + n + 1))
                        splits.after(base + 16 + n, t)
                    splits.c = c_start
                splits.c = c_start + 72
                chain.n += 48
                act.wait_ge(p_landed, 16 * (layer + 1))
                s.activation(XH[:, 0:2 * TOK], PRAW, ACT.Copy).then_inc(ph_ready, 1)
                ln_proj(2 * layer + 1, layer)
                for k in range(KT):
                    o = O0[f"gate{layer}"] + k
                    act.wait_ge(tile_done, o + 1)
                    if k >= 2:
                        act.wait_ge(y_ready, 8 * layer + k - 1)
                    s.activation(halves(LT[:, (k % 2) * TOK:(k % 2 + 1) * TOK]), banks(o), ACT.Sigmoid)\
                        .then_inc(act_took, 1)
                    splits.after(o)
                    if layer == 0:
                        act.wait_ge(y_ready, k + 1)
                        s.activation(XH3[:, k, :], X3[:, k, :], ACT.Copy).then_inc(xh_ready, 1)

            def ln_proj(idx, layer):
                for k in range(KT):
                    act.wait_ge(d_ready, 8 * idx + k + 1)
                    act.wait_ge(var_done, 8 * idx + k - 1)
                    s.activation(SQ[:, (k % 2) * TOK:(k % 2 + 1) * TOK], X3[:, k, :], ACT.Square).then_inc(sq_ready, 1)

                def proj(k):
                    o = O0[f"proj{layer}"] + k
                    act.wait_ge(tile_done, o + 1)
                    s.activation(halves(PP3[:, k, :]), banks(o), ACT.Copy).then_inc(act_took, 1)
                    splits.after(o)

                proj(0)
                proj(1)
                act.wait_ge(v_ready, idx + 1)
                chain.did(s.activation(RS, LT[:, 0:TOK], ACT.Ln))
                chain.sync()
                s.activation(RS, RS, ACT.Exp, scale=-0.5).then_inc(r0_ready, 1)
                for k in range(KT):
                    if k < 6:
                        proj(k + 2)
                    act.wait_ge(ln_out, 8 * idx + k + 1)
                    s.activation(GH3[:, k, :], X3[:, k, :], ACT.Copy).then_inc(gh_ready, 1)

            tail(0)
            s.activation(SMALL[:, 509:510], SMALL[:, 1:2], ACT.Copy).then_inc(phase_end, 1)
            at_phase(act, 3)
            act.wait_ge(lam_ready, 1)
            s.activation(SMALL[:, 40:48], SMALL[:, 40:48], ACT.Exp, scale=-1.0).then_inc(sp_ready, 1)
            for n in range(8):
                o = O0["rec"] + n
                act.wait_ge(tile_done, o + 1)
                if n >= 2:
                    act.wait_ge(rec_ready, n - 1)
                else:
                    act.wait_ge(lam_ready, 2)
                e = REXT[:, (n % 2) * UR:(n % 2 + 1) * UR]
                es = e[:, 3 + SEQ:UR].rearrange("p (h b c) -> p h b c", h=2, b=4)
                chain.did(s.activation(e[:, 3:3 + SEQ].rearrange("p (h t) -> p h t", h=2), banks(o)[:, :, 0:HP], ACT.Copy))
                s.activation(es[:, :, :, 3:7], banks(o)[:, :, HP:HALF].rearrange("p h (b s) -> p h b s", b=4),
                             ACT.Copy).then_inc(act_took, 1)
                splits.after(o)
                act.wait_ge(rec_ready, n + 1)
                s.activation(GH3[:, n, :], REC3[:, n, :], ACT.Copy).then_inc(gh_ready, 1)
            act.wait_ge(sp_ready, 2)
            for n in range(8):
                o = O0["rgate"] + 2 * n
                act.wait_ge(tile_done, o + 1)
                s.activation(halves(RR3[:, n, :]), banks(o), ACT.Sigmoid, bias=par("ga_b", n)).then_inc(act_took, 1)
                act.wait_ge(tile_done, o + 2)
                if n >= 2:
                    act.wait_ge(m_ready, n - 1)
                s.activation(halves(RTM[:, (n % 2) * TOK:(n % 2 + 1) * TOK]), banks(o + 1), ACT.Sigmoid,
                             bias=par("gx_b", n)).then_inc(act_took, 1)
                splits.after(o + 1)
                act.wait_ge(act_took, taken(o)[1])
                s.activation(VV3[:, n, :], RR3[:, n, :], ACT.Tanh, scale=SMALL[:, 56 + n:57 + n]).then_inc(sig_ready, 1)
            act.wait_ge(sig_ready, 8)
            for n in range(8):
                s.activation(RR3[:, n, :], RR3[:, n, :], ACT.Exp, scale=SMALL[:, 48 + n:49 + n]).then_inc(a_ready, 1)
            for n in range(8):
                s.activation(VV3[:, n, :], VV3[:, n, :], ACT.Sqrt).then_inc(sqrt_ready, 1)
            for n in range(8):
                o = O0["gbr"] + n
                act.wait_ge(tile_done, o + 1)
                if n >= 2:
                    act.wait_ge(prod_done, GATED0 + n - 1)
                else:
                    act.wait_ge(m_ready, 8)
                s.activation(halves(RTM[:, (n % 2) * TOK:(n % 2 + 1) * TOK]), banks(o), ACT.Gelu_apprx_tanh)\
                    .then_inc(act_took, 1)
                splits.after(o)
                act.wait_ge(prod_done, GATED0 + n + 1)
                s.activation(GH3[:, n, :], REC3[:, n, :], ACT.Copy).then_inc(gh_ready, 1)
            for k in range(8):
                act.wait_ge(tile_done, O0["rg_out"] + k + 1)
                splits.after(O0["rg_out"] + k)
            s.activation(SMALL[:, 509:510], SMALL[:, 1:2], ACT.Copy).then_inc(phase_end, 1)
            tail(1)

        @block.vector
        def _(dve):
            v = nc.vector
            chain = Chain(dve, dve_chain)
            splits = Splits(dve, split_lo)

            def sub_lo(dst, full, hi, s):
                return v.tensor_tensor(dst, full, hi.bitcast(F32), ALU.subtract).then_inc(s, 1)

            dve.wait_ge(x_landed, 16)
            for k in range(KT):
                dve.wait_ge(xh_ready, k + 1)
                sub_lo(XL3[:, k, :], X3[:, k, :], XH3[:, k, :], xl_ready)
                if k in (0, 1, 2):
                    split_lo(dve, k)
            splits.c = 3
            CR = CACHE.rearrange("p (n v m c) -> p n v m c", n=NB * PAGES, v=2, m=16)

            def cmp_lo(kv, hi, dst, piece):
                dve.wait_ge(cs_hi, piece + 1)
                view = lambda t: t[:, 0:4096].rearrange("p (m b n c) -> p b n m c", m=16, b=NB, n=PAGES)
                for b in range(NB):
                    ins = v.tensor_tensor(view(dst)[:, b], CR[:, b * PAGES:(b + 1) * PAGES, kv],
                                          view(hi)[:, b].bitcast(F32), ALU.subtract)
                    if b < NB - 1:
                        chain.did(ins)
                ins.then_inc(cs_lo, 1)

            def cmp_lo_prompt(kv, hi, dst, piece):
                dve.wait_ge(cs_hi, piece + 1)
                view = lambda t: t[:, 4096:OPW].rearrange("p (m c) -> p m c", m=8)
                for gg in range(2):
                    cols = slice(gg * 32, gg * 32 + 32)
                    chain.did(v.tensor_tensor(view(dst)[:, :, cols],
                                              XPR[:, kv * 512 + gg * 256:kv * 512 + gg * 256 + 256]
                                              .rearrange("p (m c) -> p m c", m=8),
                                              view(hi)[:, :, cols].bitcast(F32), ALU.subtract))
                v.tensor_tensor(view(dst)[:, :, 64:66], par("pe", kv * 16, 16).rearrange("p (m c) -> p m c", m=8),
                                view(hi)[:, :, 64:66].bitcast(F32), ALU.subtract).then_inc(cs_lo, 1)

            for n in range(15):
                dve.wait_ge(tile_done, n + 1)
                splits.after(n)
                if n == 3:
                    cmp_lo(0, GH, GL, 0)
            cmp_lo_prompt(0, GH, GL, 1)
            cmp_lo(1, XH, XL, 2)
            cmp_lo_prompt(1, XH, XL, 3)
            dve.wait_ge(par_landed, 32)
            dve.wait_ge(consts_ready, 1)
            chain.did(v.memset(HS[:, :], 0.0))
            chain.did(v.memset(HPR[:, :], 0.0))
            chain.sync()
            for n in range(8):
                kv, hh = n // 4, (n // 2) % 2
                o = O0["cmp"] + n
                b = 2 * (o % 2)
                if n % 2:
                    dve.wait_ge(tile_done, o + 1)
                    dve.wait_ge(act_took, taken(o - 1)[1])
                    if n == 5:
                        dve.wait_ge(w2_done, 1)
                    rows = lambda ap: ap.rearrange("p (r c) -> p r c", c=32)
                    chain.did(v.tensor_tensor(rows(HS[:, hh * 512:(hh + 1) * 512])[:, :, 0:NC],
                                              rows(AT[:, 0:512])[:, :, 0:NC],
                                              rows(PS[:, b, :])[:, :, 1:32], ALU.add))
                    chain.did(v.tensor_tensor(rows(HPR[:, hh * 64:(hh + 1) * 64])[:, :, 0:NC],
                                              rows(AT[:, 512:576])[:, :, 0:NC],
                                              rows(PS[:, b + 1, 0:64])[:, :, 1:32], ALU.add))
                    bt = SMALL[:, 8 + n // 2:9 + n // 2]
                    chain.did(v.tensor_tensor(bt, AT[:, 576:577], PS[:, b + 1, 65:66], ALU.add))
                    chain.sync()
                    v.tensor_tensor(bt, bt, par("cmp_b1", n // 2), ALU.add).then_inc(hid_sum, 1)
                    dve.wait_ge(hid_sum, n // 2 + 1)
                    v.memset(SMALL[:, 6:7], 0.0).then_inc(dve_took, 1)
                splits.after(o)
            dve.wait_ge(consts_ready, 1)
            dve.wait_ge(tr_took, 1)
            g0 = GT[:, 0:48].rearrange("p (h r) -> p h r", r=3)[:, :, 0:1]
            dve.wait_ge(dve_took, 4)
            v.tensor_scalar(g0, g0, SMALL[:, 0:1], None, ALU.mult).then_inc(phase_end, 1)
            at_phase(dve, 1)
            PT3 = PT.rearrange("p (r k) -> p r k", r=2)
            SUMS = SMALL[:, 64:64 + 96].rearrange("p (u c) -> p u c", u=2)
            SCL = SMALL[:, 160:172]

            def neg_max(u, w):
                dve.wait_ge(s_done, u + 1)
                nm = SMALL[:, 16 + 2 * (u % 2):18 + 2 * (u % 2)]
                chain.did(v.tensor_reduce(nm, PS[:, 2 * (u % 2):2 * (u % 2) + 2, 0:w], AX_X, ALU.max))
                chain.sync()
                v.tensor_scalar(nm, nm, -SCALE, None, ALU.mult).then_inc(negmax_ready, 1)

            for i in range(4):
                w = P * (i + 1)
                sc3 = SC.rearrange("p (h c) -> p h c", c=32)
                dve.wait_ge(sc_done, i + 1)
                if i:
                    dve.wait_ge(pct_done, i)
                for gg in range(2):
                    chain.did(v.tensor_tensor(sc3[:, NJ * gg:NJ * gg + NJ, :],
                                              PS[:, 4 + gg, 0:256].rearrange("p (h c) -> p h c", c=32),
                                              CMASK[:, 32 * i:32 * i + 32].unsqueeze(1).to_broadcast([P, NJ, 32]),
                                              ALU.add))
                chain.sync()
                mx = SMALL[:, 176:192]
                chain.did(v.tensor_reduce(mx, sc3, AX_X, ALU.max))
                chain.sync()
                v.tensor_tensor(sc3, sc3, mx.unsqueeze(2).to_broadcast([P, 16, 32]), ALU.subtract)\
                    .then_inc(sc_masked, 1)
                neg_max(16 * i, w)
                neg_max(16 * i + 1, w)
                dve.wait_ge(pc_ready, i + 1)
                chain.did(v.tensor_reduce(SUMS[:, i % 2, :].rearrange("p (j g r) -> p g j r", g=2, r=3)[:, :, :, 0],
                                          SC.rearrange("p (g j c) -> p g j c", g=2, c=32), AX_X, ALU.add))
                for vv in range(16):
                    u = 16 * i + vv
                    dve.wait_ge(pt_done, u + 1)
                    if u:
                        dve.wait_ge(pv_done, u)
                    v.tensor_copy(PT3[:, 0, 0:w], PS[:, 4, 0:w]).then_inc(pt_dve, 1)
                    if vv < 14:
                        neg_max(u + 2, w)
                    if vv % 2:
                        pair = u // 2
                        j = pair % NJ
                        sc = SCL[:, 6 * (pair % 2):6 * (pair % 2) + 6]
                        dve.wait_ge(p_ready, u + 1)
                        chain.sync()
                        chain.did(v.reciprocal(sc, SUMS[:, i % 2, 6 * j:6 * j + 6]))
                        chain.sync()
                        chain.did(v.tensor_tensor(sc, sc, GT[:, 48 * i + 6 * j:48 * i + 6 * j + 6], ALU.mult))
                        chain.sync()
                        dve.wait_ge(pv_done, u + 1)
                        if vv in (1, 9) and u > 8:
                            dve.wait_ge(ot_done, u // 8)
                        ot = OTMP.rearrange("p (r d) -> p r d", r=6)
                        chain.did(v.tensor_tensor(ot, PS[:, 6 + pair % 2, 0:384].rearrange("p (r d) -> p r d", r=6),
                                                  sc.unsqueeze(2).to_broadcast([P, 6, HD]), ALU.mult))
                        chain.sync()
                        o4 = OTMP.rearrange("p (g r d) -> p g r d", g=2, r=3)
                        os = OS[:, (j % 4) * P:(j % 4 + 1) * P].rearrange("p (g d) -> p g d", g=2)
                        chain.did(v.tensor_tensor(os, o4[:, :, 0, :], o4[:, :, 1, :], ALU.add))
                        chain.sync()
                        v.tensor_tensor(os, os, o4[:, :, 2, :], ALU.add).then_inc(o_ready, 1)
                        dve.wait_ge(o_ready, pair + 1)
                    if vv % 8 == 7:
                        n = u // 8
                        dve.wait_ge(ot_hi, n + 1)
                        jj = 4 * (n % 2)
                        c0 = (i // 2) * HALF + P * (i % 2)
                        sub_lo(XL3[:, jj:jj + 4, c0:c0 + P], PS[:, 4, :].rearrange("p (j t) -> p j t", j=4),
                               XH3[:, jj:jj + 4, c0:c0 + P], ot_lo)
            PMS = SC[:, 0:96]
            chain.did(v.memset(PMS, 0.0))
            chain.sync()
            for vv in range(4):
                u = 64 + vv
                hb, gg = vv // 2, vv % 2
                dve.wait_ge(s_done, u + 1)
                if vv:
                    dve.wait_ge(pt_done, u)
                mb = PS[:, 6, :]
                w0 = PS[:, 2 * (u % 2) + 1, 0:4]
                chain.did(v.tensor_tensor(w0, w0, SMASK[:, 4:8], ALU.add))
                chain.did(v.tensor_copy(PMS[:, 0:32], mb[:, 0:32]))
                for r in (1, 2):
                    chain.did(v.tensor_tensor(PMS[:, 32 * r:32 * r + 4], mb[:, 32 * r:32 * r + 4], SMASK[:, 0:4], ALU.add))
                chain.sync()
                chain.did(v.memset(PMS[:, NC:NC + 1], NEG))
                nm, nm2 = SMALL[:, 24:27], SMALL[:, 28:30]
                chain.did(v.tensor_reduce(nm[:, 1:3], PS[:, 2 * (u % 2):2 * (u % 2) + 2, :], AX_X, ALU.max))
                chain.did(v.tensor_reduce(nm2, PMS[:, 32:96].rearrange("p (r c) -> p r c", r=2)[:, :, 0:4], AX_X, ALU.max))
                chain.sync()
                chain.did(v.tensor_reduce(nm[:, 0:1], PMS[:, 0:32], AX_X, ALU.max))
                chain.did(v.tensor_tensor(nm[:, 1:3], nm[:, 1:3], nm2, ALU.max))
                chain.sync()
                v.tensor_scalar(nm, nm, -SCALE, None, ALU.mult).then_inc(negmax_ready, 1)
                dve.wait_ge(pt_done, u + 1)
                dve.wait_ge(pv_done, u)
                chain.did(v.tensor_copy(OTMP[0:96, 256:384], PS[0:96, 6, 128:256]))
                v.tensor_copy(PT3[:, 0, :], PS[:, 4, :]).then_inc(pt_dve, 1)
                dve.wait_ge(p_ready, u + 1)
                sums = SMALL[:, 32:37]
                chain.did(v.tensor_tensor(sums[:, 1:3], sums[:, 1:3], sums[:, 3:5], ALU.add))
                chain.sync()
                sc = SCL[:, 0:3]
                chain.did(v.reciprocal(sc, sums[:, 0:3]))
                chain.sync()
                if vv == 0:
                    dve.wait_ge(gate_dma, 16 * 34)
                chain.did(v.tensor_tensor(sc, sc, GS[:, 6 * hb + 3 * gg:6 * hb + 3 * gg + 3], ALU.mult))
                chain.sync()
                dve.wait_ge(pv_done, u + 1)
                if gg == 0:
                    dve.wait_ge(ot_done, 8 + hb)
                o3 = OTMP[:, 0:192].rearrange("p (r d) -> p r d", r=3)
                chain.did(v.tensor_copy(o3, PS[:, 7, 0:192].rearrange("p (r d) -> p r d", r=3)))
                chain.sync()
                chain.did(v.tensor_tensor(o3[:, 1:3, :], o3[:, 1:3, :], PS[:, 2 * (u % 2):2 * (u % 2) + 2, 0:HD], ALU.add))
                chain.sync()
                chain.did(v.tensor_tensor(o3, o3, sc.unsqueeze(2).to_broadcast([P, 3, HD]), ALU.mult))
                chain.sync()
                os = OS[:, gg * HD:(gg + 1) * HD]
                chain.did(v.tensor_tensor(os, o3[:, 0, :], o3[:, 1, :], ALU.add))
                chain.sync()
                v.tensor_tensor(os, os, o3[:, 2, :], ALU.add).then_inc(o_ready, 1)
                dve.wait_ge(o_ready, 32 + vv + 1)
                if gg == 1:
                    dve.wait_ge(ot_hi, 8 + hb + 1)
                    xo = lambda t: t[:, :, hb * HALF + HP:(hb + 1) * HALF].rearrange("p j (b s) -> p b j s", b=4)
                    sub_lo(xo(XL3), PS[:, 4, 0:P].rearrange("p (b j s) -> p b j s", b=4, j=NJ), xo(XH3), ot_lo)
            v.memset(SMALL[:, 6:7], 0.0).then_inc(phase_end, 1)
            at_phase(dve, 2)
            dve.wait_ge(x_back, 16)

            def residual(name):
                for k in range(KT):
                    o = O0[name] + k
                    dve.wait_ge(tile_done, o + 1)
                    v.scalar_tensor_tensor(out=halves(X3[:, k, :]), in0=halves(X3[:, k, :]), scalar=ALPHA,
                                           in1=banks(o), op0=ALU.mult, op1=ALU.add).then_inc(dve_took, 1)
                    splits.after(o)

            residual("w_out")

            def ln(idx, outh, outl, sem_h, h0, sem_l, last_o):
                dve.wait_ge(mean_done, idx + 1)
                dve.wait_ge(dve_took, taken(last_o)[1])
                for k in range(KT):
                    v.tensor_tensor(halves(X3[:, k, :]), halves(X3[:, k, :]), PS[:, 4:6, 0:HALF], ALU.subtract)\
                        .then_inc(d_ready, 1)
                dve.wait_ge(var_done, 8 * idx + 8)
                v.tensor_scalar(halves(LT[:, 0:TOK]), PS[:, 6:8, 0:HALF], EPS, None, ALU.add).then_inc(v_ready, 1)
                dve.wait_ge(r0_ready, idx + 1)
                tmp = LT[:, TOK:2 * TOK]
                chain.did(v.tensor_tensor(tmp, RS, RS, ALU.mult))
                chain.sync()
                chain.did(v.scalar_tensor_tensor(out=tmp, in0=tmp, scalar=-0.5, in1=LT[:, 0:TOK], op0=ALU.mult,
                                                 op1=ALU.mult))
                chain.sync()
                chain.did(v.scalar_tensor_tensor(out=RS, in0=tmp, scalar=1.5, in1=RS, op0=ALU.add, op1=ALU.mult))
                chain.sync()
                dve.wait_ge(d_ready, 8 * idx + 8)
                for k in range(KT):
                    if k >= 2:
                        lo_part(k - 2, outh, outl, sem_h, h0, sem_l)
                    v.tensor_tensor(X3[:, k, :], X3[:, k, :], RS, ALU.mult).then_inc(n_ready, 1)
                for k in (6, 7):
                    lo_part(k, outh, outl, sem_h, h0, sem_l)

            def lo_part(k, outh, outl, sem_h, h0, sem_l):
                dve.wait_ge(sem_h, h0 + k + 1)
                sub_lo(outl[:, k, :], X3[:, k, :], outh[:, k, :], sem_l)

            def tail(layer):
                for e in range(4):
                    v.memset(EXT[:, e * U:e * U + 2], 0.0).then_inc(ext_free, 1)
                for e in range(2):
                    v.memset(SMALL[:, 4 + e:5 + e], 0.0).then_inc(prod_done, 1)
                if layer == 0:
                    v.memset(SMALL[:, 7:8], 0.0).then_inc(gl_ready, 1)
                ln(2 * layer, XH3, XL3, xh_ready, XL_COUNT[f"ln1_{layer}"], xl_ready, O0[f"ffn{layer}"] - 1)
                base = O0[f"ffn{layer}"]
                nb = 48 * layer
                d0 = taken(base - 1)[1]
                c_start = splits.c
                n_chain = chain.n
                n_per = 16 + 8
                with dve.Fori(0, 3) as t:
                    for n in range(16):
                        e = EXT[:, (n % 4) * U:(n % 4 + 1) * U]
                        cv = CV[:, (n % 4) * U:(n % 4) * U + UO]
                        dve.wait_ge(tap0_done, 16 * t + (nb + n + 1))
                        v.scalar_tensor_tensor(out=cv, in0=e[:, 1:1 + UO],
                                               scalar=CWS[:, 4 * (n % 4) + 1:4 * (n % 4) + 2],
                                               in1=cv, op0=ALU.mult, op1=ALU.add).then_inc(dve_chain, 1)
                        dve.wait_ge(dve_chain, n_per * t + (n_chain + n + n // 2 + 1))
                        v.scalar_tensor_tensor(out=cv, in0=e[:, 2:2 + UO],
                                               scalar=CWS[:, 4 * (n % 4) + 2:4 * (n % 4) + 3],
                                               in1=cv, op0=ALU.mult, op1=ALU.add).then_inc(ext_free, 1)
                        splits.after(base + n, t)
                        if n % 2 == 1:
                            p = n // 2
                            dve.wait_ge(gelu_done, 8 * t + (24 * layer + p + 1))
                            dve.wait_ge(ext_free, 16 * t + (EXT0[layer] + n + 1))
                            dve.wait_ge(gl_ready, 8 * t + (GL_COUNT[f"ffn{layer}"] + p))
                            v.tensor_tensor(halves(PR)[:, :, 0:HP], G1[:, 0:SEQ].rearrange("p (h t) -> p h t", h=2),
                                            cv[:, 0:SEQ].rearrange("p (h t) -> p h t", h=2), ALU.mult)\
                                .then_inc(dve_chain, 1)
                            v.tensor_tensor(halves(PR)[:, :, HP:HALF].rearrange("p h (b s) -> p h b s", b=4),
                                            seqs(G1), seqs(CV[:, (n % 4) * U:(n % 4 + 1) * U]), ALU.mult).then_inc(prod_done, 1)
                            dve.wait_ge(gh_ready, 8 * t + (GL_COUNT[f"ffn{layer}"] + p + 1))
                            dve.wait_ge(prod_done, 8 * t + (PROD0[layer] + p + 1))
                            sub_lo(GL3[:, p, :], PR, GH3[:, p, :], gl_ready)
                    for n in range(8):
                        o = base + 16 + n
                        dve.wait_ge(tile_done, 24 * t + (o + 1))
                        if n == 0:
                            dve.wait_ge(res_ready, 8 * layer + 8)
                            dve.wait_ge(dve_took, 8 * t + d0)
                        v.tensor_tensor(halves(X3[:, n, :]), halves(X3[:, n, :]), banks(o), ALU.add).then_inc(dve_took, 1)
                        splits.after(o, t)
                    splits.c = c_start
                splits.c = c_start + 72
                chain.n = n_chain + 3 * n_per
                dve.wait_ge(ph_ready, layer + 1)
                sub_lo(XL[:, 0:2 * TOK], PRAW, XH[:, 0:2 * TOK], pl_ready)
                ln_proj(2 * layer + 1, layer)
                for k in range(KT):
                    o = O0[f"gate{layer}"] + k
                    lt = LT[:, (k % 2) * TOK:(k % 2 + 1) * TOK]
                    dve.wait_ge(act_took, taken(o)[1])
                    chain.did(v.tensor_tensor(PP3[:, k, :], PP3[:, k, :], lt, ALU.mult))
                    chain.sync()
                    v.tensor_tensor(X3[:, k, :], X3[:, k, :], PP3[:, k, :], ALU.add).then_inc(y_ready, 1)
                    splits.after(o)
                    if layer == 0:
                        dve.wait_ge(xh_ready, XL_COUNT["x1"] + k + 1)
                        sub_lo(XL3[:, k, :], X3[:, k, :], XH3[:, k, :], xl_ready)

            def seqs(ap):
                return ap[:, SEQ + 2:U].rearrange("p (h b c) -> p h b c", h=2, b=4)[:, :, :, 0:4]

            def ln_proj(idx, layer):
                dve.wait_ge(mean_done, idx + 1)
                dve.wait_ge(dve_took, taken(O0[f"proj{layer}"] - 1)[1])
                for k in range(KT):
                    v.tensor_tensor(halves(X3[:, k, :]), halves(X3[:, k, :]), PS[:, 4:6, 0:HALF], ALU.subtract)\
                        .then_inc(d_ready, 1)
                for k in range(2):
                    dve.wait_ge(tile_done, O0[f"proj{layer}"] + k + 1)
                    splits.after(O0[f"proj{layer}"] + k)
                dve.wait_ge(var_done, 8 * idx + 8)
                v.tensor_scalar(halves(LT[:, 0:TOK]), PS[:, 6:8, 0:HALF], EPS, None, ALU.add).then_inc(v_ready, 1)
                dve.wait_ge(r0_ready, idx + 1)
                tmp = LT[:, TOK:2 * TOK]
                chain.did(v.tensor_tensor(tmp, RS, RS, ALU.mult))
                chain.sync()
                chain.did(v.scalar_tensor_tensor(out=tmp, in0=tmp, scalar=-0.5, in1=LT[:, 0:TOK], op0=ALU.mult,
                                                 op1=ALU.mult))
                chain.sync()
                chain.did(v.scalar_tensor_tensor(out=RS, in0=tmp, scalar=1.5, in1=RS, op0=ALU.add, op1=ALU.mult))
                chain.sync()
                dve.wait_ge(d_ready, 8 * idx + 8)
                h0 = GL_COUNT[f"ln2_{layer}"]
                for k in range(KT):
                    v.tensor_tensor(X3[:, k, :], X3[:, k, :], RS, ALU.mult).then_inc(n_ready, 1)
                    if k < 6:
                        splits.after(O0[f"proj{layer}"] + k + 2)
                    if k >= 2:
                        lo_part(k - 2, GH3, GL3, gh_ready, h0, gl_ready)
                for k in (6, 7):
                    lo_part(k, GH3, GL3, gh_ready, h0, gl_ready)

            tail(0)
            v.memset(SMALL[:, 6:7], 0.0).then_inc(phase_end, 1)
            at_phase(dve, 3)
            lam = par("lam", 0, 8)
            z, sp = SMALL[:, 40:48], SMALL[:, 48:56]
            q, q2, acc = SMALL[:, 320:328], SMALL[:, 328:336], SMALL[:, 336:344]
            chain.did(v.tensor_scalar(z, lam, -1.0, None, ALU.mult))
            chain.sync()
            v.tensor_tensor(z, z, lam, ALU.max).then_inc(lam_ready, 1)

            def old_rows(n):
                e = REXT[:, (n % 2) * UR:(n % 2 + 1) * UR]
                es = e[:, 3 + SEQ:UR].rearrange("p (b c) -> p b c", b=NB)
                chain.did(v.tensor_copy(es[:, :, 0:3], par("rstate", 24 * n, 24).rearrange("p (b c) -> p b c", b=NB)))

            for n in range(2):
                chain.did(v.memset(REXT[:, n * UR:n * UR + 3], 0.0))
                old_rows(n)
            v.memset(SMALL[:, 7:8], 0.0).then_inc(lam_ready, 1)
            dve.wait_ge(sp_ready, 1)
            chain.did(v.tensor_scalar(q, z, 2.0, None, ALU.add))
            chain.sync()
            chain.did(v.reciprocal(q, q))
            chain.sync()
            chain.did(v.tensor_tensor(q, q, z, ALU.mult))
            chain.sync()
            chain.did(v.tensor_tensor(q2, q, q, ALU.mult))
            chain.did(v.memset(acc, 1.0 / 19))
            chain.sync()
            for m in range(17, 0, -2):
                chain.did(v.tensor_tensor(acc, acc, q2, ALU.mult))
                chain.sync()
                chain.did(v.tensor_scalar(acc, acc, 1.0 / m, None, ALU.add))
                chain.sync()
            chain.did(v.scalar_tensor_tensor(out=acc, in0=acc, scalar=2.0, in1=q, op0=ALU.mult, op1=ALU.mult))
            chain.did(v.tensor_scalar(sp, lam, -1.0, 0.0, ALU.mult, ALU.max))
            chain.sync()
            chain.did(v.tensor_tensor(sp, sp, acc, ALU.add))
            chain.sync()
            chain.did(v.tensor_scalar(SMALL[:, 56:64], sp, 4.0, None, ALU.mult))
            chain.sync()
            v.tensor_scalar(sp, sp, -8.0, None, ALU.mult).then_inc(sp_ready, 1)
            rg0 = GL_COUNT["rec"]
            for n in range(8):
                o = O0["rec"] + n
                e = REXT[:, (n % 2) * UR:(n % 2 + 1) * UR]
                es = e[:, 3 + SEQ:UR].rearrange("p (b c) -> p b c", b=NB)
                w = lambda k: par("rconv_w", 8 * k + n)
                dve.wait_ge(act_took, taken(o)[1])
                chain.did(v.tensor_scalar(RCV[:, 0:URO], e[:, 0:URO], w(0), par("rconv_b", n), ALU.mult, ALU.add))
                lt = LAST[:, 36 * n:36 * n + 36]
                chain.did(v.tensor_copy(lt[:, 0:3], e[:, SEQ:SEQ + 3]))
                chain.did(v.tensor_copy(lt[:, 3:27].rearrange("p (b c) -> p b c", b=NB), es[:, :, 4:7]))
                for k in (1, 2):
                    chain.sync()
                    chain.did(v.scalar_tensor_tensor(out=RCV[:, 0:URO], in0=e[:, k:k + URO], scalar=w(k), in1=RCV[:, 0:URO], op0=ALU.mult,
                                                     op1=ALU.add))
                chain.sync()
                r3 = halves(REC3[:, n, :])
                chain.did(v.scalar_tensor_tensor(out=r3[:, :, 0:HP], in0=e[:, 3:3 + SEQ].rearrange("p (h t) -> p h t", h=2),
                                                 scalar=w(3), in1=RCV[:, 0:SEQ].rearrange("p (h t) -> p h t", h=2),
                                                 op0=ALU.mult, op1=ALU.add))
                for h in range(2):
                    rows = RCV[:, SEQ + 3 + 28 * h:SEQ + 31 + 28 * h].rearrange("p (b c) -> p b c", b=4)[:, :, 0:4]
                    ins = v.scalar_tensor_tensor(out=r3[:, h, HP:HALF].rearrange("p (b s) -> p b s", b=4),
                                                 in0=es[:, 4 * h:4 * h + 4, 3:7], scalar=w(3),
                                                 in1=rows, op0=ALU.mult, op1=ALU.add)
                    if h == 0:
                        chain.did(ins)
                ins.then_inc(rec_ready, 1)
                dve.wait_ge(rec_ready, n + 1)
                if n < 6:
                    old_rows(n + 2)
                splits.after(o)
                dve.wait_ge(gh_ready, rg0 + n + 1)
                sub_lo(GL3[:, n, :], REC3[:, n, :], GH3[:, n, :], gl_ready)
            dve.wait_ge(gl_ready, rg0 + 8)
            for n in range(8):
                o = O0["rgate"] + 2 * n
                dve.wait_ge(act_took, taken(o + 1)[1])
                v.tensor_tensor(REC3[:, n, :], REC3[:, n, :], RTM[:, (n % 2) * TOK:(n % 2 + 1) * TOK], ALU.mult)\
                    .then_inc(m_ready, 1)
                splits.after(o + 1)
            dve.wait_ge(m_ready, 8)
            for n in range(8):
                dve.wait_ge(a_ready, n + 1)
                chain.did(v.scalar_tensor_tensor(out=REC3[:, n, :], in0=RR3[:, n, :], scalar=1.0, in1=REC3[:, n, :],
                                                 op0=ALU.add, op1=ALU.mult))
            for n in range(8):
                dve.wait_ge(sqrt_ready, n + 1)
                chain.sync()
                chain.did(v.tensor_tensor(VV3[:, n, :], VV3[:, n, :], REC3[:, n, :], ALU.mult))
                chain.sync()
                chain.did(v.tensor_tensor_scan(REC3[:, n, 0:HP], RR3[:, n, 0:HP], VV3[:, n, 0:HP], 0.0, ALU.mult, ALU.add))
                chain.sync()
                v.tensor_tensor_scan(REC3[:, n, HALF:HALF + HP], RR3[:, n, HALF:HALF + HP], VV3[:, n, HALF:HALF + HP],
                                     REC3[:, n, HP - 1:HP], ALU.mult, ALU.add).then_inc(h_ready, 1)
            smp = lambda t: t.rearrange("p (k t) -> p k t", k=16)[:, :, HP:HALF].rearrange("p k (b s) -> p k b s", b=4)
            prev = par("h0", 0, 64).rearrange("p (k b) -> p k b", k=16)
            tmp = SMALL[:, 256:320].rearrange("p (k b) -> p k b", k=16)
            for st in range(NS):
                chain.sync()
                chain.did(v.tensor_tensor(tmp, smp(RR)[:, :, :, st], prev, ALU.mult))
                chain.sync()
                chain.did(v.tensor_tensor(smp(REC)[:, :, :, st], tmp, smp(VV)[:, :, :, st], ALU.add))
                prev = smp(REC)[:, :, :, st]
            chain.sync()
            dve.wait_ge(h_ready, 8)
            l3 = LAST.rearrange("p (k c) -> p k c", k=8)
            chain.did(v.tensor_copy(l3[:, :, 27:28], REC3[:, :, HALF + HP - 1:HALF + HP]))
            v.tensor_copy(l3[:, :, 28:36].rearrange("p k (h b) -> p k h b", h=2),
                          smp(REC)[:, :, :, 3].rearrange("p (k h) b -> p k h b", h=2)).then_inc(h_ready, 1)
            dve.wait_ge(h_ready, 9)
            for n in range(8):
                o = O0["gbr"] + n
                dve.wait_ge(act_took, taken(o)[1])
                v.tensor_tensor(REC3[:, n, :], REC3[:, n, :], RTM[:, (n % 2) * TOK:(n % 2 + 1) * TOK], ALU.mult)\
                    .then_inc(prod_done, 1)
                splits.after(o)
                dve.wait_ge(gh_ready, GL_COUNT["gated"] + n + 1)
                dve.wait_ge(prod_done, GATED0 + n + 1)
                sub_lo(GL3[:, n, :], REC3[:, n, :], GH3[:, n, :], gl_ready)
            residual("rg_out")
            v.memset(SMALL[:, 6:7], 0.0).then_inc(phase_end, 1)
            at_phase(dve, 4)
            tail(1)

        @block.tensor
        def _(pe):
            mm, tr = nc.tensor.matmul, nc.tensor.transpose

            def wt(ring, c, k):
                at = (c % SLOTS) * CH + k * P
                return ring[:, at:at + P]

            def chunk_ready(c, t=None):
                pe.wait_ge(lo_ready, dyn(c + 1, t, 24))

            def tile(o, c, ks, xh, xl, x0, rows=P, t=None, each=None):
                chunk_ready(c, t)
                wait_taken(pe, o - 2, t) if o >= 2 else None
                b = 2 * (o % 2)
                for n, k in enumerate(ks):
                    if each:
                        each(n)
                    for w, parts in ((wt(HI, c, k), (xh, xl)), (wt(LO, c, k), (xh,))):
                        for x in parts:
                            for h in range(2):
                                first = n == 0 and w is not None and x is xh and parts[-1] is xl
                                last = n == len(ks) - 1 and len(parts) == 1
                                ins = mm(PS[0:rows, b + h, 0:HALF], w[:, 0:rows], x[:, x0 + n, h * HALF:(h + 1) * HALF],
                                         start=first, stop=last)
                ins.then_inc(tile_done, 1)

            for n in range(15):
                tile(n, C0["w_in"] + n, range(KT), XH3, XL3, 0, rows=48 if n == 6 else P,
                     each=(lambda k: pe.wait_ge(xl_ready, k + 1)) if n == 0 else None)
            for n in range(8):
                o, c = O0["cmp"] + n, C0["cmp"] + n
                kv = n // 4
                h_, l_ = ((GH, GL), (XH, XL))[kv]
                b = 2 * (o % 2)
                pe.wait_ge(cs_lo, 2 * kv + 2)
                chunk_ready(c)
                wait_taken(pe, o - 2)
                rows = lambda ap, m: ap[:, 0:4096].rearrange("p (g m c) -> p g m c", g=2, m=8)[:, :, m, :]
                pro = lambda ap, m: ap[:, 4096 + 66 * m:4096 + 66 * m + 66]
                for m in range(8):
                    for w, parts in ((wt(HI, c, m), (h_, l_)), (wt(LO, c, m), (h_,))):
                        for x in parts:
                            first, last = m == 0 and x is h_ and len(parts) == 2, m == 7 and len(parts) == 1
                            mm(PS[:, b, :].rearrange("p (g c) -> p g c", g=2), w, rows(x, m), start=first, stop=last)
                            ins = mm(PS[:, b + 1, 0:66], w, pro(x, m), start=first, stop=last)
                ins.then_inc(tile_done, 1)
                if n == 3:
                    pe.wait_ge(hid_ready, 2)
                    pe.wait_ge(w2_landed, 16)
                    for gg in range(2):
                        for hh in range(2):
                            mm(PS[64 * gg:64 * gg + 64, 4, 0:256], VP[:, hh * 64:hh * 64 + 64],
                               HS[:, hh * 512 + gg * 256:hh * 512 + gg * 256 + 256], start=hh == 0, stop=hh == 1)
                    for gg in range(2):
                        for hh in range(2):
                            ins = mm(PS[64 * gg:64 * gg + 64, 5, 0:32], VP[:, hh * 64:hh * 64 + 64],
                                     HPR[:, hh * 64 + gg * 32:hh * 64 + gg * 32 + 32], start=hh == 0, stop=hh == 1)
                    ins.then_inc(w2_done, 1)
            pe.wait_ge(hid_ready, 4)
            pe.wait_ge(w2_took, 1)
            for b in range(NB):
                for gg in range(2):
                    for hh in range(2):
                        mm(PS[0:32, 6 + b // 4, (b % 4) * P + gg * HD:(b % 4) * P + gg * HD + HD],
                           HS[:, hh * 512 + gg * 256 + b * 32:hh * 512 + gg * 256 + b * 32 + 32],
                           VP[:, 128 + hh * 64:128 + hh * 64 + 64], start=hh == 0, stop=hh == 1)
            for r in range(4):
                for gg in range(2):
                    for hh in range(2):
                        ins = mm(PS[32 * r:32 * r + 32, 5, gg * HD:gg * HD + HD],
                                 HPR[:, hh * 64 + gg * 32:hh * 64 + gg * 32 + 32],
                                 VP[:, 128 + hh * 64:128 + hh * 64 + 64], start=hh == 0, stop=hh == 1)
            ins.then_inc(w2_done, 1)
            pe.wait_ge(consts_ready, 1)
            wait_taken(pe, O0["w_out"] - 1)
            wait_taken(pe, O0["w_out"] - 2)
            for r in range(2):
                for kt in range(4):
                    tr(PS[:, r, kt * P:(kt + 1) * P], KT4[:, (2 * r + 1) * SEQ + kt * P:(2 * r + 1) * SEQ + (kt + 1) * P],
                       IDENT[:, :])
            for i in range(4):
                c0 = (i // 2) * HALF + P * (i % 2)
                ins = tr(PS[:, 2, 48 * i:48 * i + 48], GTC[0:48, c0:c0 + P], IDENT[0:48, 0:48])
            ins.then_inc(tr_done, 1)
            pe.wait_ge(w2_took, 2)
            for r, (row, tl) in enumerate(((32, 3), (64, 5))):
                for b in range(NB):
                    ins = mm(PS[row:row + 4, 4 + 2 * r + b // 4, (b % 4) * P:(b % 4 + 1) * P],
                             KS[:, tl * 32 + 4 * b:tl * 32 + 4 * b + 4], IDENT[:, :], start=True, stop=True)
            ins.then_inc(tr_done, 1)
            at_phase(pe, 1)
            P4 = PB.rearrange("p (u r k) -> p u r k", u=2, r=2)
            PT3 = PT.rearrange("p (r k) -> p r k", r=2)

            def scores(u):
                i, j, gg = u // 16, (u // 2) % NJ, u % 2
                w = P * (i + 1)
                rows = slice(64 * gg, 64 * gg + 64)
                if u >= 2:
                    pe.wait_ge(p_ready, u - 1)
                for r in range(2):
                    b = 2 * (u % 2) + r
                    mm(PS[:, b, 0:w], Q[rows, j, i * P:(i + 1) * P], KT4[rows, 2 * r * SEQ:2 * r * SEQ + w],
                       start=True, stop=False)
                    ins = mm(PS[:, b, w - P:w], IDENTB[:, :], DMASK[:, :], start=False, stop=True)
                ins.then_inc(s_done, 1)

            def trans(u, w):
                pe.wait_ge(p_ready, u + 1)
                if u:
                    pe.wait_ge(pt_act, u)
                    pe.wait_ge(pt_dve, u)
                for r in range(2):
                    for kt in range(w // P):
                        ins = tr(PS[:, 4 + r, kt * P:(kt + 1) * P], P4[:, u % 2, r, kt * P:(kt + 1) * P], IDENT[:, :])
                return ins

            for i in range(4):
                w = P * (i + 1)
                if i:
                    pe.wait_ge(pt_act, 16 * i)
                    pe.wait_ge(pt_dve, 16 * i)
                    pe.wait_ge(ot_lo, 2 * i)
                for gg in range(2):
                    for j in range(NJ):
                        rows = slice(64 * gg, 64 * gg + 64)
                        ins = mm(PS[:, 4 + gg, 32 * j:32 * j + 32], Q[rows, j, i * P:(i + 1) * P],
                                 KCP[rows, :], start=True, stop=True)
                ins.then_inc(sc_done, 1)
                scores(16 * i)
                scores(16 * i + 1)
                pe.wait_ge(pc_ready, i + 1)
                for n in range(4):
                    ins = tr(PS[:, 4, n * P:(n + 1) * P], SC[:, n * P:(n + 1) * P], IDENT[:, :])
                ins.then_inc(pct_done, 1)
                pe.wait_ge(pct_took, i + 1)
                for v in range(16):
                    u = 16 * i + v
                    j, gg = v // 2, v % 2
                    pair = u // 2
                    if v == 8:
                        pe.wait_ge(ot_lo, u // 8)
                    trans(u, w).then_inc(pt_done, 1)
                    if v < 14:
                        scores(u + 2)
                    pe.wait_ge(pt_act, u + 1)
                    pe.wait_ge(pt_dve, u + 1)
                    if pair >= 2 and gg == 0:
                        pe.wait_ge(o_ready, pair - 1)
                    ob = PS[:, 6 + pair % 2, gg * 192:gg * 192 + 192]
                    hh = NJ * gg + j
                    hr = slice(32 * (hh % 4), 32 * (hh % 4) + 32)
                    mm(ob[:, 0:HD], PCT[hr, (hh // 4) * P:(hh // 4 + 1) * P], VCP[hr, gg * HD:gg * HD + HD],
                       start=True, stop=True)
                    for r in range(2):
                        for kt in range(w // P):
                            ins = mm(ob[:, HD * (r + 1):HD * (r + 2)], PT3[:, r, kt * P:(kt + 1) * P],
                                     VP[:, r * SEQ + kt * P + gg * HD:r * SEQ + kt * P + gg * HD + HD],
                                     start=kt == 0, stop=kt == w // P - 1)
                    ins.then_inc(pv_done, 1)
                    if v % 8 == 7:
                        pe.wait_ge(o_ready, pair + 1)
                        for n in range(4):
                            ins = tr(PS[:, 4, n * P:(n + 1) * P], OS[:, n * P:(n + 1) * P], IDENT[:, :])
                        ins.then_inc(ot_done, 1)
            CA = CACHE.rearrange("p (k b n c) -> p k b n c", k=2, b=4, n=PAGES)
            for vv in range(4):
                u = 64 + vv
                hb, gg = vv // 2, vv % 2
                rows = slice(64 * gg, 64 * gg + 64)
                pe.wait_ge(cache_landed[hb], 16 * 20)
                pe.wait_ge(p_ready, u - 1)
                if vv == 0:
                    pe.wait_ge(ot_lo, 8)
                    pe.wait_ge(o_ready, 32)
                for bb in range(4):
                    b = 4 * hb + bb
                    out = slice(32 * bb, 32 * bb + 32)
                    qb = QS[rows, 32 * b:32 * b + 32]
                    for r in range(2):
                        mm(PS[out, 2 * (u % 2) + r, :].rearrange("p (n c) -> p n c", n=PAGES), qb,
                           CA[rows, r, bb, :, 0:P], start=True, stop=True)
                    mm(PS[out, 6, 0:32], qb, KC[rows, 32 * b:32 * b + 32], start=True, stop=True)
                    for r in range(2):
                        ins = mm(PS[out, 6, 32 * (r + 1):32 * (r + 1) + 4], qb,
                                 KS[rows, (2 + 2 * r) * 32 + 4 * b:(2 + 2 * r) * 32 + 4 * b + 4], start=True, stop=True)
                ins.then_inc(s_done, 1)
                trans(u, SEQ)
                tr(PS[0:96, 6, 128:256], SC[:, 0:96], IDENT[:, :]).then_inc(pt_done, 1)
                pe.wait_ge(pt_act, u + 1)
                pe.wait_ge(pt_dve, u + 1)
                if vv:
                    pe.wait_ge(o_ready, 32 + vv)
                ptm = OTMP[:, 256:384]
                for bb in range(4):
                    b = 4 * hb + bb
                    out = slice(32 * bb, 32 * bb + 32)
                    cols = slice(b * P + gg * HD, b * P + gg * HD + HD)
                    mm(PS[out, 7, 0:HD], ptm[0:32, out], VM[0:32, cols], start=True, stop=True)
                    for r in range(2):
                        ob = PS[out, 7, HD * (r + 1):HD * (r + 2)]
                        new = slice(32 * (r + 1), 32 * (r + 1) + 4)
                        for n in range(PAGES):
                            mm(ob, PT3[:, r, n * P + 32 * bb:n * P + 32 * bb + 32],
                               CA[:, r, bb, n, P + gg * HD:P + gg * HD + HD], start=n == 0, stop=n == PAGES - 1)
                        ins = mm(PS[out, 2 * (u % 2) + r, 0:HD], ptm[new, out], VM[new, cols], start=True, stop=True)
                ins.then_inc(pv_done, 1)
                if gg == 1:
                    pe.wait_ge(o_ready, 32 + vv + 1)
                    tr(PS[:, 4, 0:P], OS[:, 0:P], IDENT[:, :]).then_inc(ot_done, 1)
                    pe.wait_ge(ot_lo, 8 + hb + 1)
            pe.wait_ge(ot_lo, 10)
            for n in range(8):
                tile(O0["w_out"] + n, C0["w_out"] + n, range(KT), XH3, XL3, 0)

            def stat(bank, src, first, last):
                for h in range(2):
                    ins = mm(PS[:, bank + h, 0:HALF], ONES[:, :], src[:, h * HALF:(h + 1) * HALF], start=first, stop=last)
                return ins

            def ln_sums(idx, last_o, between=None):
                d8 = taken(last_o)[1] - 8
                if idx:
                    pe.wait_ge(n_ready, 8 * idx)
                for k in range(KT):
                    pe.wait_ge(dve_took, d8 + k + 1)
                    ins = stat(4, X3[:, k, :], k == 0, k == KT - 1)
                ins.then_inc(mean_done, 1)
                if between:
                    between()
                for k in range(KT):
                    pe.wait_ge(sq_ready, 8 * idx + k + 1)
                    stat(6, SQ[:, (k % 2) * TOK:(k % 2 + 1) * TOK], k == 0, k == KT - 1).then_inc(var_done, 1)

            def tail(layer):
                ln_sums(2 * layer, O0[f"ffn{layer}"] - 1)
                base, c0 = O0[f"ffn{layer}"], C0[f"ffn{layer}"]
                xl0, gl0 = XL_COUNT[f"ln1_{layer}"], GL_COUNT[f"ffn{layer}"]
                with pe.Fori(0, 3) as t:
                    for n in range(16):
                        tile(base + n, c0 + n, range(KT), XH3, XL3, 0, t=t,
                             each=(lambda k: pe.wait_ge(xl_ready, xl0 + k + 1)) if n == 0 else None)
                    for n in range(8):
                        tile(base + 16 + n, c0 + 16 + n, range(KT), GH3, GL3, 0, t=t,
                             each=(lambda k: pe.wait_ge(gl_ready, 8 * t + (gl0 + k + 1))) if n == 0 else None)
                pc, po = C0[f"proj{layer}"], O0[f"proj{layer}"]
                ph3, pl3 = XH[:, 0:2 * TOK].rearrange("p (k t) -> p k t", k=2), XL[:, 0:2 * TOK].rearrange("p (k t) -> p k t", k=2)

                def proj(lo, hi):
                    pe.wait_ge(pl_ready, layer + 1)
                    for n in range(lo, hi):
                        tile(po + n, pc + n // 4, (2 * (n % 4), 2 * (n % 4) + 1), ph3, pl3, 0)

                ln_sums(2 * layer + 1, po - 1, between=lambda: proj(0, 2))
                proj(2, 8)
                for n in range(8):
                    tile(O0[f"gate{layer}"] + n, C0[f"gate{layer}"] + n, range(KT), GH3, GL3, 0,
                         each=(lambda k: pe.wait_ge(gl_ready, GL_COUNT[f"ln2_{layer}"] + k + 1)) if n == 0 else None)

            tail(0)
            for n in range(8):
                tile(O0["rec"] + n, C0["rec"] + n, range(KT), XH3, XL3, 0,
                     each=(lambda k: pe.wait_ge(xl_ready, XL_COUNT["x1"] + k + 1)) if n == 0 else None)
            for n in range(8):
                pe.wait_ge(gl_ready, GL_COUNT["rec"] + 2 * (n // 2) + 2)
                for gate in range(2):
                    tile(O0["rgate"] + 2 * n + gate, C0["rgate"] + 2 * (n // 4) + gate, (2 * (n % 4), 2 * (n % 4) + 1),
                         GH3, GL3, 2 * (n // 2))
            for n in range(8):
                tile(O0["gbr"] + n, C0["gbr"] + n, range(KT), XH3, XL3, 0)
            for n in range(8):
                tile(O0["rg_out"] + n, C0["rg_out"] + n, range(KT), GH3, GL3, 0,
                     each=(lambda k: pe.wait_ge(gl_ready, GL_COUNT["gated"] + k + 1)) if n == 0 else None)
            tail(1)


def token_columns(prompt, sample):
    c = prompt.shape[1]
    return np.concatenate([prompt.reshape(2, HP, c), sample.reshape(2, 16, c)], axis=1).reshape(TOK, c).T


def channels(x):
    return np.ascontiguousarray(x.reshape(-1, P, x.shape[1]).transpose(1, 0, 2).reshape(P, -1))


def chunks(w):
    return w.reshape(8, P, -1, P).transpose(2, 1, 0, 3).reshape(-1, P, CH)


def pair_chunks(w):
    return w.reshape(-1, 4, 2, P, P).transpose(0, 3, 1, 2, 4).reshape(-1, P, CH)


def lay_out(x):
    z = {k: np.asarray(v) for k, v in x.items()}
    f = np.float32
    heads = [gg * NJ + j for j in range(NJ) for gg in range(2)]
    win = z["nsa_w_in"][0]
    kv0 = D
    q = win[:, :D].reshape(D, 16, HD)[:, heads].reshape(D, D)
    gate = win[:, D + 6 * P:].reshape(D, 2, NJ, 3).transpose(0, 2, 1, 3).reshape(D, 48)
    w_in = np.concatenate([win[:, kv0:kv0 + 6 * P], gate, np.zeros((D, P - 48), f), q], axis=1)
    w1 = z["nsa_cmp_w1"][0].reshape(2, 2, 8, 2, HD, 2, P).transpose(0, 5, 1, 3, 4, 2, 6).reshape(8, P, CH)
    w_out = z["nsa_w_out"][0].reshape(16, HD, D)[heads].reshape(D, D)
    parts = [chunks(w_in), w1, chunks(w_out)]

    def ffn(i):
        up = chunks(z["ffn_w_up"][i])
        out = []
        for t in range(3):
            for p in range(8):
                out += [up[8 * t + p][None], up[24 + 8 * t + p][None]]
            out.append(chunks(z["ffn_w_down"][i][D * t:D * (t + 1)]))
        proj = z["ple_w_proj"][i].reshape(256, 8, P).transpose(1, 0, 2)
        return out + [pair_chunks(proj), chunks(z["ple_w_gate"][i])]

    def block_gate(w):
        return pair_chunks(w.reshape(4, 256, 2, P).transpose(0, 2, 1, 3).reshape(8, 256, P))

    rin = chunks(z["rg_w_in"][0])
    ga, gx = block_gate(z["rg_gate_a_w"][0]), block_gate(z["rg_gate_x_w"][0])
    parts += ffn(0) + [rin[8:], ga[:1], gx[:1], ga[1:], gx[1:], rin[:8], chunks(z["rg_w_out"][0])] + ffn(1)
    stream = np.concatenate(parts, axis=0)
    assert stream.shape == (N_CHUNKS, P, CH), (stream.shape, N_CHUNKS)

    col = lambda v: v.reshape(-1, P).T
    cols = []
    for i in (0, 1):
        taps = np.concatenate([z["ffn_conv_w"][i], z["ffn_conv_b"][i][None]], axis=0)
        cols += [channels(taps.T), col(z["ln_mix_g"][i]), col(z["ln_mix_b"][i]),
                 col(z["ln_ffn_g"][i]), col(z["ln_ffn_b"][i])]
    pe = z["nsa_cmp_pe"][0].reshape(2, 2, 8, 2, HD).transpose(3, 4, 0, 2, 1).reshape(P, 32)
    cols += [col(z["rg_conv_w"][0].reshape(-1)), col(z["rg_conv_b"][0]), col(z["rg_gate_a_b"][0]), col(z["rg_gate_x_b"][0]),
             col(z["rg_lambda"][0]), col(z["nsa_cmp_b1"][0].reshape(-1)), pe,
             channels(z["state_rglru_h"][0].T), channels(z["state_rglru_conv"][0].transpose(2, 0, 1).reshape(D, 24))]
    params = np.ascontiguousarray(np.concatenate(cols, axis=1))
    assert params.shape == (P, NPAR)

    kv = z["cache_nsa_kv"][0]
    n_pool = kv.shape[0]
    cmp_rows = kv[:, :, 0:2].reshape(n_pool, 8, 8, 2, 2, 2, HD).transpose(0, 3, 6, 4, 5, 2, 1).reshape(n_pool * P, 256)
    sel_k = kv[:, :, 2].reshape(n_pool, P, P).transpose(0, 2, 1)
    sel = np.concatenate([sel_k, kv[:, :, 3].reshape(n_pool, P, P)], axis=2).reshape(n_pool * P, 256)
    wn = z["cache_nsa_win"][0].reshape(NB, 4, P, 2, P)
    wk, wv = wn[:, :, :, 0].transpose(0, 3, 1, 2), wn[:, :, :, 1].transpose(0, 2, 1, 3)
    cache_win = np.concatenate([wk, wv], axis=3).reshape(NB, P, 1024)
    s_of = np.arange(P) % NS
    k4 = np.arange(4)
    smask = np.concatenate([np.where(k4[None] <= s_of[:, None], 0, NEG), np.where(k4[None] >= s_of[:, None], 0, NEG)], axis=1)
    return {
        "w_stream": stream.reshape(N_CHUNKS * P, CH),
        "x": channels(token_columns(z["x_prompt"][0], z["x_sample"].reshape(32, D))),
        "p": np.stack([channels(token_columns(z["p_prompt"][i][0], z["p_sample"][i].reshape(32, 256))) for i in (0, 1)]),
        "params": params,
        "pages": z["page_table"].reshape(1, -1).astype(np.int32),
        "cache_cmp": np.ascontiguousarray(cmp_rows),
        "cache_sel": np.ascontiguousarray(sel),
        "cache_win": np.ascontiguousarray(cache_win),
        "win_copy": np.ascontiguousarray(z["cache_nsa_win"][0][:, NS:].reshape(NB * 127, 1024)),
        "cmp_w2": np.ascontiguousarray(z["nsa_cmp_w2"][0].reshape(2, 2, P, HD).transpose(2, 0, 1, 3).reshape(P, 256)),
        "smask": smask.astype(f),
        "ffn_state": np.stack([channels(z["state_ffn_conv"][i].transpose(2, 0, 1).reshape(6 * D, 16)) for i in (0, 1)]),
    }


OUTPUTS = {"y": (P, KT * TOK), "kcmp": (P, 1024), "kt4": (P, 4 * SEQ), "ks": (P, 192), "win_old": (NB * 127, 1024),
           "rg": (P, 8 * 36), "ffn_conv": (2, P, 48 * 18)}


def kernel(**inputs):
    import concourse.bacc as bacc
    from concourse.bass_utils import run_bass_kernel_spmd

    nc = bacc.Bacc("TRN2", target_bir_lowering=False, num_devices=1)
    arrays = {f"in_{k}": np.ascontiguousarray(v) for k, v in lay_out(inputs).items()}
    a = {k[3:]: nc.dram_tensor(k, v.shape, mybir.dt.from_np(v.dtype), kind="ExternalInput").ap()
         for k, v in arrays.items()}
    a["gate_scratch"] = nc.dram_tensor("gate_scratch", (2, P, 6), F32, kind="Internal").ap()
    outs = {k: nc.dram_tensor(f"out_{k}", s, F32, kind="ExternalOutput").ap() for k, s in OUTPUTS.items()}
    build(nc, a, outs)
    r = run_bass_kernel_spmd(nc, [arrays], core_ids=[0]).results[0]
    o = {k: np.asarray(r[f"out_{k}"]) for k in OUTPUTS}

    y = o["y"].reshape(P, KT, 2, HALF).transpose(2, 3, 1, 0).reshape(2, HALF, D)
    y_prompt = y[:, :HP].reshape(1, SEQ, D)
    y_sample = y[:, HP:].reshape(NB, NS, D)
    kc = o["kcmp"].reshape(2, HD, 2, 2, 8, 32).transpose(5, 4, 3, 2, 0, 1).reshape(SEQ, 2, 2, HD)
    k4 = o["kt4"].reshape(2, HD, 4, SEQ).transpose(3, 2, 0, 1)
    ks = o["ks"].reshape(2, HD, 6, 32).transpose(3, 2, 0, 1)
    kv_prompt = np.concatenate([kc, k4[:, 0:2]], axis=1)[None, None]
    win_prompt = np.ascontiguousarray(k4[:, 2:4])[None, None]
    kv_sample = np.ascontiguousarray(ks[:, 0:4]).reshape(1, NB, NS, 4, 2, HD)
    win_new = ks[:, 4:6].reshape(NB, NS, 2, 2, HD)
    win_sample = np.concatenate([o["win_old"].reshape(NB, SEQ - NS, 2, 2, HD), win_new], axis=1)[None]
    rg = o["rg"].reshape(P, 8, 36).transpose(2, 1, 0).reshape(36, D)
    fc = o["ffn_conv"].reshape(2, P, 48, 18).transpose(0, 3, 2, 1).reshape(2, 18, 6 * D)
    c = np.ascontiguousarray
    return (c(y_prompt), c(y_sample), c(kv_prompt), kv_sample, win_prompt, win_sample,
            c(rg[27:28])[None], c(rg[28:36])[None], c(rg[0:3])[None, None], c(rg[3:27]).reshape(1, NB, 3, D),
            c(fc[:, 0:2])[:, None], c(fc[:, 2:18]).reshape(2, NB, 2, 6 * D))
```

```python
from contextlib import ExitStack

import numpy as np
import concourse.bass as bass
from concourse import mybir

F32 = mybir.dt.float32
F32R = mybir.dt.float32r
BF16 = mybir.dt.bfloat16
I32 = mybir.dt.int32
ALU = mybir.AluOpType
ACT = mybir.ActivationFunctionType
AX_X = mybir.AxisListType.X

P = 128
D = 1024
KT = D // P
SEQ = 512
NB, NS = 8, 4
HALF = 272
HP = 256
TOK = 2 * HALF
HD = 64
NJ = 8
PAGES = 4
NC = 31
SCALE = HD ** -0.5
NEG = -1e30
ALPHA = 4 ** 0.25
EPS = 1e-5
FT = 24
THIRD = 8
CH = KT * P
OPW = 4624

IN_TILES = ["kcmp", "vcmp", "ksel", "vsel", "kwin", "vwin", "gate"] + ["q"] * 8


def plan():
    first_chunk, first_tile = {}, {}
    taker, last_user, used_up = [], [], []

    def section(name, tiles, takers, chunks_of):
        first_chunk[name], first_tile[name] = len(last_user), len(taker)
        n_chunks = 1 + max(max(chunks_of(n)) for n in range(tiles))
        base_t, base_c = len(taker), len(last_user)
        last = [0] * n_chunks
        for n in range(tiles):
            taker.append(takers(n))
            for c in chunks_of(n):
                last[c] = base_t + n
        last_user.extend(last)
        for n in range(tiles):
            used_up.append(base_c + sum(1 for u in last if u <= base_t + n))

    one = lambda n: [n]
    section("w_in", 15, lambda n: "act", one)
    section("cmp", 8, lambda n: "dve" if n % 2 else "act", one)
    section("w_out", 8, lambda n: "dve", one)
    for layer in (0, 1):
        if layer == 1:
            section("rec", 8, lambda n: "act", one)
            section("rgate", 16, lambda n: "act", lambda n: [2 * (n // 8) + n % 2])
            section("gbr", 8, lambda n: "act", one)
            section("rg_out", 8, lambda n: "dve", one)
        section(f"ffn{layer}", 72, lambda n: "act" if n % 24 < 16 else "dve", one)
        section(f"proj{layer}", 8, lambda n: "act", lambda n: [n // 4])
        section(f"gate{layer}", 8, lambda n: "act", one)
    return first_chunk, first_tile, taker, last_user, used_up


C0, O0, TAKER, LAST_USER, USED_UP = plan()
N_CHUNKS = len(LAST_USER)
RAWS, SLOTS, AHEAD = 2, 4, 3


def taken(o):
    return TAKER[o], sum(1 for t in TAKER[:o + 1] if t == TAKER[o])


PCOL = {}
_n = 0
for _name, _w in ([(f"{k}{i}", w) for i in (0, 1) for k, w in
                   (("conv", 192), ("ln_mg", 8), ("ln_mb", 8), ("ln_fg", 8), ("ln_fb", 8))]
                  + [("rconv_w", 32), ("rconv_b", 8), ("ga_b", 8), ("gx_b", 8), ("lam", 8), ("cmp_b1", 4),
                     ("pe", 32), ("h0", 64), ("rstate", 192)]):
    PCOL[_name] = _n
    _n += _w
NPAR = _n

U = 2 + SEQ + NB * 6
UO = U - 2
UR = 3 + SEQ + NB * 7
URO = UR - 3


def build(nc, a, outs):
    ctx = ExitStack()
    with ctx:
        def sb(name, cols, dt=F32, parts=P):
            return ctx.enter_context(nc.sbuf_tensor(name, [parts, cols], dt))

        def sem(name):
            return ctx.enter_context(nc.semaphore(name))

        RAW = sb("RAW", RAWS * CH)
        HI, LO = sb("HI", SLOTS * CH, F32R), sb("LO", SLOTS * CH, F32R)
        XH, XL = sb("XH", OPW, F32R), sb("XL", OPW, F32R)
        GH, GL = sb("GH", OPW, F32R), sb("GL", OPW, F32R)
        X_AT = nc.sbuf_base
        X = sb("X", KT * TOK)
        PAR = sb("PAR", NPAR)
        IDENT, IDENTB, ONES = sb("IDENT", P), sb("IDENTB", P, BF16), sb("ONES", P)
        DMASK = sb("DMASK", P, BF16)
        CMASK = sb("CMASK", 4 * 32)
        SMASK = sb("SMASK", 8)
        SMALL = sb("SMALL", 512)
        CWS = sb("CWS", 16)
        PAGE = sb("PAGE", NB * PAGES, I32, parts=1)
        NA = (nc.sbuf_bytes_remaining if not callable(nc.sbuf_bytes_remaining) else nc.sbuf_bytes_remaining()) // 4 - 8
        ARENA_AT = nc.sbuf_base
        ARENA = sb("ARENA", NA)

        def over(name, base, col, cols):
            return nc.alloc_sbuf_tensor_at(name, [P, cols], F32R, offset=base + 4 * col)[:, :]
        PS = ctx.enter_context(nc.psum_tensor("PS", [P, 8, 512], F32))

        def carve(at, sizes):
            views = []
            for n in sizes:
                views.append(ARENA[:, at:at + n])
                at += n
            assert at <= NA, (at, NA)
            return views, at

        sizes = [8192, 1024, 192, 256, 256, 192, 16, 128, 2048, 1024, 1024, 1024]
        (CACHE, VM, KS, QS, KC, GT, GS, _, KT4, KR, XPR, VH_), at = carve(0, sizes)
        (W2, AT, HS, HPR, GTC), _ = carve(at, [256, 578, 1024, 128, TOK])
        at_kcz, at_kt4 = sum(sizes[:7]), sum(sizes[:8])
        KH, KL = over("KH", ARENA_AT, at_kt4 + 2048, 1024), over("KL", ARENA_AT, at_kt4 + 3072, 1024)
        VH, VL = over("VH", ARENA_AT, at_kt4 + 4096, 1024), over("VL", ARENA_AT, at_kt4 + 1024, 1024)
        SC, ZERO = KT4[:, 0:512], SMALL[:, 499:500]
        VCZ = over("VCZ", ARENA_AT, at_kt4 + 512, 512)
        KCZ = over("KCZ", ARENA_AT, at_kcz, 128)
        (PB,), _ = carve(at, [2048])
        QF = X[:, 0:NJ * SEQ].rearrange("p (j t) -> p j t", j=NJ)
        QH = GH[:, 0:NJ * SEQ].rearrange("p (j t) -> p j t", j=NJ)
        QL = GL[:, 0:NJ * SEQ].rearrange("p (j t) -> p j t", j=NJ)
        PCH, PCL = GH[:, 4096:4608], GL[:, 4096:4608]
        PTS = over("PTS", X_AT, 0, 4096).rearrange("p (u s r k) -> p u s r k", u=2, s=2, r=2)
        PT, OS, OTMP = XPR, VH_[:, 0:512], VH_[:, 512:896]
        (PP, SQ, RS, LT, PRAW), at_ln = carve(0, [KT * TOK, 2 * TOK, TOK, 2 * TOK, 2 * TOK])
        (EXT, CV, G1, PR, ST, CS), _ = carve(at_ln, [4 * U, 4 * U, U, TOK, 48 * 16, 48 * 18])
        SQ4 = (SQ[:, 0:TOK], SQ[:, TOK:2 * TOK], G1[:, 0:TOK], PR)
        XSUM_ = LT[:, TOK:2 * TOK]
        RES = SMALL[:, 500:501]
        (REC, RR, VV, REXT, RCV, RTM, LAST), _ = carve(0, [KT * TOK, KT * TOK, KT * TOK, 2 * UR, UR, 2 * TOK, 8 * 36])

        def t3(ap, n=KT):
            return ap.rearrange("p (k t) -> p k t", k=n)

        X3, PP3, REC3, RR3, VV3 = t3(X[:, :]), t3(PP), t3(REC), t3(RR), t3(VV)
        XH3, XL3 = t3(XH[:, 0:KT * TOK]), t3(XL[:, 0:KT * TOK])
        GH3, GL3 = t3(GH[:, 0:KT * TOK]), t3(GL[:, 0:KT * TOK])

        def par(name, k=0, n=1):
            return PAR[:, PCOL[name] + k:PCOL[name] + k + n]

        def half(ap, h):
            return ap[:, h * HALF:(h + 1) * HALF]

        def halves(ap):
            return ap.rearrange("p (h t) -> p h t", h=2)

        def banks(o):
            b = 2 * (o % 2)
            return PS[:, b:b + 2, 0:HALF]

        raw_landed = [sem(f"raw_landed{i}") for i in range(RAWS)]
        hi_ready, lo_ready = sem("hi_ready"), sem("lo_ready")
        tile_done = sem("tile_done")
        act_took, dve_took = sem("act_took"), sem("dve_took")
        act_chain, dve_chain, pool_chain = sem("act_chain"), sem("dve_chain"), sem("pool_chain")
        phase_end = sem("phase_end")
        x_back = sem("x_back")
        x_landed, par_landed, page_landed = sem("x_landed"), sem("par_landed"), sem("page_landed")
        cmp_landed, cache_landed = sem("cmp_landed"), [sem("cache_landed0"), sem("cache_landed1")]
        w2_landed, st_landed, p_landed = sem("w2_landed"), sem("st_landed"), sem("p_landed")
        consts_ready = sem("consts_ready")
        xh_ready, xl_ready = sem("xh_ready"), sem("xl_ready")
        gh_ready, gl_ready = sem("gh_ready"), sem("gl_ready")
        shift_landed = sem("shift_landed")
        cs_hi, cs_lo = sem("cs_hi"), sem("cs_lo")
        kv_out, qk_hi, qk_lo, vcz_clear = sem("kv_out"), sem("qk_hi"), sem("qk_lo"), sem("vcz_clear")
        pc_scaled, pc_hi, pc_lo = sem("pc_scaled"), sem("pc_hi"), sem("pc_lo")
        ps_ready = sem("ps_ready")
        win_landed = sem("win_landed")
        hid_sum, hid_ready, w2_done, w2_took = sem("hid_sum"), sem("hid_ready"), sem("w2_done"), sem("w2_took")
        tr_done, tr_took = sem("tr_done"), sem("tr_took")
        out_dma, gate_dma = sem("out_dma"), sem("gate_dma")
        sc_done, sc_masked, pc_ready, pct_done = sem("sc_done"), sem("sc_masked"), sem("pc_ready"), sem("pct_done")
        s_done, negmax_ready, p_ready = sem("s_done"), sem("negmax_ready"), sem("p_ready")
        pt_done, pt_act, pt_dve, pv_done = sem("pt_done"), sem("pt_act"), sem("pt_dve"), sem("pv_done")
        o_ready, ot_done, ot_hi, ot_lo = sem("o_ready"), sem("ot_done"), sem("ot_hi"), sem("ot_lo")
        mean_done, d_ready, sq_ready, var_done = sem("mean_done"), sem("d_ready"), sem("sq_ready"), sem("var_done")
        r0_ready, n_ready, ln_out, scale_set = sem("r0_ready"), sem("n_ready"), sem("ln_out"), sem("scale_set")
        v_ready, xsum_ready, pair_ready = sem("v_ready"), sem("xsum_ready"), sem("pair_ready")
        ext_free, old_in, tap0_done, gelu_done = (sem("ext_free"), sem("old_in"),
                                                                      sem("tap0_done"), sem("gelu_done"))
        prod_done = sem("prod_done")
        ph_ready, pl_ready = sem("ph_ready"), sem("pl_ready")
        y_ready = sem("y_ready")
        rec_ready, m_ready, lam_ready, sp_ready = sem("rec_ready"), sem("m_ready"), sem("lam_ready"), sem("sp_ready")
        sig_ready, a_ready, sqrt_ready, h_ready = (sem("sig_ready"), sem("a_ready"), sem("sqrt_ready"),
                                                          sem("h_ready"))

        XL_COUNT = {name: 8 * n for n, name in enumerate(("x", "ln1_0", "x1", "ln1_1"))}
        GL_COUNT = {"ffn0": 1, "ln2_0": 25, "rec": 33, "gated": 41, "ffn1": 49, "ln2_1": 73}
        XSUM = (1, 4, 5, 8)
        PROD0 = (2, 2 + 24 + 8 + 2)
        GATED0 = 26
        EXT0 = (4, 4 + 48 + 4)

        def sums_of(n, gg):
            rows = PS[64 * gg:64 * gg + 64, 6 + n % 2, :]
            return rows.rearrange("p (j g t) -> p j g t", j=2, g=2)[:, :, gg, :]

        def heads_of(x, n, gg):
            j, i = 2 * (n % 4), n // 4
            c0 = (i // 2) * HALF + P * (i % 2)
            return x[64 * gg:64 * gg + 64, j:j + 2, c0:c0 + P]

        class Chain:

            def __init__(self, eng, s):
                self.eng, self.s, self.n = eng, s, 0

            def did(self, ins):
                self.n += 1
                ins.then_inc(self.s, 1)

            def sync(self):
                self.eng.wait_ge(self.s, self.n)

        def wait_taken(eng, o, t=None):
            who, n = taken(o)
            if t is None:
                eng.wait_ge(act_took if who == "act" else dve_took, n)
            elif who == "act":
                eng.wait_ge(act_took, 16 * t + n)
            else:
                eng.wait_ge(dve_took, 8 * t + n)

        def transposed(n):
            return 2 * n if n <= 64 else 64 + n

        def dyn(n, t, k):
            return n if t is None else k * t + n

        def at_phase(eng, n):
            eng.wait_ge(phase_end, 3 * n)
            if n == 1:
                eng.wait_ge(tr_done, 2)
            elif n == 2:
                eng.wait_ge(ot_done, 2)
            else:
                eng.wait_ge(tile_done, O0["rec"] if n == 3 else O0["ffn1"])

        def split_hi(act, c, t=None):
            s = c % SLOTS
            act.wait_ge(raw_landed[c % RAWS], dyn(16 * (c // RAWS + 1), t, 16 * 24 // RAWS))
            if c >= SLOTS:
                act.wait_ge(tile_done, dyn(LAST_USER[c - SLOTS] + 1, t, 24))
            nc.scalar.activation(HI[:, s * CH:(s + 1) * CH], RAW[:, (c % RAWS) * CH:(c % RAWS + 1) * CH],
                                 ACT.Copy).then_inc(hi_ready, 1)

        def split_lo(dve, c, t=None):
            s = c % SLOTS
            dve.wait_ge(hi_ready, dyn(c + 1, t, 24))
            nc.vector.tensor_tensor(LO[:, s * CH:(s + 1) * CH], RAW[:, (c % RAWS) * CH:(c % RAWS + 1) * CH],
                                    HI[:, s * CH:(s + 1) * CH].bitcast(F32), ALU.subtract).then_inc(lo_ready, 1)

        class Splits:

            def __init__(self, eng, fn):
                self.eng, self.fn, self.c = eng, fn, 0

            def after(self, o, t=None):
                upto = (USED_UP[o] if o >= 0 else 0) + AHEAD
                while self.c < upto:
                    if self.c < N_CHUNKS:
                        self.fn(self.eng, self.c, t)
                    self.c += 1

        block = ctx.enter_context(nc.Block())

        @block.sync
        def _(sp):
            W = a["w_stream"]

            def load(c, slot):
                sp.dma_start(RAW[:, slot * CH:(slot + 1) * CH], W[c * P:(c + 1) * P, :]).then_inc(raw_landed[slot], 16)

            sp.dma_start(X[:, :], a["x"]).then_inc(x_landed, 16)
            load(0, 0)
            load(1, 1)
            with sp.Fori(1, N_CHUNKS // RAWS) as r:
                for k in range(RAWS):
                    sp.wait_ge(lo_ready, RAWS * r + (k + 1 - RAWS))
                    sp.dma_start(RAW[:, k * CH:(k + 1) * CH],
                                 W[bass.ds((RAWS * r + k) * P, P), :]).then_inc(raw_landed[k], 16)
            for c in range(N_CHUNKS // RAWS * RAWS, N_CHUNKS):
                sp.wait_ge(lo_ready, c + 1 - RAWS)
                load(c, c % RAWS)

        @block.gpsimd
        def _(pool):
            g = nc.gpsimd
            chain = Chain(pool, pool_chain)
            pool.dma_start(PAGE[:, :], a["pages"]).then_inc(page_landed, 16)
            pool.dma_start(PAR[:, :], a["params"]).then_inc(par_landed, 16)
            pool.wait_ge(page_landed, 16)
            CR = CACHE.rearrange("p (n c) -> p n c", n=NB * PAGES)
            for n in range(NB * PAGES):
                pg = pool.value_load(PAGE[0:1, n:n + 1], min_val=0, max_val=a["cache_cmp"].shape[0] // P - 1)
                pool.dma_start(CR[:, n, :], a["cache_cmp"][bass.ds(pg * P, P), :]).then_inc(cmp_landed, 16)
            chain.did(g.memset(IDENT[:, :], 0.0))
            chain.did(g.memset(ONES[:, :], 1.0 / D))
            chain.did(g.memset(DMASK[:, :], 0.0))
            chain.did(g.memset(CMASK[:, :], 0.0))
            chain.did(g.memset(SMALL[:, 0:1], 1.0))
            chain.did(g.memset(SMALL[:, 1:512], 0.0))
            chain.sync()
            chain.did(g.affine_select(out=IDENT[:, :], in_=IDENT[:, :], compare_op=ALU.not_equal, fill=1.0, base=0,
                                      pattern=[[-1, P]], channel_multiplier=1))
            chain.did(g.affine_select(out=DMASK[:, :], in_=DMASK[:, :], compare_op=ALU.is_ge, fill=NEG, base=0,
                                      pattern=[[-1, P]], channel_multiplier=1))
            cm = CMASK[:, :].rearrange("p (i c) -> p i c", i=4)
            chain.did(g.affine_select(out=cm, in_=cm, compare_op=ALU.is_ge, fill=NEG, base=-31,
                                      pattern=[[P, 4], [-16, 32]], channel_multiplier=1))
            chain.did(g.affine_select(out=SMALL[:, 0:1], in_=SMALL[:, 0:1], compare_op=ALU.is_ge, fill=0.0, base=-31,
                                      pattern=[[0, 1]], channel_multiplier=1))
            chain.sync()
            chain.did(g.tensor_copy(IDENTB[:, :], IDENT[:, :]))
            chain.did(g.memset(cm[:, :, NC:NC + 1], NEG))
            chain.sync()
            pool.dma_start(SMASK[:, :], a["smask"]).then_inc(par_landed, 16)
            pool.dma_start(W2, a["cmp_w2"]).then_inc(w2_landed, 16)
            g.memset(SMALL[:, 1:2], EPS).then_inc(consts_ready, 1)

            for kv in range(2):
                pool.wait_ge(act_took, kv + 1)
                for gg in range(2):
                    for pr in range(2):
                        src = KR[gg * 64:gg * 64 + 64, kv * 512 + pr * 256:kv * 512 + pr * 256 + 256]
                        dst = XPR[pr * 64:pr * 64 + 64, kv * 512 + gg * 256:kv * 512 + gg * 256 + 256]
                        pool.dma_start(dst, src).then_inc(shift_landed, 16)
            pool.wait_ge(act_took, 6)
            pool.dma_start(outs["kcmp"], KR).then_inc(kv_out, 16)
            pool.dma_start(outs["kt4"], KT4).then_inc(kv_out, 16)
            pool.dma_start(outs["ks"], KS).then_inc(out_dma, 16)
            pool.wait_ge(act_took, 7)
            gsc = a["gate_scratch"]
            with nc.allow_non_contiguous_dma(reason="48 gates per sampled token, 4 bytes each"):
                for h in range(2):
                    for bs in range(4 * NS):
                        rows = gsc[h].rearrange("(b j s) r -> b s j r", b=4, j=NJ)[bs // NS, bs % NS]
                        pool.dma_start(rows, GTC[0:48, h * HALF + HP + bs:h * HALF + HP + bs + 1]).then_inc(gate_dma, 16)
            pool.wait_ge(gate_dma, 16 * 32)
            for h in range(2):
                pool.dma_start(GS[:, h * 6:h * 6 + 6], gsc[h]).then_inc(gate_dma, 16)
            CA = CACHE.rearrange("p (k b n c) -> p k b n c", k=2, b=4, n=PAGES)

            def load_cache(hb):
                for bb in range(4):
                    b = 4 * hb + bb
                    for n in range(PAGES):
                        pg = pool.value_load(PAGE[0:1, b * PAGES + n:b * PAGES + n + 1], min_val=0,
                                             max_val=a["cache_sel"].shape[0] // P - 1)
                        pool.dma_start(CA[:, 0, bb, n, :], a["cache_sel"][bass.ds(pg * P, P), :])\
                            .then_inc(cache_landed[hb], 16)
                    if hb == 0:
                        pool.dma_start(CACHE[:, 4096 + bb * 1024:4096 + (bb + 1) * 1024], a["cache_win"][b])\
                            .then_inc(cache_landed[hb], 16)

            pool.wait_ge(cs_lo, 4)
            load_cache(0)
            pool.wait_ge(kv_out, 32)
            g.memset(SMALL[:, 501:502], 0.0).then_inc(phase_end, 1)
            pool.dma_start(outs["win_old"], a["win_copy"]).then_inc(out_dma, 16)
            pool.wait_ge(pv_done, 64)
            pool.dma_start(X[:, :], a["x"]).then_inc(x_back, 16)
            pool.wait_ge(pv_done, 66)
            load_cache(1)
            g.memset(SMALL[:, 502:503], 0.0).then_inc(phase_end, 1)

            def tail(layer, ph):
                base_a = taken(O0[f"ffn{layer}"])[1] - 1
                at_phase(pool, ph)
                pool.dma_start(ST[:, :], a["ffn_state"][layer]).then_inc(st_landed, 16)
                pool.dma_start(PRAW[:, :], a["p"][layer]).then_inc(p_landed, 16)
                ln(2 * layer, "ln_mg", "ln_mb", layer)
                pool.wait_ge(st_landed, 16 * (layer + 1))
                nb = 48 * layer
                with pool.Fori(0, 3) as t:
                    for n in range(16):
                        f = (n // 2) if n % 2 == 0 else 24 + n // 2
                        e = EXT[:, (n % 4) * U:(n % 4 + 1) * U]
                        es = e[:, 2 + SEQ:U].rearrange("p (b c) -> p b c", b=NB)
                        cv = CV[:, (n % 4) * U:(n % 4) * U + UO]
                        pool.wait_ge(ext_free, 16 * t + (nb + 4 * layer + n + 1))
                        g.tensor_copy(CWS[:, 4 * (n % 4):4 * (n % 4) + 4],
                                      PAR[:, bass.ds(32 * t + (PCOL[f"conv{layer}"] + 4 * f), 4)]).then_inc(pool_chain, 1)
                        g.tensor_copy(es[:, :, 0:2], ST[:, bass.ds(128 * t + 16 * f, 16)]
                                      .rearrange("p (b c) -> p b c", b=NB)).then_inc(old_in, 1)
                        pool.wait_ge(act_took, 16 * t + (base_a + n + 1))
                        pool.wait_ge(old_in, 16 * t + (nb + n + 1))
                        pool.wait_ge(prod_done, 8 * t + (PROD0[layer] + n // 2 - 1))
                        g.tensor_copy(CS[:, bass.ds(144 * t + 18 * f, 2)], e[:, SEQ:SEQ + 2]).then_inc(pool_chain, 1)
                        g.tensor_copy(CS[:, bass.ds(144 * t + (18 * f + 2), 16)].rearrange("p (b c) -> p b c", b=NB),
                                      es[:, :, 4:6]).then_inc(pool_chain, 1)
                        g.tensor_scalar(cv, e[:, 0:UO], CWS[:, 4 * (n % 4):4 * (n % 4) + 1],
                                        CWS[:, 4 * (n % 4) + 3:4 * (n % 4) + 4], ALU.mult, ALU.add)\
                            .then_inc(tap0_done, 1)
                chain.n += 3 * 48
                chain.sync()
                pool.dma_start(outs["ffn_conv"][layer], CS[:, :]).then_inc(out_dma, 16)
                ln(2 * layer + 1, "ln_fg", "ln_fb", layer)

            def ln(idx, gn, bn, layer):
                for k in range(KT):
                    pool.wait_ge(n_ready, 8 * idx + k + 1)
                    g.tensor_scalar(X3[:, k, :], X3[:, k, :], par(f"{gn}{layer}", k), par(f"{bn}{layer}", k),
                                    ALU.mult, ALU.add).then_inc(ln_out, 1)

            pool.wait_ge(par_landed, 32)
            tail(0, 2)
            pool.wait_ge(out_dma, 48)
            g.memset(SMALL[:, 503:504], 0.0).then_inc(phase_end, 1)
            at_phase(pool, 3)
            pool.wait_ge(h_ready, 9)
            pool.dma_start(outs["rg"], LAST[:, :]).then_inc(out_dma, 16)
            pool.wait_ge(out_dma, 64)
            g.memset(SMALL[:, 504:505], 0.0).then_inc(phase_end, 1)
            tail(1, 4)
            pool.wait_ge(y_ready, 16)
            pool.dma_start(outs["y"], X[:, :]).then_inc(out_dma, 16)
            pool.wait_ge(out_dma, 96)

        @block.scalar
        def _(act):
            s = nc.scalar
            chain = Chain(act, act_chain)
            splits = Splits(act, split_hi)
            act.wait_ge(x_landed, 16)
            for k in range(KT):
                s.activation(XH3[:, k, :], X3[:, k, :], ACT.Copy).then_inc(xh_ready, 1)
                if k in (0, 1, 2):
                    splits.c = k
                    split_hi(act, k)
            splits.c = 3
            CR = CACHE.rearrange("p (n v m c) -> p n v m c", n=NB * PAGES, v=2, m=16)

            def cmp_hi(kv, dst):
                out = dst[:, 0:4096].rearrange("p (m b n c) -> p b n m c", m=16, b=NB, n=PAGES)
                for b in range(NB):
                    ins = s.activation(out[:, b], CR[:, b * PAGES:(b + 1) * PAGES, kv], ACT.Copy)
                    if b < NB - 1:
                        chain.did(ins)
                ins.then_inc(cs_hi, 1)

            def cmp_hi_prompt(kv, dst):
                out = dst[:, 4096:OPW].rearrange("p (m c) -> p m c", m=8)
                for gg in range(2):
                    chain.did(s.activation(out[:, :, gg * 32:gg * 32 + 32],
                                           XPR[:, kv * 512 + gg * 256:kv * 512 + gg * 256 + 256]
                                           .rearrange("p (m c) -> p m c", m=8), ACT.Copy))
                s.activation(out[:, :, 64:66], par("pe", kv * 16, 16).rearrange("p (m c) -> p m c", m=8),
                             ACT.Copy).then_inc(cs_hi, 1)

            for n in range(15):
                act.wait_ge(tile_done, n + 1)
                o = banks(n)
                if n < 2:
                    for h in range(2):
                        dst = KR[:, n * 512:(n + 1) * 512].rearrange("p (r m h c) -> p h c m r", r=2, m=8, h=2)
                        chain.did(s.activation(dst[:, h], o[:, h, 0:HP].rearrange("p (c m r) -> p c m r", m=8, r=2),
                                               ACT.Copy))
                elif n < 6:
                    at = {2: 0, 3: 2, 4: 1, 5: 3}[n] * SEQ
                    chain.did(s.activation(KT4[:, at:at + SEQ].rearrange("p (h t) -> p h t", h=2),
                                           o[:, :, 0:HP], ACT.Copy))
                elif n == 6:
                    s.activation(halves(GTC[0:48, :]), o[0:48, :, :], ACT.Sigmoid).then_inc(act_took, 1)
                else:
                    j = n - 7
                    if j == 0:
                        act.wait_ge(xl_ready, 8)
                    chain.did(s.activation(QF[:, j, :].rearrange("p (h t) -> p h t", h=2), o[:, :, 0:HP], ACT.Copy,
                                           scale=SCALE))
                    qs = QS.rearrange("p (h b j s) -> p h b j s", h=2, b=4, j=NJ)
                    s.activation(qs[:, :, :, j, :], o[:, :, HP:HALF].rearrange("p h (b s) -> p h b s", b=4),
                                 ACT.Copy, scale=SCALE).then_inc(act_took, 1)
                if n < 6:
                    s.activation(KS[:, n * 32:(n + 1) * 32].rearrange("p (h t) -> p h t", h=2), o[:, :, HP:HALF],
                                 ACT.Copy).then_inc(act_took, 1)
                splits.after(n)
                if n == 3:
                    act.wait_ge(cmp_landed, 16 * NB * PAGES)
                    cmp_hi(0, GH)
            act.wait_ge(shift_landed, 128)
            act.wait_ge(par_landed, 32)
            cmp_hi_prompt(0, GH)
            cmp_hi(1, XH)
            cmp_hi_prompt(1, XH)
            for n in range(8):
                kv, hh = n // 4, (n // 2) % 2
                o = O0["cmp"] + n
                b = 2 * (o % 2)
                if n % 2 == 0:
                    act.wait_ge(tile_done, o + 1)
                    if n:
                        act.wait_ge(hid_sum, n // 2)
                    chain.did(s.activation(AT[:, 0:512], PS[:, b, :], ACT.Copy))
                    s.activation(AT[:, 512:578], PS[:, b + 1, 0:66], ACT.Copy).then_inc(act_took, 1)
                else:
                    act.wait_ge(hid_sum, n // 2 + 1)
                    bt = SMALL[:, 8 + n // 2:9 + n // 2]
                    hs = HS[:, hh * 512:(hh + 1) * 512].rearrange("p (r c) -> p r c", c=32)[:, :, 0:NC]
                    hp = HPR[:, hh * 64:(hh + 1) * 64].rearrange("p (r c) -> p r c", c=32)[:, :, 0:NC]
                    chain.did(s.activation(hs, hs, ACT.Gelu_apprx_tanh, bias=bt))
                    s.activation(hp, hp, ACT.Gelu_apprx_tanh, bias=bt).then_inc(hid_ready, 1)
                splits.after(o)
                if n == 3:
                    act.wait_ge(tr_done, 1)
                    act.wait_ge(vcz_clear, 1)
                    chain.did(s.activation(KC, PS[:, 4, 0:256], ACT.Copy))
                    chain.did(s.activation(KCZ[0:64, 0:32], PS[0:64, 5, 0:32], ACT.Copy))
                    chain.did(s.activation(KCZ[64:128, 32:64], PS[64:128, 5, 0:32], ACT.Copy))
                    s.activation(GT, PS[:, 5, 64:256], ACT.Copy).then_inc(w2_took, 1)
                    s.activation(VH.rearrange("p (h c) -> p h c", h=2), PS[:, 6:8, :], ACT.Copy).then_inc(tr_took, 1)
                if n == 4:
                    act.wait_ge(kv_out, 32)
                    act.wait_ge(cs_lo, 4)
                    s.activation(KH, KT4[:, 0:1024], ACT.Copy).then_inc(qk_hi, 1)
                if n in (4, 6):
                    for j in range(2 * n - 8, 2 * n - 4):
                        s.activation(QH[:, j, :], QF[:, j, :], ACT.Copy).then_inc(qk_hi, 1)
                if n == 7:
                    act.wait_ge(w2_done, 2)
                    vm = VM[0:32, :].rearrange("p (h c) -> p h c", h=2)
                    chain.did(s.activation(vm, PS[0:32, 6:8, :], ACT.Copy))
                    act.wait_ge(vcz_clear, 2)
                    for r in range(4):
                        ins = s.activation(VCZ[32 * r:32 * r + 32, 64 * r:64 * r + 64],
                                           PS[32 * r:32 * r + 32, 5, 64 * (r % 2):64 * (r % 2) + 64], ACT.Copy)
                        if r < 3:
                            chain.did(ins)
                    ins.then_inc(w2_took, 1)
            act.wait_ge(tr_done, 2)
            for r in (32, 64):
                ins = s.activation(VM[r:r + 4, :].rearrange("p (h c) -> p h c", h=2),
                                   PS[r:r + 4, (4 if r == 32 else 6):(6 if r == 32 else 8), :], ACT.Copy)
                if r == 32:
                    chain.did(ins)
            ins.then_inc(phase_end, 1)
            at_phase(act, 1)
            P4 = PB.rearrange("p (u r k) -> p u r k", u=2, r=2)
            PT3 = PT.rearrange("p (r k) -> p r k", r=2)

            def exps(u):
                w = P * (u // 16 + 1)
                act.wait_ge(negmax_ready, u + 1)
                if u >= 2:
                    act.wait_ge(pt_done, transposed(u - 1))
                for r in range(2):
                    c = 2 * (u % 2) + r
                    ins = s.activation(P4[:, u % 2, r, 0:w], PS[:, c, 0:w], ACT.Exp,
                                       bias=SMALL[:, 16 + c:17 + c], accum_out=SMALL[:, 64 + c:65 + c])
                    if r == 0:
                        chain.did(ins)
                ins.then_inc(p_ready, 1)

            def cmp_exp(i):
                act.wait_ge(sc_masked, i + 1)
                s.activation(SC, SC, ACT.Exp).then_inc(pc_ready, 1)

            def cmp_hi_part(i):
                act.wait_ge(pct_done, i + 1)
                s.activation(PCH, PS[:, 6, :], ACT.Copy).then_inc(pc_hi, 1)

            def out_hi(n):
                act.wait_ge(pv_done, 4 * n + 4)
                for gg in range(2):
                    ins = s.activation(heads_of(XH3, n, gg), sums_of(n, gg), ACT.Copy)
                    if gg == 0:
                        chain.did(ins)
                ins.then_inc(ot_hi, 1)

            cmp_exp(0)
            exps(0)
            exps(1)
            cmp_hi_part(0)
            for u in range(64):
                w = P * (u // 16 + 1)
                if u >= 2:
                    act.wait_ge(pv_done, u - 1)
                for r in range(2):
                    act.wait_ge(pt_done, 2 * u + r + 1)
                    s.activation(PTS[:, u % 2, 0, r, 0:w], PS[:, 4 + r, 0:w], ACT.Copy).then_inc(pt_act, 1)
                if u < 62:
                    exps(u + 2)
                if u % 4 == 0 and u:
                    out_hi(u // 4 - 1)
                if u % 16 == 10 and u < 48:
                    cmp_exp(u // 16 + 1)
                if u % 16 == 15 and u < 48:
                    cmp_hi_part(u // 16 + 1)
            out_hi(15)
            PMS = SC[:, 0:96]
            for v in range(4):
                u = 64 + v
                if v == 2:
                    act.wait_ge(pv_done, 66)
                    for bb in range(4):
                        act.dma_start(CACHE[:, 4096 + bb * 1024:4096 + (bb + 1) * 1024], a["cache_win"][4 + bb])\
                            .then_inc(win_landed, 16)
                hb, gg = v // 2, v % 2
                act.wait_ge(negmax_ready, u + 1)
                act.wait_ge(pt_done, transposed(u))
                nm = lambda r: SMALL[:, 24 + r:25 + r]
                sm = lambda r: SMALL[:, 32 + r:33 + r]
                for r in range(2):
                    chain.did(s.activation(P4[:, u % 2, r, :], PS[:, 2 * (u % 2) + r, :], ACT.Exp, bias=nm(1 + r), accum_out=sm(1 + r)))
                    reg = PMS[:, 32 * (r + 1):32 * (r + 1) + 4]
                    chain.did(s.activation(reg, reg, ACT.Exp, bias=nm(1 + r), accum_out=sm(3 + r)))
                s.activation(PMS[:, 0:32], PMS[:, 0:32], ACT.Exp, bias=nm(0), accum_out=sm(0))\
                    .then_inc(p_ready, 1)
                act.wait_ge(pt_done, transposed(u + 1))
                s.activation(PT3[:, 1, :], PS[:, 5, :], ACT.Copy).then_inc(pt_act, 1)
                if gg == 1:
                    act.wait_ge(ot_done, hb + 1)
                    xo = XH3[:, :, hb * HALF + HP:(hb + 1) * HALF].rearrange("p j (b s) -> p b j s", b=4)
                    s.activation(xo, PS[:, 4, 0:P].rearrange("p (b j s) -> p b j s", b=4, j=NJ), ACT.Copy)\
                        .then_inc(ot_hi, 1)
            act.wait_ge(ot_hi, 18)
            s.activation(SMALL[:, 509:510], SMALL[:, 1:2], ACT.Copy).then_inc(phase_end, 1)
            for k in range(8):
                act.wait_ge(tile_done, O0["w_out"] + k + 1)
                splits.after(O0["w_out"] + k)

            def ln(idx, outh, sem_h):
                for k in range(KT):
                    act.wait_ge(d_ready, 8 * idx + k + 1)
                    if k >= 4:
                        act.wait_ge(var_done, 4 * idx + k // 2 - 1)
                    s.activation(SQ4[k % 4], X3[:, k, :], ACT.Square).then_inc(sq_ready, 1)
                act.wait_ge(v_ready, idx + 1)
                chain.did(s.activation(RS, LT[:, 0:TOK], ACT.Ln))
                chain.sync()
                s.activation(RS, RS, ACT.Exp, scale=-0.5).then_inc(r0_ready, 1)
                for k in range(KT):
                    act.wait_ge(ln_out, 8 * idx + k + 1)
                    s.activation(outh[:, k, :], X3[:, k, :], ACT.Copy).then_inc(sem_h, 1)

            def tail(layer):
                if layer == 0:
                    s.activation(SMALL[:, 508:509], SMALL[:, 1:2], ACT.Copy).then_inc(gh_ready, 1)
                ln(2 * layer, XH3, xh_ready)
                base = O0[f"ffn{layer}"]
                nb = 48 * layer
                at_a = taken(base)[1] - 1
                c_start = splits.c
                with act.Fori(0, 3) as t:
                    for n in range(16):
                        e = EXT[:, (n % 4) * U:(n % 4 + 1) * U]
                        es = e[:, 2 + SEQ:U].rearrange("p (h b c) -> p h b c", h=2, b=4)
                        act.wait_ge(tile_done, 24 * t + (base + n + 1))
                        act.wait_ge(ext_free, 16 * t + (nb + 4 * layer + n + 1))
                        o = banks(base + n)
                        s.activation(e[:, 2:2 + SEQ].rearrange("p (h t) -> p h t", h=2), o[:, :, 0:HP], ACT.Copy)\
                            .then_inc(act_chain, 1)
                        s.activation(es[:, :, :, 2:6], o[:, :, HP:HALF].rearrange("p h (b s) -> p h b s", b=4),
                                     ACT.Copy).then_inc(act_took, 1)
                        splits.after(base + n, t)
                        if n % 2 == 1:
                            p = n // 2
                            act.wait_ge(ext_free, 16 * t + (EXT0[layer] + n))
                            s.activation(G1[:, 0:UO], CV[:, ((n - 1) % 4) * U:((n - 1) % 4) * U + UO], ACT.Gelu_apprx_tanh)\
                                .then_inc(gelu_done, 1)
                            act.wait_ge(prod_done, 8 * t + (PROD0[layer] + p + 1))
                            s.activation(GH3[:, p, :], PR, ACT.Copy).then_inc(gh_ready, 1)
                    for n in range(8):
                        act.wait_ge(tile_done, 24 * t + (base + 16 + n + 1))
                        splits.after(base + 16 + n, t)
                    splits.c = c_start
                splits.c = c_start + 72
                chain.n += 48
                act.wait_ge(p_landed, 16 * (layer + 1))
                s.activation(XH[:, 0:2 * TOK], PRAW, ACT.Copy).then_inc(ph_ready, 1)
                ln_proj(2 * layer + 1, layer)
                for k in range(KT):
                    o = O0[f"gate{layer}"] + k
                    act.wait_ge(tile_done, o + 1)
                    if k >= 2:
                        act.wait_ge(y_ready, 8 * layer + k - 1)
                    s.activation(halves(LT[:, (k % 2) * TOK:(k % 2 + 1) * TOK]), banks(o), ACT.Sigmoid)\
                        .then_inc(act_took, 1)
                    splits.after(o)
                    if layer == 0:
                        act.wait_ge(y_ready, k + 1)
                        s.activation(XH3[:, k, :], X3[:, k, :], ACT.Copy).then_inc(xh_ready, 1)

            def ln_proj(idx, layer):
                for k in range(KT):
                    act.wait_ge(d_ready, 8 * idx + k + 1)
                    act.wait_ge(var_done, 4 * idx + max(k // 2 - 1, 0))
                    s.activation(SQ4[k % 4], X3[:, k, :], ACT.Square).then_inc(sq_ready, 1)

                def proj(k):
                    o = O0[f"proj{layer}"] + k
                    act.wait_ge(tile_done, o + 1)
                    s.activation(halves(PP3[:, k, :]), banks(o), ACT.Copy).then_inc(act_took, 1)
                    splits.after(o)

                proj(0)
                proj(1)
                act.wait_ge(v_ready, idx + 1)
                chain.did(s.activation(RS, LT[:, 0:TOK], ACT.Ln))
                chain.sync()
                s.activation(RS, RS, ACT.Exp, scale=-0.5).then_inc(r0_ready, 1)
                for k in range(KT):
                    if k < 6:
                        proj(k + 2)
                    act.wait_ge(ln_out, 8 * idx + k + 1)
                    s.activation(GH3[:, k, :], X3[:, k, :], ACT.Copy).then_inc(gh_ready, 1)

            tail(0)
            s.activation(SMALL[:, 509:510], SMALL[:, 1:2], ACT.Copy).then_inc(phase_end, 1)
            at_phase(act, 3)
            act.wait_ge(lam_ready, 1)
            s.activation(SMALL[:, 40:48], SMALL[:, 40:48], ACT.Exp, scale=-1.0).then_inc(sp_ready, 1)
            for n in range(8):
                o = O0["rec"] + n
                act.wait_ge(tile_done, o + 1)
                if n >= 2:
                    act.wait_ge(rec_ready, n - 1)
                else:
                    act.wait_ge(lam_ready, 2)
                e = REXT[:, (n % 2) * UR:(n % 2 + 1) * UR]
                es = e[:, 3 + SEQ:UR].rearrange("p (h b c) -> p h b c", h=2, b=4)
                chain.did(s.activation(e[:, 3:3 + SEQ].rearrange("p (h t) -> p h t", h=2), banks(o)[:, :, 0:HP], ACT.Copy))
                s.activation(es[:, :, :, 3:7], banks(o)[:, :, HP:HALF].rearrange("p h (b s) -> p h b s", b=4),
                             ACT.Copy).then_inc(act_took, 1)
                splits.after(o)
                act.wait_ge(rec_ready, n + 1)
                s.activation(GH3[:, n, :], REC3[:, n, :], ACT.Copy).then_inc(gh_ready, 1)
            act.wait_ge(sp_ready, 2)
            for n in range(8):
                o = O0["rgate"] + 2 * n
                act.wait_ge(tile_done, o + 1)
                s.activation(halves(RR3[:, n, :]), banks(o), ACT.Sigmoid, bias=par("ga_b", n)).then_inc(act_took, 1)
                act.wait_ge(tile_done, o + 2)
                if n >= 2:
                    act.wait_ge(m_ready, n - 1)
                s.activation(halves(RTM[:, (n % 2) * TOK:(n % 2 + 1) * TOK]), banks(o + 1), ACT.Sigmoid,
                             bias=par("gx_b", n)).then_inc(act_took, 1)
                splits.after(o + 1)
                act.wait_ge(act_took, taken(o)[1])
                s.activation(VV3[:, n, :], RR3[:, n, :], ACT.Tanh, scale=SMALL[:, 56 + n:57 + n]).then_inc(sig_ready, 1)
            act.wait_ge(sig_ready, 8)
            for n in range(8):
                s.activation(RR3[:, n, :], RR3[:, n, :], ACT.Exp, scale=SMALL[:, 48 + n:49 + n]).then_inc(a_ready, 1)
            for n in range(8):
                s.activation(VV3[:, n, :], VV3[:, n, :], ACT.Sqrt).then_inc(sqrt_ready, 1)
            for n in range(8):
                o = O0["gbr"] + n
                act.wait_ge(tile_done, o + 1)
                if n >= 2:
                    act.wait_ge(prod_done, GATED0 + n - 1)
                else:
                    act.wait_ge(m_ready, 8)
                s.activation(halves(RTM[:, (n % 2) * TOK:(n % 2 + 1) * TOK]), banks(o), ACT.Gelu_apprx_tanh)\
                    .then_inc(act_took, 1)
                splits.after(o)
                act.wait_ge(prod_done, GATED0 + n + 1)
                s.activation(GH3[:, n, :], REC3[:, n, :], ACT.Copy).then_inc(gh_ready, 1)
            for k in range(8):
                act.wait_ge(tile_done, O0["rg_out"] + k + 1)
                splits.after(O0["rg_out"] + k)
            s.activation(SMALL[:, 509:510], SMALL[:, 1:2], ACT.Copy).then_inc(phase_end, 1)
            tail(1)

        @block.vector
        def _(dve):
            v = nc.vector
            chain = Chain(dve, dve_chain)
            splits = Splits(dve, split_lo)

            def sub_lo(dst, full, hi, s):
                return v.tensor_tensor(dst, full, hi.bitcast(F32), ALU.subtract).then_inc(s, 1)

            dve.wait_ge(x_landed, 16)
            for k in range(KT):
                dve.wait_ge(xh_ready, k + 1)
                sub_lo(XL3[:, k, :], X3[:, k, :], XH3[:, k, :], xl_ready)
                if k in (0, 1, 2):
                    split_lo(dve, k)
            splits.c = 3
            CR = CACHE.rearrange("p (n v m c) -> p n v m c", n=NB * PAGES, v=2, m=16)

            def cmp_lo(kv, hi, dst, piece):
                dve.wait_ge(cs_hi, piece + 1)
                view = lambda t: t[:, 0:4096].rearrange("p (m b n c) -> p b n m c", m=16, b=NB, n=PAGES)
                for b in range(NB):
                    ins = v.tensor_tensor(view(dst)[:, b], CR[:, b * PAGES:(b + 1) * PAGES, kv],
                                          view(hi)[:, b].bitcast(F32), ALU.subtract)
                    if b < NB - 1:
                        chain.did(ins)
                ins.then_inc(cs_lo, 1)

            def cmp_lo_prompt(kv, hi, dst, piece):
                dve.wait_ge(cs_hi, piece + 1)
                view = lambda t: t[:, 4096:OPW].rearrange("p (m c) -> p m c", m=8)
                for gg in range(2):
                    cols = slice(gg * 32, gg * 32 + 32)
                    chain.did(v.tensor_tensor(view(dst)[:, :, cols],
                                              XPR[:, kv * 512 + gg * 256:kv * 512 + gg * 256 + 256]
                                              .rearrange("p (m c) -> p m c", m=8),
                                              view(hi)[:, :, cols].bitcast(F32), ALU.subtract))
                v.tensor_tensor(view(dst)[:, :, 64:66], par("pe", kv * 16, 16).rearrange("p (m c) -> p m c", m=8),
                                view(hi)[:, :, 64:66].bitcast(F32), ALU.subtract).then_inc(cs_lo, 1)

            for n in range(15):
                dve.wait_ge(tile_done, n + 1)
                splits.after(n)
                if n == 3:
                    cmp_lo(0, GH, GL, 0)
            cmp_lo_prompt(0, GH, GL, 1)
            cmp_lo(1, XH, XL, 2)
            cmp_lo_prompt(1, XH, XL, 3)
            dve.wait_ge(par_landed, 32)
            dve.wait_ge(consts_ready, 1)
            chain.did(v.memset(HS[:, :], 0.0))
            chain.did(v.memset(HPR[:, :], 0.0))
            v.tensor_copy(KCZ, ZERO.to_broadcast([P, 128])).then_inc(vcz_clear, 1)
            chain.sync()
            def q_lo(at):
                for j in range(at, at + 4):
                    dve.wait_ge(qk_hi, j + 2)
                    sub_lo(QL[:, j, :], QF[:, j, :], QH[:, j, :], qk_lo)

            for n in range(8):
                kv, hh = n // 4, (n // 2) % 2
                o = O0["cmp"] + n
                b = 2 * (o % 2)
                if n % 2:
                    dve.wait_ge(tile_done, o + 1)
                    dve.wait_ge(act_took, taken(o - 1)[1])
                    if n == 5:
                        dve.wait_ge(w2_done, 1)
                        q_lo(0)
                    rows = lambda ap: ap.rearrange("p (r c) -> p r c", c=32)
                    chain.did(v.tensor_tensor(rows(HS[:, hh * 512:(hh + 1) * 512])[:, :, 0:NC],
                                              rows(AT[:, 0:512])[:, :, 0:NC],
                                              rows(PS[:, b, :])[:, :, 1:32], ALU.add))
                    chain.did(v.tensor_tensor(rows(HPR[:, hh * 64:(hh + 1) * 64])[:, :, 0:NC],
                                              rows(AT[:, 512:576])[:, :, 0:NC],
                                              rows(PS[:, b + 1, 0:64])[:, :, 1:32], ALU.add))
                    bt = SMALL[:, 8 + n // 2:9 + n // 2]
                    chain.did(v.tensor_tensor(bt, AT[:, 576:577], PS[:, b + 1, 65:66], ALU.add))
                    chain.sync()
                    v.tensor_tensor(bt, bt, par("cmp_b1", n // 2), ALU.add).then_inc(hid_sum, 1)
                    dve.wait_ge(hid_sum, n // 2 + 1)
                    v.memset(SMALL[:, 6:7], 0.0).then_inc(dve_took, 1)
                splits.after(o)
                if n == 3:
                    dve.wait_ge(w2_took, 1)
                    for gg in range(2):
                        rows = slice(64 * gg, 64 * gg + 64)
                        v.tensor_tensor(KCZ[rows, 64 + 32 * gg:96 + 32 * gg], PS[rows, 5, 0:32],
                                        KCZ[rows, 32 * gg:32 * gg + 32].bitcast(F32), ALU.subtract).then_inc(qk_lo, 1)
                    dve.wait_ge(tr_took, 1)
                    dve.wait_ge(kv_out, 32)
                    hv = lambda ap: ap.rearrange("p (h c) -> p h c", h=2)
                    sub_lo(hv(VL), PS[:, 6:8, :], hv(VH), qk_lo)
                if n == 5:
                    dve.wait_ge(qk_hi, 1)
                    sub_lo(KL, KT4[:, 0:1024], KH, qk_lo)
                    dve.wait_ge(qk_lo, 8)
                    v.tensor_copy(VCZ, ZERO.to_broadcast([P, 512])).then_inc(vcz_clear, 1)
            q_lo(4)
            dve.wait_ge(w2_took, 2)
            for r in range(4):
                v.tensor_tensor(VCZ[32 * r:32 * r + 32, 256 + 64 * r:320 + 64 * r],
                                PS[32 * r:32 * r + 32, 5, 64 * (r % 2):64 * (r % 2) + 64],
                                VCZ[32 * r:32 * r + 32, 64 * r:64 * r + 64].bitcast(F32), ALU.subtract).then_inc(qk_lo, 1)
            dve.wait_ge(consts_ready, 1)
            g0 = GT[:, 0:48].rearrange("p (h r) -> p h r", r=3)[:, :, 0:1]
            dve.wait_ge(dve_took, 4)
            v.tensor_scalar(g0, g0, SMALL[:, 0:1], None, ALU.mult).then_inc(phase_end, 1)
            at_phase(dve, 1)
            SCL = SMALL[:, 168:174]
            P4 = PB.rearrange("p (u r k) -> p u r k", u=2, r=2)
            sc3 = SC.rearrange("p (h c) -> p h c", c=32)

            def neg_max(u):
                w = P * (u // 16 + 1)
                dve.wait_ge(s_done, u + 1)
                nm = SMALL[:, 16 + 2 * (u % 2):18 + 2 * (u % 2)]
                v.tensor_reduce(nm, PS[:, 2 * (u % 2):2 * (u % 2) + 2, 0:w], AX_X, ALU.max, negate=True)\
                    .then_inc(negmax_ready, 1)

            def gate_over_sum(u):
                w = P * (u // 16 + 1)
                dve.wait_ge(p_ready, u + 1)
                c = SMALL[:, 160 + 2 * (u % 2):162 + 2 * (u % 2)]
                chain.did(v.reciprocal(c, SMALL[:, 64 + 2 * (u % 2):66 + 2 * (u % 2)]))
                chain.sync()
                g0 = 48 * (u // 16) + 3 * (u % 16) + 1
                chain.did(v.tensor_tensor(c, c, GT[:, g0:g0 + 2], ALU.mult))
                chain.sync()
                if w == P:
                    pr = P4[:, u % 2, :, 0:w]
                    v.tensor_tensor(pr, pr, c.unsqueeze(2).to_broadcast([P, 2, w]), ALU.mult).then_inc(ps_ready, 2)
                else:
                    for r in range(2):
                        pr = P4[:, u % 2, r, 0:w]
                        v.tensor_scalar(pr, pr, c[:, r:r + 1], None, ALU.mult).then_inc(ps_ready, 1)

            def cmp_mask(i):
                dve.wait_ge(sc_done, i + 1)
                if i:
                    dve.wait_ge(pct_done, i)
                chain.did(v.tensor_tensor(sc3, PS[:, 7, :].rearrange("p (h c) -> p h c", c=32),
                                          CMASK[:, 32 * i:32 * i + 32].unsqueeze(1).to_broadcast([P, 16, 32]), ALU.add))
                chain.sync()
                mx = SMALL[:, 176:192]
                chain.did(v.tensor_reduce(mx, sc3, AX_X, ALU.max))
                chain.sync()
                v.tensor_tensor(sc3, sc3, mx.unsqueeze(2).to_broadcast([P, 16, 32]), ALU.subtract)\
                    .then_inc(sc_masked, 1)

            def cmp_scale(i):
                dve.wait_ge(pc_ready, i + 1)
                sm = SMALL[:, 192:208]
                chain.did(v.tensor_reduce(sm, sc3, AX_X, ALU.add))
                chain.sync()
                chain.did(v.reciprocal(sm, sm))
                chain.sync()
                chain.did(v.tensor_tensor(sm, sm, GT[:, 48 * i:48 * i + 48].rearrange("p (h r) -> p h r", r=3)[:, :, 0],
                                          ALU.mult))
                chain.sync()
                v.tensor_tensor(sc3, sc3, sm.unsqueeze(2).to_broadcast([P, 16, 32]), ALU.mult).then_inc(pc_scaled, 1)

            def cmp_lo_part(i):
                dve.wait_ge(pc_hi, i + 1)
                sub_lo(PCL, PS[:, 6, :], PCH, pc_lo)

            def out_lo(n):
                dve.wait_ge(ot_hi, n + 1)
                for gg in range(2):
                    ins = v.tensor_tensor(heads_of(XL3, n, gg), sums_of(n, gg), heads_of(XH3, n, gg).bitcast(F32),
                                          ALU.subtract)
                    if gg == 0:
                        chain.did(ins)
                ins.then_inc(ot_lo, 1)

            cmp_mask(0)
            neg_max(0)
            neg_max(1)
            cmp_scale(0)
            gate_over_sum(0)
            cmp_lo_part(0)
            for u in range(64):
                w = P * (u // 16 + 1)
                if u < 63:
                    gate_over_sum(u + 1)
                for r in range(2):
                    dve.wait_ge(pt_act, 2 * u + r + 1)
                    sub_lo(PTS[:, u % 2, 1, r, 0:w], PS[:, 4 + r, 0:w], PTS[:, u % 2, 0, r, 0:w], pt_dve)
                if u < 62:
                    neg_max(u + 2)
                if u % 4 == 0 and u:
                    out_lo(u // 4 - 1)
                if u % 16 == 10 and u < 48:
                    cmp_mask(u // 16 + 1)
                if u % 16 == 11 and u < 48:
                    cmp_scale(u // 16 + 1)
                if u % 16 == 15 and u < 48:
                    cmp_lo_part(u // 16 + 1)
            out_lo(15)
            PT3 = PT.rearrange("p (r k) -> p r k", r=2)
            PMS = SC[:, 0:96]
            chain.did(v.memset(PMS, 0.0))
            chain.sync()
            for vv in range(4):
                u = 64 + vv
                hb, gg = vv // 2, vv % 2
                dve.wait_ge(s_done, u + 1)
                if vv:
                    dve.wait_ge(pt_done, transposed(u))
                mb = PS[:, 6, :]
                w0 = PS[:, 2 * (u % 2) + 1, 0:4]
                chain.did(v.tensor_tensor(w0, w0, SMASK[:, 4:8], ALU.add))
                chain.did(v.tensor_copy(PMS[:, 0:32], mb[:, 0:32]))
                for r in (1, 2):
                    chain.did(v.tensor_tensor(PMS[:, 32 * r:32 * r + 4], mb[:, 32 * r:32 * r + 4], SMASK[:, 0:4], ALU.add))
                chain.sync()
                chain.did(v.memset(PMS[:, NC:NC + 1], NEG))
                nm, nm2 = SMALL[:, 24:27], SMALL[:, 28:30]
                chain.did(v.tensor_reduce(nm[:, 1:3], PS[:, 2 * (u % 2):2 * (u % 2) + 2, :], AX_X, ALU.max, negate=True))
                chain.did(v.tensor_reduce(nm2, PMS[:, 32:96].rearrange("p (r c) -> p r c", r=2)[:, :, 0:4], AX_X, ALU.max, negate=True))
                chain.sync()
                chain.did(v.tensor_reduce(nm[:, 0:1], PMS[:, 0:32], AX_X, ALU.max, negate=True))
                v.tensor_tensor(nm[:, 1:3], nm[:, 1:3], nm2, ALU.min).then_inc(negmax_ready, 1)
                dve.wait_ge(pt_done, transposed(u + 1))
                dve.wait_ge(pv_done, u)
                chain.did(v.tensor_copy(OTMP[0:96, 256:384], PS[0:96, 6, 128:256]))
                v.tensor_copy(PT3[:, 0, :], PS[:, 4, :]).then_inc(pt_dve, 1)
                dve.wait_ge(p_ready, u + 1)
                sums = SMALL[:, 32:37]
                chain.did(v.tensor_tensor(sums[:, 1:3], sums[:, 1:3], sums[:, 3:5], ALU.add))
                chain.sync()
                sc = SCL[:, 0:3]
                chain.did(v.reciprocal(sc, sums[:, 0:3]))
                chain.sync()
                if vv == 0:
                    dve.wait_ge(gate_dma, 16 * 34)
                chain.did(v.tensor_tensor(sc, sc, GS[:, 6 * hb + 3 * gg:6 * hb + 3 * gg + 3], ALU.mult))
                chain.sync()
                dve.wait_ge(pv_done, u + 1)
                if gg == 0:
                    if hb:
                        dve.wait_ge(ot_done, hb)
                o3 = OTMP[:, 0:192].rearrange("p (r d) -> p r d", r=3)
                chain.did(v.tensor_copy(o3, PS[:, 7, 0:192].rearrange("p (r d) -> p r d", r=3)))
                chain.sync()
                chain.did(v.tensor_tensor(o3[:, 1:3, :], o3[:, 1:3, :], PS[:, 2 * (u % 2):2 * (u % 2) + 2, 0:HD], ALU.add))
                chain.sync()
                chain.did(v.tensor_tensor(o3, o3, sc.unsqueeze(2).to_broadcast([P, 3, HD]), ALU.mult))
                chain.sync()
                os = OS[:, gg * HD:(gg + 1) * HD]
                chain.did(v.tensor_tensor(os, o3[:, 0, :], o3[:, 1, :], ALU.add))
                chain.sync()
                v.tensor_tensor(os, os, o3[:, 2, :], ALU.add).then_inc(o_ready, 1)
                dve.wait_ge(o_ready, vv + 1)
                if gg == 1:
                    dve.wait_ge(ot_hi, 16 + hb + 1)
                    xo = lambda t: t[:, :, hb * HALF + HP:(hb + 1) * HALF].rearrange("p j (b s) -> p b j s", b=4)
                    sub_lo(xo(XL3), PS[:, 4, 0:P].rearrange("p (b j s) -> p b j s", b=4, j=NJ), xo(XH3), ot_lo)
            v.memset(SMALL[:, 6:7], 0.0).then_inc(phase_end, 1)
            at_phase(dve, 2)
            dve.wait_ge(x_back, 16)

            def residual(name):
                for k in range(KT):
                    o = O0[name] + k
                    dve.wait_ge(tile_done, o + 1)
                    v.scalar_tensor_tensor(out=halves(X3[:, k, :]), in0=halves(X3[:, k, :]), scalar=ALPHA,
                                           in1=banks(o), op0=ALU.mult, op1=ALU.add).then_inc(dve_took, 1)
                    if k:
                        dve.wait_ge(dve_took, taken(o)[1])
                        if k > 1:
                            chain.sync()
                        ins = v.tensor_tensor(XSUM_, XSUM_ if k > 1 else X3[:, 0, :], X3[:, k, :], ALU.add)
                        if k < KT - 1:
                            chain.did(ins)
                        else:
                            ins.then_inc(xsum_ready, 1)
                    splits.after(o)

            residual("w_out")

            def ln(idx, outh, outl, sem_h, h0, sem_l, last_o):
                dve.wait_ge(mean_done, idx + 1)
                dve.wait_ge(dve_took, taken(last_o)[1])
                centre(idx)
                dve.wait_ge(var_done, 4 * idx + 4)
                v.tensor_scalar(halves(LT[:, 0:TOK]), PS[:, 6:8, 0:HALF], EPS, None, ALU.add).then_inc(v_ready, 1)
                dve.wait_ge(r0_ready, idx + 1)
                tmp = LT[:, TOK:2 * TOK]
                chain.did(v.tensor_tensor(tmp, RS, RS, ALU.mult))
                chain.sync()
                chain.did(v.scalar_tensor_tensor(out=tmp, in0=tmp, scalar=-0.5, in1=LT[:, 0:TOK], op0=ALU.mult,
                                                 op1=ALU.mult))
                chain.sync()
                chain.did(v.scalar_tensor_tensor(out=RS, in0=tmp, scalar=1.5, in1=RS, op0=ALU.add, op1=ALU.mult))
                chain.sync()
                dve.wait_ge(d_ready, 8 * idx + 8)
                for k in range(KT):
                    if k >= 2:
                        lo_part(k - 2, outh, outl, sem_h, h0, sem_l)
                    v.tensor_tensor(X3[:, k, :], X3[:, k, :], RS, ALU.mult).then_inc(n_ready, 1)
                for k in (6, 7):
                    lo_part(k, outh, outl, sem_h, h0, sem_l)

            def centre(idx):
                for k in range(KT):
                    v.tensor_tensor(halves(X3[:, k, :]), halves(X3[:, k, :]), PS[:, 4:6, 0:HALF], ALU.subtract)\
                        .then_inc(d_ready, 1)
                    for pair in {2: (0,), 4: (1,), 6: (2,), 7: (3,)}.get(k, ()):
                        dve.wait_ge(sq_ready, 8 * idx + 2 * pair + 2)
                        a0, a1 = SQ4[2 * (pair % 2)], SQ4[2 * (pair % 2) + 1]
                        v.tensor_tensor(a0, a0, a1, ALU.add).then_inc(pair_ready, 1)

            def lo_part(k, outh, outl, sem_h, h0, sem_l):
                dve.wait_ge(sem_h, h0 + k + 1)
                sub_lo(outl[:, k, :], X3[:, k, :], outh[:, k, :], sem_l)

            def tail(layer):
                for e in range(4):
                    v.memset(EXT[:, e * U:e * U + 2], 0.0).then_inc(ext_free, 1)
                for e in range(2):
                    v.memset(SMALL[:, 4 + e:5 + e], 0.0).then_inc(prod_done, 1)
                if layer == 0:
                    v.memset(SMALL[:, 7:8], 0.0).then_inc(gl_ready, 1)
                    v.memset(RES, ALPHA).then_inc(scale_set, 1)
                else:
                    dve.wait_ge(scale_set, 4)
                    chain.did(v.memset(RES, ALPHA))
                    chain.sync()
                ln(2 * layer, XH3, XL3, xh_ready, XL_COUNT[f"ln1_{layer}"], xl_ready, O0[f"ffn{layer}"] - 1)
                base = O0[f"ffn{layer}"]
                nb = 48 * layer
                d0 = taken(base - 1)[1]
                c_start = splits.c
                n_chain = chain.n
                n_per = 16 + 8 + 6
                with dve.Fori(0, 3) as t:
                    for n in range(16):
                        e = EXT[:, (n % 4) * U:(n % 4 + 1) * U]
                        cv = CV[:, (n % 4) * U:(n % 4) * U + UO]
                        dve.wait_ge(tap0_done, 16 * t + (nb + n + 1))
                        v.scalar_tensor_tensor(out=cv, in0=e[:, 1:1 + UO],
                                               scalar=CWS[:, 4 * (n % 4) + 1:4 * (n % 4) + 2],
                                               in1=cv, op0=ALU.mult, op1=ALU.add).then_inc(dve_chain, 1)
                        dve.wait_ge(dve_chain, n_per * t + (n_chain + n + n // 2 + 1))
                        v.scalar_tensor_tensor(out=cv, in0=e[:, 2:2 + UO],
                                               scalar=CWS[:, 4 * (n % 4) + 2:4 * (n % 4) + 3],
                                               in1=cv, op0=ALU.mult, op1=ALU.add).then_inc(ext_free, 1)
                        splits.after(base + n, t)
                        if n % 2 == 1:
                            p = n // 2
                            dve.wait_ge(gelu_done, 8 * t + (24 * layer + p + 1))
                            dve.wait_ge(ext_free, 16 * t + (EXT0[layer] + n + 1))
                            dve.wait_ge(gl_ready, 8 * t + (GL_COUNT[f"ffn{layer}"] + p))
                            v.tensor_tensor(halves(PR)[:, :, 0:HP], G1[:, 0:SEQ].rearrange("p (h t) -> p h t", h=2),
                                            cv[:, 0:SEQ].rearrange("p (h t) -> p h t", h=2), ALU.mult)\
                                .then_inc(dve_chain, 1)
                            v.tensor_tensor(halves(PR)[:, :, HP:HALF].rearrange("p h (b s) -> p h b s", b=4),
                                            seqs(G1), seqs(CV[:, (n % 4) * U:(n % 4 + 1) * U]), ALU.mult).then_inc(prod_done, 1)
                            dve.wait_ge(gh_ready, 8 * t + (GL_COUNT[f"ffn{layer}"] + p + 1))
                            dve.wait_ge(prod_done, 8 * t + (PROD0[layer] + p + 1))
                            sub_lo(GL3[:, p, :], PR, GH3[:, p, :], gl_ready)
                    for n in range(8):
                        o = base + 16 + n
                        dve.wait_ge(tile_done, 24 * t + (o + 1))
                        if n == 0:
                            dve.wait_ge(dve_took, 8 * t + d0)
                            dve.wait_ge(scale_set, t + (1 + 3 * layer))
                        v.scalar_tensor_tensor(out=halves(X3[:, n, :]), in0=halves(X3[:, n, :]), scalar=RES,
                                               in1=banks(o), op0=ALU.mult, op1=ALU.add).then_inc(dve_took, 1)
                        if n:
                            dve.wait_ge(dve_took, 8 * t + (d0 + n + 1))
                            if n == 1:
                                dve.wait_ge(xsum_ready, t + XSUM[2 * layer])
                            else:
                                dve.wait_ge(dve_chain, n_per * t + (n_chain + 24 + n - 1))
                            v.tensor_tensor(XSUM_, XSUM_ if n > 1 else X3[:, 0, :], X3[:, n, :], ALU.add)\
                                .then_inc(xsum_ready if n == KT - 1 else dve_chain, 1)
                        if n == KT - 1:
                            dve.wait_ge(dve_took, 8 * t + (d0 + n + 1))
                            v.memset(RES, 1.0).then_inc(scale_set, 1)
                        splits.after(o, t)
                    splits.c = c_start
                splits.c = c_start + 72
                chain.n = n_chain + 3 * n_per
                dve.wait_ge(ph_ready, layer + 1)
                sub_lo(XL[:, 0:2 * TOK], PRAW, XH[:, 0:2 * TOK], pl_ready)
                ln_proj(2 * layer + 1, layer)
                for k in range(KT):
                    o = O0[f"gate{layer}"] + k
                    lt = LT[:, (k % 2) * TOK:(k % 2 + 1) * TOK]
                    dve.wait_ge(act_took, taken(o)[1])
                    chain.did(v.tensor_tensor(PP3[:, k, :], PP3[:, k, :], lt, ALU.mult))
                    chain.sync()
                    v.tensor_tensor(X3[:, k, :], X3[:, k, :], PP3[:, k, :], ALU.add).then_inc(y_ready, 1)
                    splits.after(o)
                    if layer == 0:
                        dve.wait_ge(xh_ready, XL_COUNT["x1"] + k + 1)
                        sub_lo(XL3[:, k, :], X3[:, k, :], XH3[:, k, :], xl_ready)

            def seqs(ap):
                return ap[:, SEQ + 2:U].rearrange("p (h b c) -> p h b c", h=2, b=4)[:, :, :, 0:4]

            def ln_proj(idx, layer):
                dve.wait_ge(mean_done, idx + 1)
                dve.wait_ge(dve_took, taken(O0[f"proj{layer}"] - 1)[1])
                centre(idx)
                for k in range(2):
                    dve.wait_ge(tile_done, O0[f"proj{layer}"] + k + 1)
                    splits.after(O0[f"proj{layer}"] + k)
                dve.wait_ge(var_done, 4 * idx + 4)
                v.tensor_scalar(halves(LT[:, 0:TOK]), PS[:, 6:8, 0:HALF], EPS, None, ALU.add).then_inc(v_ready, 1)
                dve.wait_ge(r0_ready, idx + 1)
                tmp = LT[:, TOK:2 * TOK]
                chain.did(v.tensor_tensor(tmp, RS, RS, ALU.mult))
                chain.sync()
                chain.did(v.scalar_tensor_tensor(out=tmp, in0=tmp, scalar=-0.5, in1=LT[:, 0:TOK], op0=ALU.mult,
                                                 op1=ALU.mult))
                chain.sync()
                chain.did(v.scalar_tensor_tensor(out=RS, in0=tmp, scalar=1.5, in1=RS, op0=ALU.add, op1=ALU.mult))
                chain.sync()
                dve.wait_ge(d_ready, 8 * idx + 8)
                h0 = GL_COUNT[f"ln2_{layer}"]
                for k in range(KT):
                    v.tensor_tensor(X3[:, k, :], X3[:, k, :], RS, ALU.mult).then_inc(n_ready, 1)
                    if k < 6:
                        splits.after(O0[f"proj{layer}"] + k + 2)
                    if k >= 2:
                        lo_part(k - 2, GH3, GL3, gh_ready, h0, gl_ready)
                for k in (6, 7):
                    lo_part(k, GH3, GL3, gh_ready, h0, gl_ready)

            tail(0)
            v.memset(SMALL[:, 6:7], 0.0).then_inc(phase_end, 1)
            at_phase(dve, 3)
            lam = par("lam", 0, 8)
            z, sp = SMALL[:, 40:48], SMALL[:, 48:56]
            q, q2, acc = SMALL[:, 320:328], SMALL[:, 328:336], SMALL[:, 336:344]
            chain.did(v.tensor_scalar(z, lam, -1.0, None, ALU.mult))
            chain.sync()
            v.tensor_tensor(z, z, lam, ALU.max).then_inc(lam_ready, 1)

            def old_rows(n):
                e = REXT[:, (n % 2) * UR:(n % 2 + 1) * UR]
                es = e[:, 3 + SEQ:UR].rearrange("p (b c) -> p b c", b=NB)
                chain.did(v.tensor_copy(es[:, :, 0:3], par("rstate", 24 * n, 24).rearrange("p (b c) -> p b c", b=NB)))

            for n in range(2):
                chain.did(v.memset(REXT[:, n * UR:n * UR + 3], 0.0))
                old_rows(n)
            v.memset(SMALL[:, 7:8], 0.0).then_inc(lam_ready, 1)
            dve.wait_ge(sp_ready, 1)
            chain.did(v.tensor_scalar(q, z, 2.0, None, ALU.add))
            chain.sync()
            chain.did(v.reciprocal(q, q))
            chain.sync()
            chain.did(v.tensor_tensor(q, q, z, ALU.mult))
            chain.sync()
            chain.did(v.tensor_tensor(q2, q, q, ALU.mult))
            chain.did(v.memset(acc, 1.0 / 19))
            chain.sync()
            for m in range(17, 0, -2):
                chain.did(v.tensor_tensor(acc, acc, q2, ALU.mult))
                chain.sync()
                chain.did(v.tensor_scalar(acc, acc, 1.0 / m, None, ALU.add))
                chain.sync()
            chain.did(v.scalar_tensor_tensor(out=acc, in0=acc, scalar=2.0, in1=q, op0=ALU.mult, op1=ALU.mult))
            chain.did(v.tensor_scalar(sp, lam, -1.0, 0.0, ALU.mult, ALU.max))
            chain.sync()
            chain.did(v.tensor_tensor(sp, sp, acc, ALU.add))
            chain.sync()
            chain.did(v.tensor_scalar(SMALL[:, 56:64], sp, 4.0, None, ALU.mult))
            chain.sync()
            v.tensor_scalar(sp, sp, -8.0, None, ALU.mult).then_inc(sp_ready, 1)
            rg0 = GL_COUNT["rec"]
            for n in range(8):
                o = O0["rec"] + n
                e = REXT[:, (n % 2) * UR:(n % 2 + 1) * UR]
                es = e[:, 3 + SEQ:UR].rearrange("p (b c) -> p b c", b=NB)
                w = lambda k: par("rconv_w", 8 * k + n)
                dve.wait_ge(act_took, taken(o)[1])
                chain.did(v.tensor_scalar(RCV[:, 0:URO], e[:, 0:URO], w(0), par("rconv_b", n), ALU.mult, ALU.add))
                lt = LAST[:, 36 * n:36 * n + 36]
                chain.did(v.tensor_copy(lt[:, 0:3], e[:, SEQ:SEQ + 3]))
                chain.did(v.tensor_copy(lt[:, 3:27].rearrange("p (b c) -> p b c", b=NB), es[:, :, 4:7]))
                for k in (1, 2):
                    chain.sync()
                    chain.did(v.scalar_tensor_tensor(out=RCV[:, 0:URO], in0=e[:, k:k + URO], scalar=w(k), in1=RCV[:, 0:URO], op0=ALU.mult,
                                                     op1=ALU.add))
                chain.sync()
                r3 = halves(REC3[:, n, :])
                chain.did(v.scalar_tensor_tensor(out=r3[:, :, 0:HP], in0=e[:, 3:3 + SEQ].rearrange("p (h t) -> p h t", h=2),
                                                 scalar=w(3), in1=RCV[:, 0:SEQ].rearrange("p (h t) -> p h t", h=2),
                                                 op0=ALU.mult, op1=ALU.add))
                for h in range(2):
                    rows = RCV[:, SEQ + 3 + 28 * h:SEQ + 31 + 28 * h].rearrange("p (b c) -> p b c", b=4)[:, :, 0:4]
                    ins = v.scalar_tensor_tensor(out=r3[:, h, HP:HALF].rearrange("p (b s) -> p b s", b=4),
                                                 in0=es[:, 4 * h:4 * h + 4, 3:7], scalar=w(3),
                                                 in1=rows, op0=ALU.mult, op1=ALU.add)
                    if h == 0:
                        chain.did(ins)
                ins.then_inc(rec_ready, 1)
                dve.wait_ge(rec_ready, n + 1)
                if n < 6:
                    old_rows(n + 2)
                splits.after(o)
                dve.wait_ge(gh_ready, rg0 + n + 1)
                sub_lo(GL3[:, n, :], REC3[:, n, :], GH3[:, n, :], gl_ready)
            dve.wait_ge(gl_ready, rg0 + 8)
            for n in range(8):
                o = O0["rgate"] + 2 * n
                dve.wait_ge(act_took, taken(o + 1)[1])
                v.tensor_tensor(REC3[:, n, :], REC3[:, n, :], RTM[:, (n % 2) * TOK:(n % 2 + 1) * TOK], ALU.mult)\
                    .then_inc(m_ready, 1)
                splits.after(o + 1)
            dve.wait_ge(m_ready, 8)
            for n in range(8):
                dve.wait_ge(a_ready, n + 1)
                chain.did(v.scalar_tensor_tensor(out=REC3[:, n, :], in0=RR3[:, n, :], scalar=1.0, in1=REC3[:, n, :],
                                                 op0=ALU.add, op1=ALU.mult))
            for n in range(8):
                dve.wait_ge(sqrt_ready, n + 1)
                chain.sync()
                chain.did(v.tensor_tensor(VV3[:, n, :], VV3[:, n, :], REC3[:, n, :], ALU.mult))
                chain.sync()
                chain.did(v.tensor_tensor_scan(REC3[:, n, 0:HP], RR3[:, n, 0:HP], VV3[:, n, 0:HP], 0.0, ALU.mult, ALU.add))
                chain.sync()
                v.tensor_tensor_scan(REC3[:, n, HALF:HALF + HP], RR3[:, n, HALF:HALF + HP], VV3[:, n, HALF:HALF + HP],
                                     REC3[:, n, HP - 1:HP], ALU.mult, ALU.add).then_inc(h_ready, 1)
            smp = lambda t: t.rearrange("p (k t) -> p k t", k=16)[:, :, HP:HALF].rearrange("p k (b s) -> p k b s", b=4)
            prev = par("h0", 0, 64).rearrange("p (k b) -> p k b", k=16)
            tmp = SMALL[:, 256:320].rearrange("p (k b) -> p k b", k=16)
            for st in range(NS):
                chain.sync()
                chain.did(v.tensor_tensor(tmp, smp(RR)[:, :, :, st], prev, ALU.mult))
                chain.sync()
                chain.did(v.tensor_tensor(smp(REC)[:, :, :, st], tmp, smp(VV)[:, :, :, st], ALU.add))
                prev = smp(REC)[:, :, :, st]
            chain.sync()
            dve.wait_ge(h_ready, 8)
            l3 = LAST.rearrange("p (k c) -> p k c", k=8)
            chain.did(v.tensor_copy(l3[:, :, 27:28], REC3[:, :, HALF + HP - 1:HALF + HP]))
            v.tensor_copy(l3[:, :, 28:36].rearrange("p k (h b) -> p k h b", h=2),
                          smp(REC)[:, :, :, 3].rearrange("p (k h) b -> p k h b", h=2)).then_inc(h_ready, 1)
            dve.wait_ge(h_ready, 9)
            for n in range(8):
                o = O0["gbr"] + n
                dve.wait_ge(act_took, taken(o)[1])
                v.tensor_tensor(REC3[:, n, :], REC3[:, n, :], RTM[:, (n % 2) * TOK:(n % 2 + 1) * TOK], ALU.mult)\
                    .then_inc(prod_done, 1)
                splits.after(o)
                dve.wait_ge(gh_ready, GL_COUNT["gated"] + n + 1)
                dve.wait_ge(prod_done, GATED0 + n + 1)
                sub_lo(GL3[:, n, :], REC3[:, n, :], GH3[:, n, :], gl_ready)
            residual("rg_out")
            v.memset(SMALL[:, 6:7], 0.0).then_inc(phase_end, 1)
            at_phase(dve, 4)
            tail(1)

        @block.tensor
        def _(pe):
            mm, tr = nc.tensor.matmul, nc.tensor.transpose

            def wt(ring, c, k):
                at = (c % SLOTS) * CH + k * P
                return ring[:, at:at + P]

            def chunk_ready(c, t=None):
                pe.wait_ge(lo_ready, dyn(c + 1, t, 24))

            def tile(o, c, ks, xh, xl, x0, rows=P, t=None, each=None):
                chunk_ready(c, t)
                wait_taken(pe, o - 2, t) if o >= 2 else None
                b = 2 * (o % 2)
                for n, k in enumerate(ks):
                    if each:
                        each(n)
                    for w, parts in ((wt(HI, c, k), (xh, xl)), (wt(LO, c, k), (xh,))):
                        for x in parts:
                            for h in range(2):
                                first = n == 0 and w is not None and x is xh and parts[-1] is xl
                                last = n == len(ks) - 1 and len(parts) == 1
                                ins = mm(PS[0:rows, b + h, 0:HALF], w[:, 0:rows], x[:, x0 + n, h * HALF:(h + 1) * HALF],
                                         start=first, stop=last)
                ins.then_inc(tile_done, 1)

            for n in range(15):
                tile(n, C0["w_in"] + n, range(KT), XH3, XL3, 0, rows=48 if n == 6 else P,
                     each=(lambda k: pe.wait_ge(xl_ready, k + 1)) if n == 0 else None)
            for n in range(8):
                o, c = O0["cmp"] + n, C0["cmp"] + n
                kv = n // 4
                h_, l_ = ((GH, GL), (XH, XL))[kv]
                b = 2 * (o % 2)
                pe.wait_ge(cs_lo, 2 * kv + 2)
                chunk_ready(c)
                wait_taken(pe, o - 2)
                rows = lambda ap, m: ap[:, 0:4096].rearrange("p (g m c) -> p g m c", g=2, m=8)[:, :, m, :]
                pro = lambda ap, m: ap[:, 4096 + 66 * m:4096 + 66 * m + 66]
                for m in range(8):
                    for w, parts in ((wt(HI, c, m), (h_, l_)), (wt(LO, c, m), (h_,))):
                        for x in parts:
                            first, last = m == 0 and x is h_ and len(parts) == 2, m == 7 and len(parts) == 1
                            mm(PS[:, b, :].rearrange("p (g c) -> p g c", g=2), w, rows(x, m), start=first, stop=last)
                            ins = mm(PS[:, b + 1, 0:66], w, pro(x, m), start=first, stop=last)
                ins.then_inc(tile_done, 1)
                if n == 3:
                    pe.wait_ge(hid_ready, 2)
                    pe.wait_ge(w2_landed, 16)
                    for gg in range(2):
                        for hh in range(2):
                            mm(PS[64 * gg:64 * gg + 64, 4, 0:256], W2[:, hh * 64:hh * 64 + 64],
                               HS[:, hh * 512 + gg * 256:hh * 512 + gg * 256 + 256], start=hh == 0, stop=hh == 1)
                    for gg in range(2):
                        for hh in range(2):
                            ins = mm(PS[64 * gg:64 * gg + 64, 5, 0:32], W2[:, hh * 64:hh * 64 + 64],
                                     HPR[:, hh * 64 + gg * 32:hh * 64 + gg * 32 + 32], start=hh == 0, stop=hh == 1)
                    ins.then_inc(w2_done, 1)
                    pe.wait_ge(consts_ready, 1)
                    for i in range(4):
                        c0 = (i // 2) * HALF + P * (i % 2)
                        tr(PS[:, 5, 64 + 48 * i:112 + 48 * i], GTC[0:48, c0:c0 + P], IDENT[0:48, 0:48])
                    for r in range(2):
                        for kt in range(4):
                            ins = tr(PS[:, 6 + r, kt * P:(kt + 1) * P],
                                     KT4[:, (2 + r) * SEQ + kt * P:(2 + r) * SEQ + (kt + 1) * P], IDENT[:, :])
                    ins.then_inc(tr_done, 1)
            pe.wait_ge(hid_ready, 4)
            pe.wait_ge(w2_took, 1)
            pe.wait_ge(qk_lo, 3)
            for b in range(NB):
                for gg in range(2):
                    for hh in range(2):
                        mm(PS[0:32, 6 + b // 4, (b % 4) * P + gg * HD:(b % 4) * P + gg * HD + HD],
                           HS[:, hh * 512 + gg * 256 + b * 32:hh * 512 + gg * 256 + b * 32 + 32],
                           W2[:, 128 + hh * 64:128 + hh * 64 + 64], start=hh == 0, stop=hh == 1)
            for r in range(4):
                for gg in range(2):
                    for hh in range(2):
                        ins = mm(PS[32 * r:32 * r + 32, 5, gg * HD:gg * HD + HD],
                                 HPR[:, hh * 64 + gg * 32:hh * 64 + gg * 32 + 32],
                                 W2[:, 128 + hh * 64:128 + hh * 64 + 64], start=hh == 0, stop=hh == 1)
            ins.then_inc(w2_done, 1)
            pe.wait_ge(w2_took, 2)
            pe.wait_ge(qk_lo, 16)
            for r, (row, tl) in enumerate(((32, 3), (64, 5))):
                for b in range(NB):
                    ins = mm(PS[row:row + 4, 4 + 2 * r + b // 4, (b % 4) * P:(b % 4 + 1) * P],
                             KS[:, tl * 32 + 4 * b:tl * 32 + 4 * b + 4], IDENT[:, :], start=True, stop=True)
            ins.then_inc(tr_done, 1)
            at_phase(pe, 1)
            P4 = PB.rearrange("p (u r k) -> p u r k", u=2, r=2)
            PT3 = PT.rearrange("p (r k) -> p r k", r=2)

            def scores(u):
                i, j, gg = u // 16, (u // 2) % NJ, u % 2
                w = P * (i + 1)
                rows = slice(64 * gg, 64 * gg + 64)
                if u >= 2:
                    pe.wait_ge(p_ready, u - 1)
                for r in range(2):
                    b = 2 * (u % 2) + r
                    for n, (q, k) in enumerate(((QH, KH), (QH, KL), (QL, KH))):
                        mm(PS[:, b, 0:w], q[rows, j, i * P:(i + 1) * P], k[rows, r * SEQ:r * SEQ + w],
                           start=n == 0, stop=False)
                    ins = mm(PS[:, b, w - P:w], IDENTB[:, :], DMASK[:, :], start=False, stop=True)
                ins.then_inc(s_done, 1)

            def trans(u, r, w):
                for kt in range(w // P):
                    ins = tr(PS[:, 4 + r, kt * P:(kt + 1) * P], P4[:, u % 2, r, kt * P:(kt + 1) * P], IDENT[:, :])
                return ins

            def cmp_scores(i):
                for j in range(NJ):
                    for n, (q, k) in enumerate(((QH, 0), (QH, 64), (QL, 0))):
                        ins = mm(PS[:, 7, 64 * j:64 * j + 64], q[:, j, i * P:(i + 1) * P], KCZ[:, k:k + 64],
                                 start=n == 0, stop=n == 2)
                ins.then_inc(sc_done, 1)

            def cmp_trans(i):
                pe.wait_ge(pc_scaled, i + 1)
                for n in range(4):
                    ins = tr(PS[:, 6, n * P:(n + 1) * P], SC[:, n * P:(n + 1) * P], IDENT[:, :])
                ins.then_inc(pct_done, 1)

            def cmp_values(n):
                pe.wait_ge(pc_lo, n // 4 + 1)
                if n >= 2:
                    pe.wait_ge(ot_lo, n - 1)
                if n % 4 == 3:
                    pe.wait_ge(sc_masked, min(n // 4 + 2, 4))
                for hh in range(4):
                    at = PS[:, 6 + n % 2, hh * P:(hh + 1) * P]
                    for m, (v0, pc) in enumerate(((0, PCH), (256, PCH), (0, PCL))):
                        v0 += P * (hh // 2)
                        mm(at, VCZ[:, v0:v0 + P], pc[:, (n % 4) * P:(n % 4 + 1) * P],
                           start=m == 0 and hh == 0, stop=False)

            def values(u):
                n = u // 4
                at = PS[:, 6 + n % 2, (u % 4) * P:(u % 4 + 1) * P]
                kts = u // 16 + 1
                if u % 4 == 0:
                    cmp_values(n)
                pe.wait_ge(pt_dve, 2 * u + 2)
                for r in range(2):
                    for kt in range(kts):
                        vs = slice(r * SEQ + kt * P, r * SEQ + kt * P + P)
                        for m, (vv, hl) in enumerate(((VH, 0), (VL, 0), (VH, 1))):
                            ins = mm(at, vv[:, vs], PTS[:, u % 2, hl, r, kt * P:(kt + 1) * P],
                                     start=False, stop=r == 1 and kt == kts - 1 and m == 2 and u % 4 == 3)
                ins.then_inc(pv_done, 1)

            cmp_scores(0)
            scores(0)
            scores(1)
            cmp_trans(0)
            for u in range(64):
                for r in range(2):
                    pe.wait_ge(ps_ready, 2 * u + r + 1)
                    if u:
                        pe.wait_ge(pt_dve, 2 * u - 1 + r)
                    trans(u, r, P * (u // 16 + 1)).then_inc(pt_done, 1)
                if u < 62:
                    scores(u + 2)
                if u:
                    values(u - 1)
                if u % 16 == 9 and u < 48:
                    pe.wait_ge(ot_lo, u // 4)
                    cmp_scores(u // 16 + 1)
                if u % 16 == 14 and u < 48:
                    pe.wait_ge(ot_lo, u // 4)
                    cmp_trans(u // 16 + 1)
            values(63)
            CA = CACHE.rearrange("p (k b n c) -> p k b n c", k=2, b=4, n=PAGES)
            for vv in range(4):
                u = 64 + vv
                hb, gg = vv // 2, vv % 2
                rows = slice(64 * gg, 64 * gg + 64)
                pe.wait_ge(cache_landed[hb], 16 * (20 - 4 * hb))
                if hb:
                    pe.wait_ge(win_landed, 64)
                pe.wait_ge(p_ready, u - 1)
                if vv == 0:
                    pe.wait_ge(ot_lo, 16)
                for bb in range(4):
                    b = 4 * hb + bb
                    out = slice(32 * bb, 32 * bb + 32)
                    qb = QS[rows, 32 * b:32 * b + 32]
                    for r in range(2):
                        mm(PS[out, 2 * (u % 2) + r, :].rearrange("p (n c) -> p n c", n=PAGES), qb,
                           CA[rows, r, bb, :, 0:P], start=True, stop=True)
                    mm(PS[out, 6, 0:32], qb, KC[rows, 32 * b:32 * b + 32], start=True, stop=True)
                    for r in range(2):
                        ins = mm(PS[out, 6, 32 * (r + 1):32 * (r + 1) + 4], qb,
                                 KS[rows, (2 + 2 * r) * 32 + 4 * b:(2 + 2 * r) * 32 + 4 * b + 4], start=True, stop=True)
                ins.then_inc(s_done, 1)
                pe.wait_ge(p_ready, u + 1)
                pe.wait_ge(pt_act, transposed(u))
                pe.wait_ge(pt_dve, transposed(u))
                trans(u, 0, SEQ)
                trans(u, 1, SEQ)
                tr(PS[0:96, 6, 128:256], SC[:, 0:96], IDENT[:, :]).then_inc(pt_done, 1)
                pe.wait_ge(pt_act, transposed(u + 1))
                pe.wait_ge(pt_dve, transposed(u + 1))
                if vv:
                    pe.wait_ge(o_ready, vv)
                ptm = OTMP[:, 256:384]
                for bb in range(4):
                    b = 4 * hb + bb
                    out = slice(32 * bb, 32 * bb + 32)
                    cols = slice(b * P + gg * HD, b * P + gg * HD + HD)
                    mm(PS[out, 7, 0:HD], ptm[0:32, out], VM[0:32, cols], start=True, stop=True)
                    for r in range(2):
                        ob = PS[out, 7, HD * (r + 1):HD * (r + 2)]
                        new = slice(32 * (r + 1), 32 * (r + 1) + 4)
                        for n in range(PAGES):
                            mm(ob, PT3[:, r, n * P + 32 * bb:n * P + 32 * bb + 32],
                               CA[:, r, bb, n, P + gg * HD:P + gg * HD + HD], start=n == 0, stop=n == PAGES - 1)
                        ins = mm(PS[out, 2 * (u % 2) + r, 0:HD], ptm[new, out], VM[new, cols], start=True, stop=True)
                ins.then_inc(pv_done, 1)
                if gg == 1:
                    pe.wait_ge(o_ready, vv + 1)
                    tr(PS[:, 4, 0:P], OS[:, 0:P], IDENT[:, :]).then_inc(ot_done, 1)
                    pe.wait_ge(ot_lo, 16 + hb + 1)
            pe.wait_ge(ot_lo, 18)
            for n in range(8):
                tile(O0["w_out"] + n, C0["w_out"] + n, range(KT), XH3, XL3, 0)

            def stat(bank, src, first, last):
                for h in range(2):
                    ins = mm(PS[:, bank + h, 0:HALF], ONES[:, :], src[:, h * HALF:(h + 1) * HALF], start=first, stop=last)
                return ins

            def ln_sums(idx, between=None):
                if idx:
                    pe.wait_ge(n_ready, 8 * idx)
                pe.wait_ge(xsum_ready, XSUM[idx])
                stat(4, XSUM_, True, True).then_inc(mean_done, 1)
                if between:
                    between()
                for k in range(4):
                    pe.wait_ge(pair_ready, 4 * idx + k + 1)
                    stat(6, SQ4[2 * (k % 2)], k == 0, k == 3).then_inc(var_done, 1)

            def tail(layer):
                ln_sums(2 * layer)
                base, c0 = O0[f"ffn{layer}"], C0[f"ffn{layer}"]
                xl0, gl0 = XL_COUNT[f"ln1_{layer}"], GL_COUNT[f"ffn{layer}"]
                with pe.Fori(0, 3) as t:
                    for n in range(16):
                        tile(base + n, c0 + n, range(KT), XH3, XL3, 0, t=t,
                             each=(lambda k: pe.wait_ge(xl_ready, xl0 + k + 1)) if n == 0 else None)
                    for n in range(8):
                        tile(base + 16 + n, c0 + 16 + n, range(KT), GH3, GL3, 0, t=t,
                             each=(lambda k: pe.wait_ge(gl_ready, 8 * t + (gl0 + k + 1))) if n == 0 else None)
                pc, po = C0[f"proj{layer}"], O0[f"proj{layer}"]
                ph3, pl3 = XH[:, 0:2 * TOK].rearrange("p (k t) -> p k t", k=2), XL[:, 0:2 * TOK].rearrange("p (k t) -> p k t", k=2)

                def proj(lo, hi):
                    pe.wait_ge(pl_ready, layer + 1)
                    for n in range(lo, hi):
                        tile(po + n, pc + n // 4, (2 * (n % 4), 2 * (n % 4) + 1), ph3, pl3, 0)

                ln_sums(2 * layer + 1, between=lambda: proj(0, 2))
                proj(2, 8)
                for n in range(8):
                    tile(O0[f"gate{layer}"] + n, C0[f"gate{layer}"] + n, range(KT), GH3, GL3, 0,
                         each=(lambda k: pe.wait_ge(gl_ready, GL_COUNT[f"ln2_{layer}"] + k + 1)) if n == 0 else None)

            tail(0)
            for n in range(8):
                tile(O0["rec"] + n, C0["rec"] + n, range(KT), XH3, XL3, 0,
                     each=(lambda k: pe.wait_ge(xl_ready, XL_COUNT["x1"] + k + 1)) if n == 0 else None)
            for n in range(8):
                pe.wait_ge(gl_ready, GL_COUNT["rec"] + 2 * (n // 2) + 2)
                for gate in range(2):
                    tile(O0["rgate"] + 2 * n + gate, C0["rgate"] + 2 * (n // 4) + gate, (2 * (n % 4), 2 * (n % 4) + 1),
                         GH3, GL3, 2 * (n // 2))
            for n in range(8):
                tile(O0["gbr"] + n, C0["gbr"] + n, range(KT), XH3, XL3, 0)
            for n in range(8):
                tile(O0["rg_out"] + n, C0["rg_out"] + n, range(KT), GH3, GL3, 0,
                     each=(lambda k: pe.wait_ge(gl_ready, GL_COUNT["gated"] + k + 1)) if n == 0 else None)
            tail(1)


def token_columns(prompt, sample):
    c = prompt.shape[1]
    return np.concatenate([prompt.reshape(2, HP, c), sample.reshape(2, 16, c)], axis=1).reshape(TOK, c).T


def channels(x):
    return np.ascontiguousarray(x.reshape(-1, P, x.shape[1]).transpose(1, 0, 2).reshape(P, -1))


def chunks(w):
    return w.reshape(8, P, -1, P).transpose(2, 1, 0, 3).reshape(-1, P, CH)


def pair_chunks(w):
    return w.reshape(-1, 4, 2, P, P).transpose(0, 3, 1, 2, 4).reshape(-1, P, CH)


def lay_out(x):
    z = {k: np.asarray(v) for k, v in x.items()}
    f = np.float32
    heads = [gg * NJ + j for j in range(NJ) for gg in range(2)]
    win = z["nsa_w_in"][0]
    kv0 = D
    q = win[:, :D].reshape(D, 16, HD)[:, heads].reshape(D, D)
    gate = win[:, D + 6 * P:].reshape(D, 2, NJ, 3).transpose(0, 2, 1, 3).reshape(D, 48)
    w_in = np.concatenate([win[:, kv0:kv0 + 6 * P], gate, np.zeros((D, P - 48), f), q], axis=1)
    w1 = z["nsa_cmp_w1"][0].reshape(2, 2, 8, 2, HD, 2, P).transpose(0, 5, 1, 3, 4, 2, 6).reshape(8, P, CH)
    w_out = z["nsa_w_out"][0].reshape(16, HD, D)[heads].reshape(D, D)
    parts = [chunks(w_in), w1, chunks(w_out)]

    def ffn(i):
        up = chunks(z["ffn_w_up"][i])
        out = []
        for t in range(3):
            for p in range(8):
                out += [up[8 * t + p][None], up[24 + 8 * t + p][None]]
            out.append(chunks(z["ffn_w_down"][i][D * t:D * (t + 1)]))
        proj = z["ple_w_proj"][i].reshape(256, 8, P).transpose(1, 0, 2)
        return out + [pair_chunks(proj), chunks(z["ple_w_gate"][i])]

    def block_gate(w):
        return pair_chunks(w.reshape(4, 256, 2, P).transpose(0, 2, 1, 3).reshape(8, 256, P))

    rin = chunks(z["rg_w_in"][0])
    ga, gx = block_gate(z["rg_gate_a_w"][0]), block_gate(z["rg_gate_x_w"][0])
    parts += ffn(0) + [rin[8:], ga[:1], gx[:1], ga[1:], gx[1:], rin[:8], chunks(z["rg_w_out"][0])] + ffn(1)
    stream = np.concatenate(parts, axis=0)
    assert stream.shape == (N_CHUNKS, P, CH), (stream.shape, N_CHUNKS)

    col = lambda v: v.reshape(-1, P).T
    cols = []
    for i in (0, 1):
        taps = np.concatenate([z["ffn_conv_w"][i], z["ffn_conv_b"][i][None]], axis=0)
        cols += [channels(taps.T), col(z["ln_mix_g"][i]), col(z["ln_mix_b"][i]),
                 col(z["ln_ffn_g"][i]), col(z["ln_ffn_b"][i])]
    pe = z["nsa_cmp_pe"][0].reshape(2, 2, 8, 2, HD).transpose(3, 4, 0, 2, 1).reshape(P, 32)
    cols += [col(z["rg_conv_w"][0].reshape(-1)), col(z["rg_conv_b"][0]), col(z["rg_gate_a_b"][0]), col(z["rg_gate_x_b"][0]),
             col(z["rg_lambda"][0]), col(z["nsa_cmp_b1"][0].reshape(-1)), pe,
             channels(z["state_rglru_h"][0].T), channels(z["state_rglru_conv"][0].transpose(2, 0, 1).reshape(D, 24))]
    params = np.ascontiguousarray(np.concatenate(cols, axis=1))
    assert params.shape == (P, NPAR)

    kv = z["cache_nsa_kv"][0]
    n_pool = kv.shape[0]
    cmp_rows = kv[:, :, 0:2].reshape(n_pool, 8, 8, 2, 2, 2, HD).transpose(0, 3, 6, 4, 5, 2, 1).reshape(n_pool * P, 256)
    sel_k = kv[:, :, 2].reshape(n_pool, P, P).transpose(0, 2, 1)
    sel = np.concatenate([sel_k, kv[:, :, 3].reshape(n_pool, P, P)], axis=2).reshape(n_pool * P, 256)
    wn = z["cache_nsa_win"][0].reshape(NB, 4, P, 2, P)
    wk, wv = wn[:, :, :, 0].transpose(0, 3, 1, 2), wn[:, :, :, 1].transpose(0, 2, 1, 3)
    cache_win = np.concatenate([wk, wv], axis=3).reshape(NB, P, 1024)
    s_of = np.arange(P) % NS
    k4 = np.arange(4)
    smask = np.concatenate([np.where(k4[None] <= s_of[:, None], 0, NEG), np.where(k4[None] >= s_of[:, None], 0, NEG)], axis=1)
    return {
        "w_stream": stream.reshape(N_CHUNKS * P, CH),
        "x": channels(token_columns(z["x_prompt"][0], z["x_sample"].reshape(32, D))),
        "p": np.stack([channels(token_columns(z["p_prompt"][i][0], z["p_sample"][i].reshape(32, 256))) for i in (0, 1)]),
        "params": params,
        "pages": z["page_table"].reshape(1, -1).astype(np.int32),
        "cache_cmp": np.ascontiguousarray(cmp_rows),
        "cache_sel": np.ascontiguousarray(sel),
        "cache_win": np.ascontiguousarray(cache_win),
        "win_copy": np.ascontiguousarray(z["cache_nsa_win"][0][:, NS:].reshape(NB * 127, 1024)),
        "cmp_w2": np.ascontiguousarray(z["nsa_cmp_w2"][0].reshape(2, 2, P, HD).transpose(2, 0, 1, 3).reshape(P, 256)),
        "smask": smask.astype(f),
        "ffn_state": np.stack([channels(z["state_ffn_conv"][i].transpose(2, 0, 1).reshape(6 * D, 16)) for i in (0, 1)]),
    }


OUTPUTS = {"y": (P, KT * TOK), "kcmp": (P, 1024), "kt4": (P, 4 * SEQ), "ks": (P, 192), "win_old": (NB * 127, 1024),
           "rg": (P, 8 * 36), "ffn_conv": (2, P, 48 * 18)}


def kernel(**inputs):
    import concourse.bacc as bacc
    from concourse.bass_utils import run_bass_kernel_spmd

    nc = bacc.Bacc("TRN2", target_bir_lowering=False, num_devices=1)
    arrays = {f"in_{k}": np.ascontiguousarray(v) for k, v in lay_out(inputs).items()}
    a = {k[3:]: nc.dram_tensor(k, v.shape, mybir.dt.from_np(v.dtype), kind="ExternalInput").ap()
         for k, v in arrays.items()}
    a["gate_scratch"] = nc.dram_tensor("gate_scratch", (2, P, 6), F32, kind="Internal").ap()
    outs = {k: nc.dram_tensor(f"out_{k}", s, F32, kind="ExternalOutput").ap() for k, s in OUTPUTS.items()}
    build(nc, a, outs)
    r = run_bass_kernel_spmd(nc, [arrays], core_ids=[0]).results[0]
    o = {k: np.asarray(r[f"out_{k}"]) for k in OUTPUTS}

    y = o["y"].reshape(P, KT, 2, HALF).transpose(2, 3, 1, 0).reshape(2, HALF, D)
    y_prompt = y[:, :HP].reshape(1, SEQ, D)
    y_sample = y[:, HP:].reshape(NB, NS, D)
    kc = o["kcmp"].reshape(2, HD, 2, 2, 8, 32).transpose(5, 4, 3, 2, 0, 1).reshape(SEQ, 2, 2, HD)
    k4 = o["kt4"].reshape(2, HD, 2, 2, SEQ).transpose(4, 3, 2, 0, 1).reshape(SEQ, 4, 2, HD)
    ks = o["ks"].reshape(2, HD, 6, 32).transpose(3, 2, 0, 1)
    kv_prompt = np.concatenate([kc, k4[:, 0:2]], axis=1)[None, None]
    win_prompt = np.ascontiguousarray(k4[:, 2:4])[None, None]
    kv_sample = np.ascontiguousarray(ks[:, 0:4]).reshape(1, NB, NS, 4, 2, HD)
    win_new = ks[:, 4:6].reshape(NB, NS, 2, 2, HD)
    win_sample = np.concatenate([o["win_old"].reshape(NB, SEQ - NS, 2, 2, HD), win_new], axis=1)[None]
    rg = o["rg"].reshape(P, 8, 36).transpose(2, 1, 0).reshape(36, D)
    fc = o["ffn_conv"].reshape(2, P, 48, 18).transpose(0, 3, 2, 1).reshape(2, 18, 6 * D)
    c = np.ascontiguousarray
    return (c(y_prompt), c(y_sample), c(kv_prompt), kv_sample, win_prompt, win_sample,
            c(rg[27:28])[None], c(rg[28:36])[None], c(rg[0:3])[None, None], c(rg[3:27]).reshape(1, NB, 3, D),
            c(fc[:, 0:2])[:, None], c(fc[:, 2:18]).reshape(2, NB, 2, 6 * D))
```
